# Optimizing a Trainium2 kernel written in Bass

```python
import jax, jax.numpy as jnp
from jax import lax
import numpy as np
import math

D_MODEL = 1024
BATCH = 1
SEQ = 256
DEPTH = 1

RET_HEADS = 4
RET_V_DIM = D_MODEL // 2 // RET_HEADS
RET_QK_DIM = RET_V_DIM // 2
RET_CHUNK = 128
ATT_HEAD_DIM = 64
ATT_HEADS = D_MODEL // 2 // ATT_HEAD_DIM
DILATED_CONFIGS = ((128, 1), (512, 4), (2048, 16))
N_EXPERTS = 16
EC_CAPACITY_FACTOR = 2
D_FF_EXPERT = 2048

RET_QK_W = RET_HEADS * RET_QK_DIM
RET_V_W = RET_HEADS * RET_V_DIM
ATT_W = ATT_HEADS * ATT_HEAD_DIM
MIX_WIDTH = RET_V_W + ATT_W
IN_PROJ_WIDTH = 2 * RET_QK_W + 2 * RET_V_W + 3 * ATT_W
RMS_EPS = 1e-6
GN_EPS = 1e-5
MASK_VALUE = -1e30


def rmsnorm(x, g):
    xf = x.astype(jnp.float32)
    y = xf * lax.rsqrt(jnp.mean(xf * xf, axis=-1, keepdims=True) + RMS_EPS)
    return (y * g.astype(jnp.float32)).astype(x.dtype)

def alibi_slopes(n):
    return 2.0 ** (-8.0 * (jnp.arange(n, dtype=jnp.float32) + 1.0) / n)

def retention_scan(q, k, v, log_gamma, inclusive):
    B, H, S, dk = q.shape
    dv = v.shape[-1]
    C = RET_CHUNK
    n = S // C
    qc = q.reshape(B, H, n, C, dk)
    kc = k.reshape(B, H, n, C, dk)
    vc = v.reshape(B, H, n, C, dv)
    pos = jnp.arange(C, dtype=jnp.float32)
    rel = pos[:, None] - pos[None, :]
    mask = (rel >= 0) if inclusive else (rel > 0)
    lg = log_gamma[:, None, None]
    intra_decay = jnp.where(mask[None], jnp.exp(lg * jnp.where(mask, rel, 0.0)[None]), 0.0)
    scores = jnp.einsum('bhnid,bhnjd->bhnij', qc, kc) * intra_decay[None, :, None]
    o = jnp.einsum('bhnij,bhnjv->bhniv', scores, vc)
    k_tail = kc * jnp.exp(log_gamma[:, None] * (C - 1.0 - pos))[None, :, None, :, None]
    kv = jnp.einsum('bhnjd,bhnjv->nbhdv', k_tail, vc)
    chunk_decay = jnp.exp(log_gamma * C)[None, :, None, None]

    def step(state, kv_n):
        return chunk_decay * state + kv_n, state

    _, prev = lax.scan(step, jnp.zeros((B, H, dk, dv), jnp.float32), kv)
    q_head = qc * jnp.exp(log_gamma[:, None] * (pos + 1.0))[None, :, None, :, None]
    o = o + jnp.einsum('bhnid,nbhdv->bhniv', q_head, prev)
    return o.reshape(B, H, S, dv)

def bidirectional_retention(q, k, v, logit_fwd, logit_bwd):
    qf, kf, vf = q.astype(jnp.float32), k.astype(jnp.float32), v.astype(jnp.float32)
    lg_f = jax.nn.log_sigmoid(logit_fwd.astype(jnp.float32))
    lg_b = jax.nn.log_sigmoid(logit_bwd.astype(jnp.float32))
    y_f = retention_scan(qf, kf, vf, lg_f, True)
    y_b = jnp.flip(retention_scan(jnp.flip(qf, 2), jnp.flip(kf, 2), jnp.flip(vf, 2), lg_b, False), 2)
    y = y_f + y_b
    mu = jnp.mean(y, axis=-1, keepdims=True)
    var = jnp.mean(jnp.square(y - mu), axis=-1, keepdims=True)
    return (y - mu) * lax.rsqrt(var + GN_EPS)

def banded_attention(q, k, v, half, slopes):
    N, H, L, dh = q.shape
    W = half
    nb = -(-L // W)
    pad = nb * W - L
    qb = jnp.pad(q, ((0, 0), (0, 0), (0, pad), (0, 0))).reshape(N, H, nb, W, dh)

    def windows(t):
        tb = jnp.pad(t, ((0, 0), (0, 0), (W, pad + W), (0, 0))).reshape(N, H, nb + 2, W, dh)
        return jnp.concatenate([tb[:, :, :-2], tb[:, :, 1:-1], tb[:, :, 2:]], axis=3)

    kw, vw = windows(k), windows(v)
    qpos = jnp.arange(nb * W).reshape(nb, W)
    kpos = jnp.arange(nb)[:, None] * W - W + jnp.arange(3 * W)[None, :]
    dist = jnp.abs(kpos[:, None, :] - qpos[:, :, None])
    valid = (dist <= W) & (kpos[:, None, :] >= 0) & (kpos[:, None, :] < L)
    s = jnp.einsum('nhbqd,nhbkd->nhbqk', qb, kw).astype(jnp.float32) * (dh ** -0.5)
    s = s - slopes[None, :, None, None, None] * dist.astype(jnp.float32)[None, None]
    s = jnp.where(valid[None, None], s, MASK_VALUE)
    lse = jax.nn.logsumexp(s, axis=-1)
    p = jnp.exp(s - lse[..., None])
    o = jnp.einsum('nhbqk,nhbkd->nhbqd', p, vw.astype(jnp.float32))
    return o.reshape(N, H, nb * W, dh)[:, :, :L], lse.reshape(N, H, nb * W)[:, :, :L]

def dilated_attention(q, k, v, window, dilation, slopes):
    B, H, S, dh = q.shape
    L = S // dilation

    def to_sub(t):
        return t.reshape(B, H, L, dilation, dh).transpose(0, 3, 1, 2, 4).reshape(B * dilation, H, L, dh)

    o, lse = banded_attention(to_sub(q), to_sub(k), to_sub(v), window // (2 * dilation), slopes * dilation)
    o = o.reshape(B, dilation, H, L, dh).transpose(0, 2, 3, 1, 4).reshape(B, H, S, dh)
    lse = lse.reshape(B, dilation, H, L).transpose(0, 2, 3, 1).reshape(B, H, S)
    return o, lse

def expert_choice_moe(h, w_router, w_gate, w_up, w_down):
    B, S, D = h.shape
    E = w_router.shape[-1]
    cap = EC_CAPACITY_FACTOR * S // E
    affinity = jax.nn.softmax((h @ w_router).astype(jnp.float32), axis=-1)
    gates, idx = lax.top_k(jnp.swapaxes(affinity, 1, 2), cap)
    flat_idx = idx.reshape(B, E * cap)
    b_idx = jnp.arange(B)[:, None]
    xe = h[b_idx, flat_idx].reshape(B, E, cap, D)
    a = jnp.einsum('becd,edf->becf', xe, w_gate)
    u = jnp.einsum('becd,edf->becf', xe, w_up)
    ye = jnp.einsum('becf,efd->becd', jax.nn.silu(a) * u, w_down)
    ye = ye * gates[..., None].astype(ye.dtype)
    out = jnp.zeros_like(h).at[b_idx, flat_idx].add(ye.reshape(B, E * cap, D).astype(h.dtype))
    return out

def first_inputs(seed: int = 0) -> dict:
    key = jax.random.key(seed)
    ks = jax.random.split(key, 20)
    f32 = jnp.float32
    D, F, E = D_MODEL, D_FF_EXPERT, N_EXPERTS
    nrm = lambda k, shape, s: jax.random.normal(k, shape, f32) * s
    base_logit = jnp.log(2.0 ** (5.0 + jnp.arange(RET_HEADS, dtype=f32)) - 1.0)
    return {
        "x": nrm(ks[0], (BATCH, SEQ, D), 1.0),
        "c": nrm(ks[1], (BATCH, D), 1.0),
        "w_ada": nrm(ks[2], (DEPTH, D, 6 * D), 0.5 * D ** -0.5),
        "b_ada": nrm(ks[3], (DEPTH, 6 * D), 0.01),
        "g_pre_mix": 1.0 + nrm(ks[4], (DEPTH, D), 0.01),
        "g_post_mix": 1.0 + nrm(ks[5], (DEPTH, D), 0.01),
        "g_pre_ffn": 1.0 + nrm(ks[6], (DEPTH, D), 0.01),
        "g_post_ffn": 1.0 + nrm(ks[7], (DEPTH, D), 0.01),
        "w_in": nrm(ks[8], (DEPTH, D, IN_PROJ_WIDTH), D ** -0.5),
        "ret_decay_fwd": base_logit[None] + nrm(ks[9], (DEPTH, RET_HEADS), 0.1),
        "ret_decay_bwd": base_logit[None] + nrm(ks[10], (DEPTH, RET_HEADS), 0.1),
        "w_out": nrm(ks[11], (DEPTH, MIX_WIDTH, D), MIX_WIDTH ** -0.5),
        "w_router": nrm(ks[12], (DEPTH, D, E), D ** -0.5),
        "w_gate_e": nrm(ks[13], (DEPTH, E, D, F), D ** -0.5),
        "w_up_e": nrm(ks[14], (DEPTH, E, D, F), D ** -0.5),
        "w_down_e": nrm(ks[15], (DEPTH, E, F, D), F ** -0.5),
    }

def first_block(x, c, w_ada, b_ada, g_pre_mix, g_post_mix, g_pre_ffn, g_post_ffn, w_in,
              ret_decay_fwd, ret_decay_bwd, w_out, w_router, w_gate_e, w_up_e, w_down_e):
    B, S, D = x.shape
    slopes = alibi_slopes(ATT_HEADS)
    split_at = np.cumsum([RET_QK_W, RET_QK_W, RET_V_W, RET_V_W, ATT_W, ATT_W]).tolist()

    def heads(t, n_heads):
        return t.reshape(B, S, n_heads, -1).transpose(0, 2, 1, 3)

    for l in range(DEPTH):
        mod = jax.nn.silu(c) @ w_ada[l] + b_ada[l]
        shift_m, scale_m, gate_m, shift_f, scale_f, gate_f = [m[:, None, :] for m in jnp.split(mod, 6, axis=-1)]

        h = rmsnorm(x, g_pre_mix[l]) * (1.0 + scale_m) + shift_m
        proj = h @ w_in[l]
        rq, rk, rv, rg, aq, ak, av = jnp.split(proj, split_at, axis=-1)

        y_ret = bidirectional_retention(heads(rq, RET_HEADS), heads(rk, RET_HEADS) * (RET_QK_DIM ** -0.5),
                                        heads(rv, RET_HEADS), ret_decay_fwd[l], ret_decay_bwd[l])
        y_ret = y_ret.transpose(0, 2, 1, 3).reshape(B, S, RET_V_W).astype(x.dtype)
        y_ret = jax.nn.silu(rg) * y_ret

        qh, kh, vh = heads(aq, ATT_HEADS), heads(ak, ATT_HEADS), heads(av, ATT_HEADS)
        results = [dilated_attention(qh, kh, vh, w, d, slopes) for (w, d) in DILATED_CONFIGS]
        outs = jnp.stack([r[0] for r in results])
        lses = jnp.stack([r[1] for r in results])
        mix_w = jax.nn.softmax(lses, axis=0)
        y_att = jnp.sum(mix_w[..., None] * outs, axis=0)
        y_att = y_att.transpose(0, 2, 1, 3).reshape(B, S, ATT_W).astype(x.dtype)

        mixed = jnp.concatenate([y_ret, y_att], axis=-1) @ w_out[l]
        x = x + gate_m * rmsnorm(mixed, g_post_mix[l])

        h = rmsnorm(x, g_pre_ffn[l]) * (1.0 + scale_f) + shift_f
        moe = expert_choice_moe(h, w_router[l], w_gate_e[l], w_up_e[l], w_down_e[l])
        x = x + gate_f * rmsnorm(moe, g_post_ffn[l])
    return x


DEPTH_2 = 2

P_DIM = 256
D_FF = 2816
ML_HEADS = 4
ML_QK_DIM = 64
ML_V_DIM = 128
ML_CHUNK = 64
SW_Q_HEADS = 8
SW_KV_HEADS = 2
SW_HEAD_DIM = 64
WINDOW = 128
REL_BUCKETS = 32
REL_MAX_DIST = 128
EPS = 1e-6

ML_QK_W = ML_HEADS * ML_QK_DIM
ML_V_W = ML_HEADS * ML_V_DIM
SW_Q_W = SW_Q_HEADS * SW_HEAD_DIM
SW_KV_W = SW_KV_HEADS * SW_HEAD_DIM
SPLITS = (ML_QK_W, ML_QK_W, ML_V_W, ML_V_W, ML_HEADS, ML_HEADS, SW_Q_W, SW_KV_W, SW_KV_W, D_MODEL, D_MODEL)
D_IN = 2 * ML_QK_W + 2 * ML_V_W + 2 * ML_HEADS + SW_Q_W + 2 * SW_KV_W + 2 * D_MODEL


def rmsnorm_2(x, g):
    xf = x.astype(jnp.float32)
    y = xf * lax.rsqrt(jnp.mean(xf * xf, axis=-1, keepdims=True) + EPS)
    return (y * g.astype(jnp.float32)).astype(x.dtype)

def swiglu_ffn(x, wi, wo):
    g, u = jnp.split(x @ wi, 2, axis=-1)
    return (jax.nn.silu(g) * u) @ wo

def t5_bucket(dist):
    max_exact = REL_BUCKETS // 2
    d = np.maximum(dist, 0)
    large = max_exact + (np.log(np.maximum(d, 1) / max_exact) / np.log(REL_MAX_DIST / max_exact)
                         * (REL_BUCKETS - max_exact)).astype(np.int32)
    large = np.minimum(large, REL_BUCKETS - 1)
    return np.where(d < max_exact, d, large).astype(np.int32)

def mlstm_chunkwise(q, k, v, i_pre, f_pre):
    B, S, H, dk = q.shape
    dv = v.shape[-1]
    L = ML_CHUNK
    NC = S // L
    f32 = jnp.float32
    qc = q.astype(f32).reshape(B, NC, L, H, dk)
    kc = (k.astype(f32) / math.sqrt(dk)).reshape(B, NC, L, H, dk)
    vc = v.astype(f32).reshape(B, NC, L, H, dv)
    log_i = jnp.swapaxes(i_pre.astype(f32).reshape(B, NC, L, H), 2, 3)
    log_f = jnp.swapaxes(jax.nn.log_sigmoid(f_pre.astype(f32)).reshape(B, NC, L, H), 2, 3)
    b = jnp.cumsum(log_f, axis=-1)
    g = b[..., -1]
    a = g[..., None] - b + log_i
    m_loc = jnp.max(a, axis=-1)
    w = jnp.exp(a - m_loc[..., None])
    C_loc = jnp.einsum('bnhl,bnlhk,bnlhv->bnhkv', w, kc, vc)
    n_loc = jnp.einsum('bnhl,bnlhk->bnhk', w, kc)

    def step(carry, xs):
        C, n, m = carry
        g_c, m_c, C_c, n_c = xs
        m_new = jnp.maximum(g_c + m, m_c)
        s_old = jnp.exp(g_c + m - m_new)
        s_new = jnp.exp(m_c - m_new)
        C_new = s_old[..., None, None] * C + s_new[..., None, None] * C_c
        n_new = s_old[..., None] * n + s_new[..., None] * n_c
        return (C_new, n_new, m_new), (C, n, m)

    init = (jnp.zeros((B, H, dk, dv), f32), jnp.zeros((B, H, dk), f32), jnp.zeros((B, H), f32))
    xs = (jnp.moveaxis(g, 1, 0), jnp.moveaxis(m_loc, 1, 0), jnp.moveaxis(C_loc, 1, 0), jnp.moveaxis(n_loc, 1, 0))
    _, (C_prev, n_prev, m_prev) = lax.scan(step, init, xs)
    C_prev = jnp.moveaxis(C_prev, 0, 1)
    n_prev = jnp.moveaxis(n_prev, 0, 1)
    m_prev = jnp.moveaxis(m_prev, 0, 1)

    causal = jnp.tril(jnp.ones((L, L), dtype=bool))
    D = b[..., :, None] - b[..., None, :] + log_i[..., None, :]
    D = jnp.where(causal, D, -jnp.inf)
    e = b + m_prev[..., None]
    m_t = jnp.maximum(jnp.max(D, axis=-1), e)
    W = jnp.exp(D - m_t[..., None]) * jnp.einsum('bnthd,bnshd->bnhts', qc, kc)
    s_inter = jnp.exp(e - m_t)
    num = (jnp.einsum('bnhts,bnshv->bnthv', W, vc)
           + jnp.swapaxes(s_inter, 2, 3)[..., None] * jnp.einsum('bnthd,bnhdv->bnthv', qc, C_prev))
    den = jnp.sum(W, axis=-1) + s_inter * jnp.einsum('bnthd,bnhd->bnht', qc, n_prev)
    denom = jnp.maximum(jnp.abs(den), jnp.exp(-m_t))
    h = num / jnp.swapaxes(denom, 2, 3)[..., None]
    return h.reshape(B, S, H, dv).astype(q.dtype)

def swa_sink_attention(q, k, v, q_gain, k_gain, sinks, rel_bias):
    B, S, Hq, d = q.shape
    Hkv = k.shape[2]
    G = Hq // Hkv
    Wn = WINDOW
    NB = S // Wn
    f32 = jnp.float32
    q = rmsnorm_2(q, q_gain)
    k = rmsnorm_2(k, k_gain)
    qb = q.astype(f32).reshape(B, NB, Wn, Hkv, G, d) * (d ** -0.5)
    kb = k.astype(f32).reshape(B, NB, Wn, Hkv, d)
    vb = v.astype(f32).reshape(B, NB, Wn, Hkv, d)
    shift = lambda t: jnp.concatenate([jnp.zeros_like(t[:, :1]), t[:, :-1]], axis=1)
    kk = jnp.concatenate([shift(kb), kb], axis=2)
    vv = jnp.concatenate([shift(vb), vb], axis=2)
    logits = jnp.einsum('bnqkgd,bnskd->bnkgqs', qb, kk)
    dist = np.arange(Wn)[:, None] + Wn - np.arange(2 * Wn)[None, :]
    in_window = (dist >= 0) & (dist < Wn)
    bias = rel_bias.astype(f32)[t5_bucket(dist)]
    bias = jnp.transpose(bias, (2, 0, 1)).reshape(Hkv, G, Wn, 2 * Wn)
    key_pos = np.arange(NB)[:, None] * Wn - Wn + np.arange(2 * Wn)[None, :]
    valid = in_window[None] & (key_pos >= 0)[:, None, :]
    logits = jnp.where(valid[None, :, None, None], logits + bias, -jnp.inf)
    sink = sinks.astype(f32).reshape(Hkv, G)[None, None, :, :, None, None]
    m = jnp.maximum(jnp.max(logits, axis=-1, keepdims=True), sink)
    pr = jnp.exp(logits - m)
    denom = jnp.sum(pr, axis=-1, keepdims=True) + jnp.exp(sink - m)
    out = jnp.einsum('bnkgqs,bnskd->bnqkgd', pr / denom, vv)
    return out.reshape(B, S, Hq * d).astype(q.dtype)

def second_inputs(seed: int = 0) -> dict:
    key = jax.random.key(seed)
    ks = jax.random.split(key, 24)
    f32 = jnp.float32
    nrm = lambda k, shape, fan_in: jax.random.normal(k, shape, f32) * (fan_in ** -0.5)
    gain = lambda k, shape: 1.0 + 0.05 * jax.random.normal(k, shape, f32)
    return {
        "x": jax.random.normal(ks[0], (BATCH, SEQ, D_MODEL), f32),
        "p": jax.random.normal(ks[1], (DEPTH_2, BATCH, SEQ, P_DIM), f32),
        "ffn1_norm": gain(ks[2], (DEPTH_2, D_MODEL)),
        "ffn1_wi": nrm(ks[3], (DEPTH_2, D_MODEL, 2 * D_FF), D_MODEL),
        "ffn1_wo": nrm(ks[4], (DEPTH_2, D_FF, D_MODEL), D_FF),
        "mix_norm": gain(ks[5], (DEPTH_2, D_MODEL)),
        "w_in": nrm(ks[6], (DEPTH_2, D_MODEL, D_IN), D_MODEL),
        "b_igate": 0.1 * jax.random.normal(ks[7], (DEPTH_2, ML_HEADS), f32),
        "b_fgate": jnp.linspace(3.0, 6.0, ML_HEADS, dtype=f32)[None, :] + 0.1 * jax.random.normal(ks[8], (DEPTH_2, ML_HEADS), f32),
        "ml_out_norm": gain(ks[9], (DEPTH_2, ML_HEADS, ML_V_DIM)),
        "q_norm": gain(ks[10], (DEPTH_2, SW_HEAD_DIM)),
        "k_norm": gain(ks[11], (DEPTH_2, SW_HEAD_DIM)),
        "sinks": 0.5 * jax.random.normal(ks[12], (DEPTH_2, SW_Q_HEADS), f32),
        "rel_bias": 0.5 * jax.random.normal(ks[13], (REL_BUCKETS, SW_Q_HEADS), f32),
        "w_a": nrm(ks[14], (DEPTH_2, ML_V_W, D_MODEL), ML_V_W),
        "w_b": nrm(ks[15], (DEPTH_2, SW_Q_W, D_MODEL), SW_Q_W),
        "w_out": nrm(ks[16], (DEPTH_2, D_MODEL, D_MODEL), D_MODEL),
        "ffn2_norm": gain(ks[17], (DEPTH_2, D_MODEL)),
        "ffn2_wi": nrm(ks[18], (DEPTH_2, D_MODEL, 2 * D_FF), D_MODEL),
        "ffn2_wo": nrm(ks[19], (DEPTH_2, D_FF, D_MODEL), D_FF),
        "ple_norm": gain(ks[20], (DEPTH_2, D_MODEL)),
        "w_ple_gate": nrm(ks[21], (DEPTH_2, D_MODEL, D_MODEL), D_MODEL),
        "w_ple": nrm(ks[22], (DEPTH_2, P_DIM, D_MODEL), P_DIM),
    }

def second_block(x, p, ffn1_norm, ffn1_wi, ffn1_wo, mix_norm, w_in, b_igate, b_fgate, ml_out_norm,
              q_norm, k_norm, sinks, rel_bias, w_a, w_b, w_out, ffn2_norm, ffn2_wi, ffn2_wo,
              ple_norm, w_ple_gate, w_ple):
    B, S, _ = x.shape
    offsets = [int(o) for o in np.cumsum(SPLITS)[:-1]]
    for i in range(DEPTH_2):
        x = x + 0.5 * swiglu_ffn(rmsnorm_2(x, ffn1_norm[i]), ffn1_wi[i], ffn1_wo[i])
        u = rmsnorm_2(x, mix_norm[i])
        z = u @ w_in[i]
        mq, mk, mv, mo, mi, mf, sq, sk, sv, ga, gb = jnp.split(z, offsets, axis=-1)
        hA = mlstm_chunkwise(mq.reshape(B, S, ML_HEADS, ML_QK_DIM),
                             mk.reshape(B, S, ML_HEADS, ML_QK_DIM),
                             mv.reshape(B, S, ML_HEADS, ML_V_DIM),
                             mi + b_igate[i], mf + b_fgate[i])
        hA = rmsnorm_2(hA, ml_out_norm[i]).reshape(B, S, ML_V_W)
        yA = (jax.nn.sigmoid(mo) * hA) @ w_a[i]
        hB = swa_sink_attention(sq.reshape(B, S, SW_Q_HEADS, SW_HEAD_DIM),
                                sk.reshape(B, S, SW_KV_HEADS, SW_HEAD_DIM),
                                sv.reshape(B, S, SW_KV_HEADS, SW_HEAD_DIM),
                                q_norm[i], k_norm[i], sinks[i], rel_bias)
        yB = hB @ w_b[i]
        mixed = jax.nn.sigmoid(ga) * yA + jax.nn.sigmoid(gb) * yB
        x = x + mixed @ w_out[i]
        x = x + 0.5 * swiglu_ffn(rmsnorm_2(x, ffn2_norm[i]), ffn2_wi[i], ffn2_wo[i])
        gate = jax.nn.sigmoid(rmsnorm_2(x, ple_norm[i]) @ w_ple_gate[i])
        x = x + gate * (p[i] @ w_ple[i])
    return x


def setup_inputs(seed=0):
    out = dict(first_inputs(seed))
    for name, value in second_inputs(seed + 1).items():
        if name != "x":
            out[name + "_2"] = value
    return out


def reference(
    x, c, w_ada, b_ada, g_pre_mix, g_post_mix, g_pre_ffn, g_post_ffn, w_in, ret_decay_fwd,
    ret_decay_bwd, w_out, w_router, w_gate_e, w_up_e, w_down_e, p_2, ffn1_norm_2, ffn1_wi_2,
    ffn1_wo_2, mix_norm_2, w_in_2, b_igate_2, b_fgate_2, ml_out_norm_2, q_norm_2, k_norm_2,
    sinks_2, rel_bias_2, w_a_2, w_b_2, w_out_2, ffn2_norm_2, ffn2_wi_2, ffn2_wo_2, ple_norm_2,
    w_ple_gate_2, w_ple_2,
):
    x = first_block(
        x, c, w_ada, b_ada, g_pre_mix, g_post_mix, g_pre_ffn, g_post_ffn, w_in, ret_decay_fwd,
        ret_decay_bwd, w_out, w_router, w_gate_e, w_up_e, w_down_e,
    )
    return second_block(
        x, p_2, ffn1_norm_2, ffn1_wi_2, ffn1_wo_2, mix_norm_2, w_in_2, b_igate_2, b_fgate_2,
        ml_out_norm_2, q_norm_2, k_norm_2, sinks_2, rel_bias_2, w_a_2, w_b_2, w_out_2,
        ffn2_norm_2, ffn2_wi_2, ffn2_wo_2, ple_norm_2, w_ple_gate_2, w_ple_2,
    )


_drawn_inputs = setup_inputs


def setup_inputs(seed=0):
    import zlib

    import numpy as np

    out = dict(_drawn_inputs(seed))
    spreads = {}
    factors = {'g_pre_mix': 3.146,
     'g_post_ffn': 8.0,
     'b_igate_2': 200.0,
     'ml_out_norm_2': 3.366,
     'q_norm_2': 8.0,
     'k_norm_2': 8.0,
     'sinks_2': 198.662,
     'ple_norm_2': 52.507,
     'rel_bias_2': 2.764,
     'ffn2_norm_2': 3.596}
    for name, (base, spread) in spreads.items():
        noise = np.random.default_rng([zlib.crc32(name.encode()), seed]).standard_normal(out[name].shape)
        drawn = base * np.exp(spread * noise) if base else spread * noise
        out[name] = __import__('jax').numpy.asarray(drawn.astype(out[name].dtype))
    for name, factor in factors.items():
        out[name] = (out[name] * factor).astype(out[name].dtype)
    return out
```

```python
import numpy as np
import concourse.bass as bass
from concourse import mybir
from contextlib import ExitStack

F32 = mybir.dt.float32
ALU = mybir.AluOpType
ACT = mybir.ActivationFunctionType
AX = mybir.AxisListType

P = 128
D = 1024
TOK = 256
NT = TOK // P
KT = D // P
MASKED = -1e30

RET_H, RET_DK, RET_DV = 4, 64, 128
ATT_H, DH = 8, 64
NE, CAP, FE = 16, 32, 2048
GROUP = 4
NQ = NE // GROUP
DFF = 2816
ML_H, ML_DV = 4, 128
SW_H, SW_KV = 8, 2
LAYERS = 2
BUCKETS, WINDOW = 32, 128
HALF = D // 2

R = 12
SLOT = 2048
ADA_CHUNKS = 12
ADA_EARLY = 4
POS_ADA = 0
POS_WIN = POS_ADA + 2 * ADA_CHUNKS
POS_WOUT = POS_WIN + 12
POS_MOE = POS_WOUT + 4
EXPERT_SLOTS = 24
GROUP_SLOTS = GROUP * EXPERT_SLOTS
POS_LAYER = POS_MOE + NE * EXPERT_SLOTS
FFN_STEP = 256
FFN_STEPS = DFF // FFN_STEP
FFN_SUBS = 2 * FFN_STEPS
FFN_SLOTS = 3 * FFN_STEPS
Z_QK, Z_V, Z_O, Z_IF, Z_SK, Z_GA, Z_GB = 0, 512, 1024, 1536, 1928, 2312, 3336
Z_PIECES = [(Z_QK, 512), (Z_IF, Z_SK - Z_IF), (Z_SK, Z_GA - Z_SK), (Z_V, 512), (Z_O, 512),
            (Z_GA, 512), (Z_GA + 512, 512), (Z_GB, 512), (Z_GB + 512, 512)]
OFF_FFN1 = 0
OFF_Z = OFF_FFN1 + FFN_SLOTS
OFF_WA = OFF_Z + 2 * len(Z_PIECES)
OFF_WB = OFF_WA + 2
OFF_WO = OFF_WB + 2
OFF_FFN2 = OFF_WO + 4
OFF_PLE = OFF_FFN2 + FFN_SLOTS
LAYER_SLOTS = OFF_PLE + 4
assert LAYER_SLOTS % R == 0 and GROUP_SLOTS % R == 0 and 4 * 3 == R

CONST_PARTS = [("ident", P), ("causal", NT * TOK), ("cap_iota", CAP), ("minus_row", ML_H * P),
               ("rel_pos", NT * TOK), ("rel_neg", NT * TOK), ("ln_count", NT * TOK),
               ("dist", NT * TOK), ("bucket", 3 * P)]
CONST_AT, _n = {}, 0
for _name, _width in CONST_PARTS:
    CONST_AT[_name] = (_n, _width)
    _n += _width
NCONST = _n
NKEPT = CONST_AT["rel_pos"][0]

ARENA = 15480
PAR_PARTS = [("ffn1", KT), ("mix", KT), ("ffn2", KT), ("ple", KT), ("b_i", 1), ("b_f", 1),
             ("ml_gain", ML_H * ML_DV), ("q_gain", DH), ("k_gain", DH), ("sink", SW_H)]
PAR_AT, _n = {}, 0
for _name, _width in PAR_PARTS:
    PAR_AT[_name] = (_n, _width)
    _n += _width
NPAR = _n
NORMS = ("ffn1", "mix", "ffn2", "ple")


def norm_turn(name, l=0):
    first = ("pre", "post", "moe", "last")
    if name in first:
        return first.index(name) + 1
    return l * len(NORMS) + (len(first) + NORMS.index(name) + 1)


def turned_turn(name, l=0):
    first, layer = ("pre", "y", "moe"), ("ffn1", "mix", "mixed", "ffn2", "ple")
    if name in first:
        return first.index(name)
    return l * len(layer) + (len(first) + layer.index(name))


class Signals:

    def __init__(self, nc, ctx):
        self.nc, self.ctx, self.by_name = nc, ctx, {}

    def __getitem__(self, name):
        if name not in self.by_name:
            self.by_name[name] = self.ctx.enter_context(self.nc.semaphore(name))
        return self.by_name[name]


class InOrder:

    def __init__(self, engine, program):
        self.engine, self.program, self.open = engine, program, False

    def settle(self):
        if self.open:
            self.engine.drain()
            self.open = False

    def wait_ge(self, signal, value):
        self.settle()
        self.program.wait_ge(signal, value)

    def run(self, instruction, *args, **kwargs):
        self.settle()
        self.open = True
        return instruction(*args, **kwargs)

    def loop(self, turns):
        self.settle()
        with self.program.Fori(0, turns) as i:
            yield i
            self.settle()


def build(nc, a, const, skew, out):
    ctx = ExitStack()
    with ctx:
        S = Signals(nc, ctx)

        def sb(name, shape):
            return ctx.enter_context(nc.sbuf_tensor(name, shape, F32))

        ring = sb("ring", [P, R, SLOT])
        cst = sb("cst", [P, NKEPT])
        x = sb("x", [P, NT, D])
        hn = sb("hn", [P, NT, D])
        hT = sb("hT", [P, KT, TOK])
        ones = sb("ones", [P, P])
        zeros = sb("zeros", [P, TOK])
        halves = sb("halves", [P, 24])
        eps_rms = sb("eps_rms", [P, 24])
        eps_group = sb("eps_group", [P, 8])
        spare = sb("spare", [P, 4])
        ms = sb("ms", [P, NT])
        ms_post = sb("ms_post", [P, NT])
        head_ms = sb("head_ms", [P, 8])
        head_mean = sb("head_mean", [P, 8])
        cur = sb("cur", [P, NPAR])
        relb = sb("relb", [BUCKETS + 1, SW_H])
        wide = sb("wide", [P, 4, D])
        p_rows = sb("p_rows", [P, NT, TOK])
        arena = sb("arena", [P, ARENA])
        PS = ctx.enter_context(nc.psum_tensor("PS", [P, 8, 512], F32))

        class Region:

            def __init__(self, at):
                self.at = at

            def take(self, *dims):
                n = int(np.prod(dims))
                v = arena[:, self.at:self.at + n]
                self.at += n
                assert self.at <= ARENA, self.at
                if len(dims) == 2:
                    v = v.rearrange("p (a b) -> p a b", a=dims[0])
                elif len(dims) == 3:
                    v = v.rearrange("p (a b c) -> p a b c", a=dims[0], b=dims[1])
                return v

        def con(name, a_=None):
            at, n = CONST_AT[name]
            v = cst[:, at:at + n]
            return v.rearrange("p (a b) -> p a b", a=a_) if a_ else v

        def p_(name):
            at, n = PAR_AT[name]
            return cur[:, at:at + n]

        ident = con("ident")

        def slot(pos, *dims):
            n = int(np.prod(dims))
            v = ring[:, pos % R, 0:n]
            return v.rearrange("p (a b) -> p a b", a=dims[0]) if len(dims) == 2 else v

        first = Region(0)
        mod = first.take(6, D)
        moe_start = 5 * D
        g_pre, g_post, g_pre_f, g_post_f = (wide[:, i, :] for i in range(4))
        small = first.take(64)
        c_col, c_tanh, silu_c = small[:, 0:8], small[:, 8:16], small[:, 16:24]
        lgt, lg_m, lg_a, lg = small[:, 24:32], small[:, 32:40], small[:, 40:48], small[:, 48:56]
        ada = Region(first.at)
        c_wide = ada.take(KT, P)
        b_rows = ada.take(3 * 512)
        bucket = ada.take(3 * P)
        qkT = first.take(4, TOK)
        rv = first.take(NT, HALF)
        rg = first.take(NT, HALF)
        aqT = first.take(4, TOK)
        akT = first.take(4, TOK)
        av = first.take(NT, HALF)
        scores = first.take(4, NT * TOK)
        att_bias = first.take(NT, TOK)
        att_stat = first.take(3, ATT_H, NT)
        decay = arena[:, 0:RET_H * NT * TOK].rearrange("p (h n) -> p h n", h=RET_H)

        rg_tanh = qkT.rearrange("p a n -> p (a n)").rearrange("p (t n) -> p t n", t=NT)

        rel = scores[:, 0:2, :]
        ln_count, dist = cur[:, 0:NT * TOK], p_rows.rearrange("p t n -> p (t n)")
        router = Region(0)
        w_router = router.take(KT, NE)
        GT = router.take(NQ, TOK)
        onehot = router.take(NT, NE * CAP).rearrange("p t (e c) -> p t e c", e=NE)
        gated = router.take(NT, NE * CAP).rearrange("p t (e c) -> p t e c", e=NE)
        xe = router.take(KT, CAP)
        aff = router.take(NT, NE)
        place = router.take(NT, NE)
        rt_stat = router.take(3, NT)
        top8 = router.take(8)
        affT = router.take(TOK)
        chosen = router.take(TOK)
        count = router.take(TOK)
        e_act = router.take(512)
        assert router.at <= 5 * D
        gate_f = mod[:, 5, :]
        e_tanh = onehot[:, 0, :, :].rearrange("p e c -> p (e c)")
        e_hid = onehot[:, 1, :, :].rearrange("p e c -> p (e c)")
        e_hT = gated[:, 0, :, :].rearrange("p e c -> p (e c)").rearrange("p (s n) -> p s n", s=4)
        moe = Region(6 * D)
        xeT = moe.take(KT, NE * CAP)
        Y = moe.take(NQ, D)

        ffn = Region(0)
        f_tanh = ffn.take(2, TOK)
        f_act = ffn.take(2, TOK)
        f_hid = ffn.take(2, TOK)
        lay = Region(0)
        gates = lay.take(8, TOK)
        mqkT = lay.take(4, TOK)
        mva = lay.take(NT, ML_H, ML_DV + 1)
        mo = lay.take(NT, HALF)
        sq = lay.take(NT, HALF)
        sk = lay.take(NT, P)
        sv = lay.take(NT, P)
        kd = lay.take(NT, 2 * P)
        sqT = hn[:, 0, :].rearrange("p (a n) -> p a n", a=4)
        skT = lay.take(2, TOK)
        ga = lay.take(NT, D)
        gb = lay.take(NT, D)
        sw_s = lay.take(2, 3 * P)
        sw_pT = lay.take(2, 3 * P)
        ml_w = lay.take(ML_H, NT * TOK)
        qk_ms = lay.take(20)
        ml_cols = lay.take(2, NT, ML_H)
        ml_den = lay.take(8)
        sw_stat = lay.take(4, SW_H, NT)
        band = wide[:, 0:2, :].rearrange("p a (h n) -> p (a h) n", h=4)
        w_ple = wide[:, 2:4, :]
        pT = sq[:, 0, :].rearrange("p (j n) -> p j n", j=2)

        block = ctx.enter_context(nc.Block())
        FILLS = LAYER_SLOTS // R

        @block.sync
        def _(sp):
            def fill(pos, src, before=0):
                if pos >= R:
                    sp.wait_ge(S["slot_used"], before + (pos - R + 1))
                n = 1
                for s in src.shape[1:]:
                    n *= s
                dst = slot(pos, *src.shape[1:])
                sp.dma_start(dst, src).then_inc(S[f"slot{pos % R}_full"], 16)

            w_ada = a["w_ada"][0].rearrange("(p k) n -> p k n", k=KT)
            w_in = a["w_in"][0].rearrange("(p k) n -> p k n", k=KT)
            w_out = a["w_out"][0].rearrange("(p k) n -> p k n", k=KT)

            def columns(pos, w, col, width):
                for half in range(2):
                    fill(pos + half, w[:, 4 * half:4 * half + 4, col:col + width])

            for j in range(ADA_CHUNKS):
                columns(POS_ADA + 2 * j, w_ada, 512 * j, 512)
            for j in range(6):
                columns(POS_WIN + 2 * j, w_in, 512 * j, 512)
            for i in range(4):
                fill(POS_WOUT + i, w_out[:, 2 * i:2 * i + 2, :])

            with sp.Fori(0, NQ) as q:
                for r in range(GROUP):
                    pos = POS_MOE + r * EXPERT_SLOTS
                    for w, at in (("w_gate_e", 0), ("w_up_e", KT)):
                        rows = a[w][0, q * GROUP + r].rearrange("(p k) n -> p k n", k=KT)
                        for k in range(KT):
                            fill(pos + at + k, rows[:, k, :], q * GROUP_SLOTS)
                    rows = a["w_down_e"][0, q * GROUP + r].rearrange("(j p s) n -> p j s n", j=4, s=4)
                    for j in range(4):
                        for s in range(2):
                            fill(pos + 2 * KT + 2 * j + s, rows[:, j, 2 * s:2 * s + 2, :], q * GROUP_SLOTS)

            with sp.Fori(0, LAYERS) as l:
                def ffn(pos, wi, wo):
                    wi_l = a[wi][l].rearrange("(p k) n -> p k n", k=KT)

                    def step(i, at, before):
                        for part in range(2):
                            fill(at + part, wi_l[:, :, bass.ds(i * FFN_STEP + part * DFF, FFN_STEP)], before)
                        fill(at + 2, a[wo][l, bass.ds(i * FFN_STEP, FFN_STEP), :].rearrange(
                            "(u p) n -> p u n", u=2), before)

                    with sp.Fori(0, FFN_STEPS // 4) as b:
                        for i in range(4):
                            step(b * 4 + i, pos + 3 * i, l * LAYER_SLOTS + b * R)
                    for i in range(FFN_STEPS // 4 * 4, FFN_STEPS):
                        step(i, pos + 3 * i, l * LAYER_SLOTS)

                def rows_of(w, pos, k):
                    w_l = a[w][l].rearrange("(p k) n -> p k n", k=k)
                    for i in range(k // 2):
                        fill(pos + i, w_l[:, 2 * i:2 * i + 2, :], l * LAYER_SLOTS)

                ffn(POS_LAYER + OFF_FFN1, "ffn1_wi_2", "ffn1_wo_2")
                z = a["w_in_2"][l].rearrange("(p k) n -> p k n", k=KT)
                for j, (col, width) in enumerate(Z_PIECES):
                    for half in range(2):
                        fill(POS_LAYER + OFF_Z + 2 * j + half, z[:, 4 * half:4 * half + 4, col:col + width],
                             l * LAYER_SLOTS)
                rows_of("w_a_2", POS_LAYER + OFF_WA, 4)
                rows_of("w_b_2", POS_LAYER + OFF_WB, 4)
                rows_of("w_out_2", POS_LAYER + OFF_WO, KT)
                ffn(POS_LAYER + OFF_FFN2, "ffn2_wi_2", "ffn2_wo_2")
                rows_of("w_ple_gate_2", POS_LAYER + OFF_PLE, KT)

            sp.wait_ge(S["x_layer"], LAYERS + 1)
            sp.dma_start(out[0].rearrange("(t p) d -> p t d", p=P), x[:, :, :]).then_inc(S["stored"], 16)
            sp.wait_ge(S["stored"], 16)

        @block.gpsimd
        def _(pool):
            nc.gpsimd.memset(ones[:, :], 1.0).then_inc(S["ones"], 1)
            nc.gpsimd.memset(zeros[:, :], 0.0).then_inc(S["zeros"], 1)
            nc.gpsimd.memset(halves[:, :], -0.5).then_inc(S["halves"], 1)
            nc.gpsimd.memset(eps_rms[:, :], 1e-6).then_inc(S["halves"], 1)
            nc.gpsimd.memset(eps_group[:, :], 1e-5).then_inc(S["halves"], 1)
            nc.gpsimd.memset(relb[:, :], MASKED).then_inc(S["relb_masked"], 1)
            nc.gpsimd.memset(spare[:, 0:1], 0.0).then_inc(S["xe_free"], 1)
            nc.gpsimd.memset(spare[:, 1:2], 0.0).then_inc(S["y_copied"], 1)

            def inverse_root(need, turn, src, eps, signal):
                pool.wait_ge(S[need], turn)
                n = src.shape[1]
                nc.gpsimd.tensor_tensor(src, src, eps[:, 0:n], ALU.add)
                nc.gpsimd.drain()
                nc.gpsimd.tensor_tensor(src, src, halves[:, 0:n], ALU.pow).then_inc(S[signal], 1)

            def row_root(name, l=0):
                into = ms_post if name in ("post", "last") else ms
                inverse_root("mean_squares", norm_turn(name, l), into[:, :], eps_rms, "row_roots")

            pool.wait_ge(S["halves"], 3)
            row_root("pre")
            inverse_root("var_ret", 1, head_ms[:, :], eps_group, "head_roots")
            row_root("post")
            row_root("moe")
            row_root("last")
            with pool.Fori(0, LAYERS) as l:
                row_root("ffn1", l)
                row_root("mix", l)
                inverse_root("ms_qk", l + 1, qk_ms, eps_rms, "qk_roots")
                inverse_root("ms_ha", l + 1, head_ms[:, :], eps_rms, "head_roots")
                row_root("ffn2", l)
                row_root("ple", l)

        used = lambda pos: pos

        @block.scalar
        def _(program):
            act = InOrder(nc.scalar, program)
            activation = lambda *args, **kwargs: act.run(nc.scalar.activation, *args, **kwargs)

            def row(src):
                return src.partition_broadcast(P)

            program.dma_start(cst[:, :], const[:, 0:NKEPT]).then_inc(S["const_full"], 16)
            program.dma_start(x[:, :, :], a["x"][0].rearrange("(t p) d -> p t d", p=P)).then_inc(S["x_full"], 16)
            program.dma_start(c_col, a["c"][0].rearrange("(p k) -> p k", k=KT)).then_inc(S["c_full"], 16)
            for g in range(4):
                program.dma_start(b_rows[32 * g:32 * g + 1], a["b_ada"][0:1, 1536 * g:1536 * (g + 1)]).then_inc(
                    S["b_rows_full"], 16)
            act.wait_ge(S["relb_masked"], 1)
            program.dma_start(relb[0:BUCKETS, :], a["rel_bias_2"]).then_inc(S["relb_full"], 16)
            for name, dst in (("bucket", bucket), ("rel_pos", rel[:, 0, :]), ("rel_neg", rel[:, 1, :]),
                              ("dist", dist), ("ln_count", ln_count)):
                at, n = CONST_AT[name]
                program.dma_start(dst, const[:, at:at + n]).then_inc(S[name + "_full"], 16)
            for i, name in enumerate(("g_pre_mix", "g_post_mix", "g_pre_ffn", "g_post_ffn")):
                program.dma_start(wide[:, i, :], row(a[name][0])).then_inc(S["gains_full"], 16)
            for i, name in enumerate(("ret_decay_fwd", "ret_decay_bwd")):
                program.dma_start(lgt[:, 4 * i:4 * i + 4], row(a[name][0])).then_inc(S["decay_full"], 16)

            def square_sums(rows, into, need, values, scale=1.0 / 32):
                for t in range(NT):
                    act.wait_ge(S[need], values[t])
                    last = activation(hn[:, t, :], rows(t), ACT.Square, scale=scale,
                                        accum_out=into[:, t:t + 1])
                last.then_inc(S["mean_squares"], 1)

            def two_banks(b):
                return PS[:, b:b + 2, :].rearrange("p b n -> p (b n)")

            act.wait_ge(S["c_full"], 16)
            activation(c_tanh, c_col, ACT.Tanh, scale=0.5).then_inc(S["c_tanh"], 1)
            square_sums(lambda t: x[:, t, :], ms, "x_full", (16, 16))
            act.wait_ge(S["rep"], 1)
            rep = arena[:, 3 * D:6 * D].rearrange("p (h n) -> p h n", h=SW_H)
            activation(rep, PS[:, 0:8, 0:3 * P], ACT.Copy).then_inc(S["rep_copied"], 1)
            act.wait_ge(S["rep_copied"], 1)
            program.dma_start(skew.rearrange("h p n -> p h n"), rep).then_inc(S["skew_written"], 16)

            def ada_copy(j):
                act.wait_ge(S["ada"], j + 1)
                activation(mod[:, j // 2, 512 * (j % 2):512 * (j % 2) + 512], PS[:, 6 + j % 2, :],
                             ACT.Copy).then_inc(S["ada_copied"], 1)

            for j in range(ADA_EARLY + 1):
                ada_copy(j)

            def plain_hT(name, base):
                for b in (0, 2):
                    act.wait_ge(S["turned"], 4 * turned_turn(name) + b + 1)
                    activation(hT[:, 2 * b:2 * b + 2, :], PS[:, base + b, :], ACT.Copy).then_inc(S["hT"], 1)

            act.wait_ge(S["lg_abs"], 1)
            activation(lg_a, lg_a, ACT.Exp, scale=-1.0)
            activation(lg_a, lg_a, ACT.Ln, bias=1.0).then_inc(S["lg_ln"], 1)
            act.wait_ge(S["skew_written"], 16)
            for j in range(ADA_EARLY + 1, ADA_CHUNKS):
                ada_copy(j)
            plain_hT("pre", 0)
            for h in range(RET_H):
                act.wait_ge(S["decay_arg"], h + 1)
                activation(decay[:, h, :], decay[:, h, :], ACT.Exp).then_inc(S["decay"], 1)
            for j, dst in ((0, qkT), (2, rg), (4, akT)):
                act.wait_ge(S["slot_used"], used(POS_WIN + 2 * j + 2))
                activation(dst.rearrange("p a n -> p (a n)"), two_banks(2 * (j % 3)), ACT.Copy).then_inc(
                    S[f"piece{j}_copied"], 1)
            act.wait_ge(S["ret_s"], RET_H)
            activation(rg_tanh, rg, ACT.Tanh, scale=0.5).then_inc(S["rg_tanh"], 1)

            def att_exp(h):
                act.wait_ge(S["att_scores"], h + 1)
                for t in range(NT):
                    last = activation(scores[:, h % 2, t * TOK:(t + 1) * TOK], scores[:, h % 2, t * TOK:(t + 1) * TOK],
                                        ACT.Exp, bias=att_stat[:, 0, h, t:t + 1],
                                        accum_out=att_stat[:, 1, h, t:t + 1])
                last.then_inc(S["att_p"], 1)

            def att_copy(h):
                act.wait_ge(S["att_t"], h + 1)
                if h >= 2:
                    act.wait_ge(S["att_av"], h - 1)
                activation(scores[:, 2 + h % 2, :], PS[:, h % 2, :], ACT.Copy).then_inc(S["att_pT"], 1)

            att_exp(0)
            for h in range(ATT_H):
                if h + 1 < ATT_H:
                    att_exp(h + 1)
                att_copy(h)
            plain_hT("y", 4)
            square_sums(lambda t: two_banks(2 * t), ms_post, "slot_used",
                        (used(POS_WOUT + 4),) * 2)
            act.wait_ge(S["x_mid"], 1)
            program.dma_start(w_router, a["w_router"][0].rearrange("(p k) e -> p k e", k=KT)).then_inc(
                S["router_full"], 16)
            square_sums(lambda t: x[:, t, :], ms, "x_mid", (1, 1))
            plain_hT("moe", 4)
            act.wait_ge(S["logits"], 1)
            act.wait_ge(S["logits_max"], 1)
            for t in range(NT):
                last = activation(aff[:, t, :], PS[:, 0, NE * t:NE * t + NE], ACT.Exp,
                                    bias=rt_stat[:, 0, t:t + 1], accum_out=rt_stat[:, 1, t:t + 1])
            last.then_inc(S["aff_exp"], 1)
            for k in range(0, KT, 2):
                act.wait_ge(S["gathered"], k + 1)
                activation(xeT[:, k, :], PS[:, k, :], ACT.Copy).then_inc(S["xeT"], 1)
            act.wait_ge(S["GT_ps"], 1)
            activation(GT.rearrange("p q n -> p (q n)"), two_banks(0), ACT.Copy).then_inc(S["GT"], 1)

            for q in act.loop(NQ):
                for r in range(GROUP):
                    pos = POS_MOE + r * EXPERT_SLOTS
                    before = q * GROUP_SLOTS
                    act.wait_ge(S["slot_used"], before + used(pos + KT))
                    activation(e_tanh, PS[:, 2, :], ACT.Tanh, scale=0.5).then_inc(S["e_tanh"], 1)
                    act.wait_ge(S["e_tr"], q * GROUP + r + 1)
                    activation(e_hT.rearrange("p s n -> p (s n)"), PS[:, 4, :], ACT.Copy).then_inc(S["e_hT"], 1)
                    act.wait_ge(S["slot_used"], before + used(pos + EXPERT_SLOTS))
                    for g in range(4):
                        last = activation(Y[32 * r:32 * r + 32, bass.ds(q, 1), 256 * g:256 * g + 256],
                                            PS[32 * g:32 * g + 32, 5, 0:256], ACT.Copy)
                    last.then_inc(S["y_copied"], 1)
            square_sums(lambda t: two_banks(2 * t), ms_post, "combined", (1, 1))

            act.wait_ge(S["x_layer"], 1)
            act.wait_ge(S["skew_written"], 16)
            program.dma_start(band, bass.AP(skew.tensor, P, [[3 * P - 1, P], [3 * P * P, SW_H], [1, TOK]])).then_inc(
                S["band_full"], 16)

            def norm(name, need, values, l):
                square_sums(lambda t: x[:, t, :], ms, need, values)
                act.wait_ge(S["row_roots"], norm_turn(name, l))
                activation(hn[:, 0, :], x[:, 0, :], ACT.Copy, scale=ms[:, 0:1]).then_inc(S["hn"], 1)

            def norm_T(name, l):
                for b in (0, 2):
                    act.wait_ge(S["turned"], 4 * turned_turn(name, l) + (b + 1))
                    for k in (2 * b, 2 * b + 1):
                        last = activation(hT[:, k, :], PS[:, 4 + b, (k % 2) * TOK:(k % 2) * TOK + TOK], ACT.Copy,
                                            scale=p_(name)[:, k:k + 1])
                    last.then_inc(S["hT"], 1)

            def ffn_tanh(base):
                def sub(c, bank):
                    act.wait_ge(S["gate_up"], base + c + 1)
                    activation(f_tanh[:, bank % 2, :], PS[:, 4 + bank, 0:TOK], ACT.Tanh,
                                 scale=0.5).then_inc(S["f_tanh"], 1)

                for b in act.loop(FFN_SUBS // 4):
                    for i in range(4):
                        sub(b * 4 + i, i)
                for c in range(FFN_SUBS // 4 * 4, FFN_SUBS):
                    sub(c, c % 4)

            for l in act.loop(LAYERS):
                before = l * LAYER_SLOTS
                act.wait_ge(S["x_layer"], l + 1)
                for name in NORMS:
                    program.dma_start(p_(name), a[{"mix": "mix_norm_2", "ple": "ple_norm_2"}.get(
                        name, name + "_norm_2")][l].rearrange("(p k) -> p k", k=KT)).then_inc(S["par_full"], 16)
                for name, src in (("b_i", "b_igate_2"), ("b_f", "b_fgate_2")):
                    program.dma_start(p_(name)[0:ML_H, :], a[src][l].rearrange("(h o) -> h o", o=1)).then_inc(
                        S["par_full"], 16)
                program.dma_start(p_("ml_gain"), row(a["ml_out_norm_2"][l].rearrange("h d -> (h d)"))).then_inc(
                    S["par_full"], 16)
                for name, src in (("q_gain", "q_norm_2"), ("k_gain", "k_norm_2"), ("sink", "sinks_2")):
                    program.dma_start(p_(name), row(a[src][l])).then_inc(S["par_full"], 16)
                program.dma_start(w_ple, a["w_ple_2"][l].rearrange("(j p) n -> p j n", p=P)).then_inc(S["ple_full"], 16)
                program.dma_start(p_rows[:, :, :], a["p_2"][l, 0].rearrange("(t p) n -> p t n", p=P)).then_inc(
                    S["ple_full"], 16)
                norm("ffn1", "x_layer", (l + 1, l + 1), l)
                act.wait_ge(S["par_full"], (l + 1) * 16 * 10)
                norm_T("ffn1", l)
                ffn_tanh(l * 2 * FFN_SUBS)
                norm("mix", "x_ffn1", (2 * l + 1, 2 * l + 2), l)
                norm_T("mix", l)

                zpos = POS_LAYER + OFF_Z
                act.wait_ge(S["slot_used"], before + used(zpos + 2))
                activation(mqkT.rearrange("p a n -> p (a n)"), two_banks(6), ACT.Copy).then_inc(S["mqkT"], 1)
                act.wait_ge(S["slot_used"], before + used(zpos + 4))
                act.wait_ge(S["gate_f"], l + 1)
                activation(gates[0:ML_H, 0, :], PS[0:ML_H, 2, 0:TOK], ACT.Identity,
                             bias=p_("b_i")[0:ML_H, :]).then_inc(S["gate_i"], 1)
                activation(sq[:, :, 0:384], PS[:, 0:2, 0:384], ACT.Copy).then_inc(S["sq_copied"], 1)
                act.wait_ge(S["f_abs"], l + 1)
                activation(gates[0:ML_H, 4, :], gates[0:ML_H, 3, :], ACT.Exp, scale=-1.0)
                activation(gates[0:ML_H, 4, :], gates[0:ML_H, 4, :], ACT.Ln, bias=1.0).then_inc(S["f_ln"], 1)
                act.wait_ge(S["slot_used"], before + used(zpos + 10))
                activation(mo.rearrange("p t n -> p (t n)"), two_banks(2), ACT.Tanh, scale=0.5).then_inc(
                    S["mo"], 1)
                act.wait_ge(S["tq"], l + 1)
                activation(sqT.rearrange("p a n -> p (a n)"), two_banks(6), ACT.Copy).then_inc(S["sqT"], 1)
                act.wait_ge(S["ml_cols_ps"], l + 1)
                act.wait_ge(S["ml_a"], l + 1)
                activation(ml_cols[:, 1, :, :], PS[:, 0, 8:16].rearrange("p (t h) -> p t h", t=NT), ACT.Exp,
                             scale=-1.0).then_inc(S["exp_minus_m"], 1)

                def sw_exp(h):
                    act.wait_ge(S["sw_scores"], l * SW_H + h + 1)
                    for t, (lo, hi) in ((1, (0, TOK)), (0, (TOK, 3 * P))):
                        last = activation(sw_s[:, h % 2, lo:hi], sw_s[:, h % 2, lo:hi], ACT.Exp,
                                            bias=sw_stat[:, 0, h, t:t + 1], accum_out=sw_stat[:, 1, h, t:t + 1])
                    last.then_inc(S["sw_p"], 1)

                def sw_copy(h):
                    act.wait_ge(S["sw_t"], l * SW_H + h + 1)
                    if h >= 2:
                        act.wait_ge(S["sw_av"], l * SW_H + h - 1)
                    activation(sw_pT[:, h % 2, :], PS[:, 2 + h % 2, 0:3 * P], ACT.Copy).then_inc(S["sw_pT"], 1)

                def g_half(i):
                    j, t = i // 2, i % 2
                    if t == 0:
                        act.wait_ge(S["g_first"], l * 4 + j + 1)
                    else:
                        act.wait_ge(S["slot_used"], before + used(zpos + 10 + 2 * j + 2))
                    activation((ga, gb)[j // 2][:, t, 512 * (j % 2):512 * (j % 2) + 512], PS[:, 4 + t, :],
                                 ACT.Tanh, scale=0.5).then_inc(S["g_copied"], 1)

                sw_exp(0)
                for h in range(SW_H):
                    if h + 1 < SW_H:
                        sw_exp(h + 1)
                    sw_copy(h)
                    g_half(h)
                act.wait_ge(S["sink_arg"], l + 1)
                activation(sw_stat[:, 2, :, :], sw_stat[:, 2, :, :], ACT.Exp).then_inc(S["sink_exp"], 1)
                for h in range(ML_H):
                    act.wait_ge(S["ml_arg"], l * ML_H + h + 1)
                    for st in range(NT):
                        last = activation(ml_w[:, h, st * TOK:(st + 1) * TOK], ml_w[:, h, st * TOK:(st + 1) * TOK],
                                            ACT.Exp, bias=ml_cols[:, 0, st, h:h + 1])
                    last.then_inc(S["ml_exp"], 1)
                act.wait_ge(S["tr_b"], l + 1)
                activation(hT[:, 4:8, :].rearrange("p k n -> p (k n)"), two_banks(2), ACT.Copy).then_inc(S["hT_b"], 1)
                act.wait_ge(S["tr_a"], l + 1)
                activation(hT[:, 0:4, :].rearrange("p k n -> p (k n)"), two_banks(0), ACT.Copy).then_inc(S["hT_a"], 1)
                for b in (0, 2):
                    act.wait_ge(S["turned"], 4 * turned_turn("mixed", l) + (b + 1))
                    activation(hT[:, 2 * b:2 * b + 2, :].rearrange("p k n -> p (k n)"), PS[:, 4 + b, :],
                                 ACT.Copy).then_inc(S["hT"], 1)
                norm("ffn2", "x_mix", (2 * l + 1, 2 * l + 2), l)
                norm_T("ffn2", l)
                ffn_tanh(l * 2 * FFN_SUBS + FFN_SUBS)
                norm("ple", "x_ffn2", (2 * l + 1, 2 * l + 2), l)
                norm_T("ple", l)
                act.wait_ge(S["pT_ps"], l + 1)
                activation(pT, PS[:, 0, :].rearrange("p (j n) -> p j n", j=2), ACT.Copy).then_inc(S["pT"], 1)
                act.wait_ge(S["slot_used"], before + used(POS_LAYER + OFF_PLE + 4))
                for t in range(NT):
                    activation(ga[:, t, :], two_banks(2 * t), ACT.Tanh, scale=0.5).then_inc(S["ple_tanh"], 1)

        @block.vector
        def _(program):
            V = nc.vector
            dve = InOrder(V, program)
            tt = lambda *args, **kwargs: dve.run(V.tensor_tensor, *args, **kwargs)
            ts = lambda *args, **kwargs: dve.run(V.tensor_scalar, *args, **kwargs)
            stt = lambda *args, **kwargs: dve.run(V.scalar_tensor_tensor, *args, **kwargs)

            def wide_of(v, n):
                return v.unsqueeze(len(v.shape)).to_broadcast(list(v.shape) + [n])

            def heads(v, h):
                return v.rearrange("p t (h d) -> p t h d", h=h)

            dve.wait_ge(S["c_tanh"], 1)
            dve.wait_ge(S["c_full"], 16)
            stt(silu_c, c_tanh, 1.0, c_col, ALU.add, ALU.mult)
            ts(c_wide, wide_of(silu_c, P), 0.5, None, ALU.mult).then_inc(S["c_wide"], 1)
            dve.wait_ge(S["decay_full"], 32)
            ts(lg_m, lgt, 0.0, None, ALU.min)
            stt(lg_a, lg_m, -2.0, lgt, ALU.mult, ALU.add).then_inc(S["lg_abs"], 1)
            dve.wait_ge(S["ada_copied"], ADA_EARLY)
            dve.wait_ge(S["gains_full"], 64)
            stt(mod[:, 1, :], mod[:, 1, :], 1.0, g_pre, ALU.add, ALU.mult)
            dve.wait_ge(S["row_roots"], norm_turn("pre"))
            dve.wait_ge(S["x_full"], 16)
            for t in range(NT):
                stt(hn[:, t, :], x[:, t, :], ms[:, t:t + 1], mod[:, 1, :], ALU.mult, ALU.mult)
            for t in range(NT):
                last = tt(hn[:, t, :], hn[:, t, :], mod[:, 0, :], ALU.add)
            last.then_inc(S["hn"], NT)

            def plain_hT(name, base):
                for b in (1, 3):
                    dve.wait_ge(S["turned"], 4 * turned_turn(name) + b + 1)
                    dve.run(V.tensor_copy, hT[:, 2 * b:2 * b + 2, :].rearrange("p k n -> p (k n)"),
                                  PS[:, base + b, :]).then_inc(S["hT"], 1)

            dve.wait_ge(S["ada_copied"], ADA_CHUNKS)
            tt(mod[:, 2, :], mod[:, 2, :], g_post, ALU.mult)
            stt(mod[:, 4, :], mod[:, 4, :], 1.0, g_pre_f, ALU.add, ALU.mult)
            tt(mod[:, 5, :], mod[:, 5, :], g_post_f, ALU.mult)
            plain_hT("pre", 0)
            dve.wait_ge(S["lg_ln"], 1)
            tt(lg, lg_m, lg_a, ALU.subtract)
            dve.wait_ge(S["const_full"], 16)
            dve.wait_ge(S["rel_pos_full"], 16)
            dve.wait_ge(S["rel_neg_full"], 16)
            for h in range(RET_H):
                ts(att_bias.rearrange("p a b -> p (a b)"), rel[:, 1, :], lg[:, 4 + h:5 + h], None, ALU.mult)
                stt(decay[:, h, :], rel[:, 0, :], lg[:, h:h + 1], att_bias.rearrange("p a b -> p (a b)"),
                    ALU.mult, ALU.add).then_inc(S["decay_arg"], 1)
            for j, dst in ((1, rv), (3, aqT), (5, av)):
                dve.wait_ge(S["slot_used"], used(POS_WIN + 2 * j + 2))
                b = 2 * (j % 3)
                dve.run(V.tensor_copy, dst.rearrange("p a n -> p (a n)"),
                              PS[:, b:b + 2, :].rearrange("p b n -> p (b n)")).then_inc(S[f"piece{j}_copied"], 1)
            for h in range(RET_H):
                dve.wait_ge(S["ret_s"], h + 1)
                dve.wait_ge(S["decay"], h + 1)
                stt(scores[:, h, :], PS[:, h, :], RET_DK ** -0.5, decay[:, h, :], ALU.mult,
                    ALU.mult).then_inc(S["ret_w"], 1)
            dve.wait_ge(S["rg_tanh"], 1)
            dve.wait_ge(S["piece2_copied"], 1)
            stt(rg, rg_tanh, 1.0, rg, ALU.add, ALU.mult)
            dve.wait_ge(S["ret_y"], 1)
            ret_out = PS[:, 0:2, :].rearrange("p t (h d) -> p t h d", h=RET_H)
            by_head = lambda v: v.rearrange("p (t h) -> p t h", t=NT)
            dve.run(V.reduce_sum, by_head(head_mean[:, :]), ret_out, AX.X)
            ts(head_mean[:, :], head_mean[:, :], -1.0 / RET_DV, None, ALU.mult)
            yc = heads(hn[:, :, 0:HALF], RET_H)
            tt(yc, ret_out, wide_of(by_head(head_mean[:, :]), RET_DV), ALU.add).then_inc(S["gn_read"], 1)
            stt(heads(hn[:, :, HALF:D], RET_H), yc, 1.0 / RET_DV, yc, ALU.mult, ALU.mult)
            dve.run(V.reduce_sum, by_head(head_ms[:, :]), heads(hn[:, :, HALF:D], RET_H), AX.X).then_inc(S["var_ret"], 1)
            dve.wait_ge(S["head_roots"], 1)
            tt(yc, yc, wide_of(by_head(head_ms[:, :]), RET_DV), ALU.mult)
            stt(hn[:, :, 0:HALF], hn[:, :, 0:HALF], 0.5, rg, ALU.mult, ALU.mult)

            dve.wait_ge(S["dist_full"], 16)
            dve.wait_ge(S["ln_count_full"], 16)
            for h in range(ATT_H):
                slope = 2.0 ** (-8.0 * (h + 1) / ATT_H)
                stt(att_bias.rearrange("p a b -> p (a b)"), dist, -slope, ln_count, ALU.mult, ALU.add)
                dve.wait_ge(S["att_s"], h + 1)
                if h >= 2:
                    dve.wait_ge(S["att_t"], h - 1)
                s_h = scores[:, h % 2, :].rearrange("p (t n) -> p t n", t=NT)
                stt(s_h, PS[:, 4 + h % 2, :].rearrange("p (t n) -> p t n", t=NT), DH ** -0.5, att_bias,
                    ALU.mult, ALU.add)
                dve.run(V.tensor_reduce, att_stat[:, 0, h, :], s_h, AX.X, ALU.max, negate=True).then_inc(S["att_scores"], 1)
            dve.wait_ge(S["att_p"], ATT_H)
            dve.run(V.reciprocal, att_stat[:, 2, :, :], att_stat[:, 1, :, :])
            dve.wait_ge(S["att_av"], ATT_H)
            tt(heads(hn[:, :, HALF:D], ATT_H), heads(PS[:, 2:4, :], ATT_H),
               wide_of(att_stat[:, 2, :, :].rearrange("p h t -> p t h"), DH), ALU.mult).then_inc(S["hn"], NT)
            plain_hT("y", 4)

            def add_normed(gate, signal, name):
                dve.wait_ge(S["row_roots"], norm_turn(name))
                for t in range(NT):
                    stt(hn[:, t, :], PS[:, 2 * t:2 * t + 2, :].rearrange("p b n -> p (b n)"), ms_post[:, t:t + 1],
                        gate, ALU.mult, ALU.mult)
                for t in range(NT):
                    last = tt(x[:, t, :], x[:, t, :], hn[:, t, :], ALU.add)
                last.then_inc(S[signal], 1)

            add_normed(mod[:, 2, :], "x_mid", "post")
            dve.wait_ge(S["row_roots"], norm_turn("moe"))
            for t in range(NT):
                stt(hn[:, t, :], x[:, t, :], ms[:, t:t + 1], mod[:, 4, :], ALU.mult, ALU.mult)
            for t in range(NT):
                last = tt(hn[:, t, :], hn[:, t, :], mod[:, 3, :], ALU.add)
            last.then_inc(S["hn"], NT)
            plain_hT("moe", 4)
            dve.wait_ge(S["logits"], 1)
            dve.run(V.tensor_reduce, rt_stat[:, 0, :], PS[:, 0, 0:NT * NE].rearrange("p (t e) -> p t e", t=NT), AX.X, ALU.max,
                            negate=True).then_inc(S["logits_max"], 1)
            dve.wait_ge(S["aff_exp"], 1)
            dve.run(V.reciprocal, rt_stat[:, 2, :], rt_stat[:, 1, :])
            tt(aff, aff, wide_of(rt_stat[:, 2, :], NE), ALU.mult).then_inc(S["aff"], 1)
            dve.wait_ge(S["affT_ps"], 1)
            dve.run(V.tensor_copy, affT[0:NE, :], PS[0:NE, 1, 0:TOK])
            for i in range(CAP // 8):
                dve.run(V.max, top8[0:NE, :], affT[0:NE, :])
                dve.run(V.match_replace, affT[0:NE, :], top8[0:NE, :], affT[0:NE, :], -1.0)
            ts(chosen[0:NE, :], affT[0:NE, :], -1.0, None, ALU.is_equal)
            dve.run(V.tensor_tensor_scan, count[0:NE, :], chosen[0:NE, :], zeros[0:NE, :], 0.0, ALU.add, ALU.add)
            tt(count[0:NE, :], count[0:NE, :], chosen[0:NE, :], ALU.mult)
            ts(affT[0:NE, :], count[0:NE, :], 1.0, None, ALU.subtract).then_inc(S["place_rows"], 1)
            dve.wait_ge(S["place_ps"], 1)
            dve.run(V.tensor_copy, place.rearrange("p t e -> p (t e)"), PS[:, 2, 0:NT * NE])
            for t in range(NT):
                tt(onehot[:, t, :, :], con("cap_iota").unsqueeze(1).to_broadcast([P, NE, CAP]),
                   wide_of(place[:, t, :], CAP), ALU.is_equal)
            for t in range(NT):
                last = tt(gated[:, t, :, :], onehot[:, t, :, :], wide_of(aff[:, t, :], CAP), ALU.mult)
            last.then_inc(S["onehot"], 1)
            for k in range(1, KT, 2):
                dve.wait_ge(S["gathered"], k + 1)
                dve.run(V.tensor_copy, xeT[:, k, :], PS[:, k, :]).then_inc(S["xeT"], 1)
            dve.wait_ge(S["xeT"], KT)

            for q in dve.loop(NQ):
                for r in range(GROUP):
                    e = q * GROUP + r
                    pos = POS_MOE + r * EXPERT_SLOTS
                    dve.wait_ge(S["xe_free"], e + 1)
                    dve.run(V.tensor_copy, xe, xeT[:, :, bass.ds(e * CAP, CAP)]).then_inc(S["xe"], 1)
                    dve.wait_ge(S["e_tanh"], e + 1)
                    stt(e_act, e_tanh, 1.0, PS[:, 2, :], ALU.add, ALU.mult)
                    dve.wait_ge(S["slot_used"], q * GROUP_SLOTS + used(pos + 2 * KT))
                    stt(e_hid, e_act, 0.5, PS[:, 3, :], ALU.mult, ALU.mult).then_inc(S["e_hid"], 1)
            add_normed(gate_f, "x_layer", "last")

            def norm(name, l):
                dve.wait_ge(S["row_roots"], norm_turn(name, l))
                ts(hn[:, 1, :], x[:, 1, :], ms[:, 1:2], None, ALU.mult).then_inc(S["hn"], 1)

            def norm_T(name, l):
                for b in (1, 3):
                    dve.wait_ge(S["turned"], 4 * turned_turn(name, l) + (b + 1))
                    tt(hT[:, 2 * b:2 * b + 2, :], PS[:, 4 + b, :].rearrange("p (k n) -> p k n", k=2),
                       wide_of(p_(name)[:, 2 * b:2 * b + 2], TOK), ALU.mult).then_inc(S["hT"], 1)

            def ffn_hidden(base):
                def sub(c, bank):
                    dve.wait_ge(S["f_tanh"], base + c + 1)
                    stt(f_act[:, bank % 2, :], f_tanh[:, bank % 2, :], 1.0, PS[:, 4 + bank, 0:TOK], ALU.add, ALU.mult)
                    tt(f_hid[:, bank % 2, :], f_act[:, bank % 2, :], PS[:, 4 + bank, TOK:2 * TOK],
                       ALU.mult).then_inc(S["f_hid"], 1)

                for b in dve.loop(FFN_SUBS // 4):
                    for i in range(4):
                        sub(b * 4 + i, i)
                for c in range(FFN_SUBS // 4 * 4, FFN_SUBS):
                    sub(c, c % 4)

            def add_rows(scale, signal):
                for t in range(NT):
                    stt(x[:, t, :], PS[:, 2 * t:2 * t + 2, :].rearrange("p b n -> p (b n)"), scale, x[:, t, :],
                        ALU.mult, ALU.add).then_inc(S[signal], 1)

            for l in dve.loop(LAYERS):
                before = l * LAYER_SLOTS
                norm("ffn1", l)
                dve.wait_ge(S["par_full"], (l + 1) * 16 * 10)
                norm_T("ffn1", l)
                ffn_hidden(l * 2 * FFN_SUBS)
                dve.wait_ge(S["slot_used"], before + used(POS_LAYER + OFF_FFN1 + FFN_SLOTS))
                add_rows(0.25, "x_ffn1")
                norm("mix", l)
                norm_T("mix", l)

                zpos = POS_LAYER + OFF_Z
                dve.run(V.memset, mva[:, :, :, ML_DV:ML_DV + 1], 1.0)
                dve.wait_ge(S["slot_used"], before + used(zpos + 4))
                G = lambda i: gates[0:ML_H, i, :]
                ts(G(1), PS[0:ML_H, 2, TOK:2 * TOK], p_("b_f")[0:ML_H, :], None, ALU.add).then_inc(S["gate_f"], 1)
                ts(G(2), G(1), 0.0, None, ALU.min)
                stt(G(3), G(2), -2.0, G(1), ALU.mult, ALU.add).then_inc(S["f_abs"], 1)
                dve.wait_ge(S["slot_used"], before + used(zpos + 6))
                dve.run(V.tensor_copy, sq[:, :, 384:512], PS[:, 4:6, 0:P])
                dve.run(V.tensor_copy, sk, PS[:, 4:6, P:2 * P])
                dve.run(V.tensor_copy, sv, PS[:, 4:6, 2 * P:3 * P]).then_inc(S["sk_copied"], 1)
                dve.wait_ge(S["f_ln"], l + 1)
                tt(G(5), G(2), G(4), ALU.subtract)
                dve.run(V.tensor_tensor_scan, G(6), G(5), zeros[0:ML_H, :], 0.0, ALU.add, ALU.add)
                dve.wait_ge(S["gate_i"], l + 1)
                tt(G(7), G(0), G(6), ALU.subtract)
                dve.run(V.tensor_tensor_scan, G(1), G(7), G(7), 0.0, ALU.max, ALU.max)
                tt(G(2), G(6), G(1), ALU.add).then_inc(S["scan"], 1)
                dve.wait_ge(S["sq_copied"], l + 1)
                by16 = lambda v: v.rearrange("p t (h d) -> p (t h) d", d=DH)
                tmp = hn[:, 0, :].rearrange("p (h d) -> p h d", d=DH)
                tmp_k = hn[:, 1, 0:TOK].rearrange("p (h d) -> p h d", d=DH)
                stt(tmp, by16(sq), 1.0 / DH, by16(sq), ALU.mult, ALU.mult)
                stt(tmp_k, by16(sk), 1.0 / DH, by16(sk), ALU.mult, ALU.mult)
                dve.run(V.reduce_sum, qk_ms[:, 0:16], tmp, AX.X)
                dve.run(V.reduce_sum, qk_ms[:, 16:20], tmp_k, AX.X).then_inc(S["ms_qk"], 1)
                dve.wait_ge(S["slot_used"], before + used(zpos + 8))
                dve.run(V.tensor_copy, mva[:, :, :, 0:ML_DV], heads(PS[:, 0:2, :], ML_H)).then_inc(S["mva"], 1)
                dve.wait_ge(S["qk_roots"], l + 1)
                tt(by16(sq), by16(sq), wide_of(qk_ms[:, 0:16], DH), ALU.mult)
                tt(by16(sk), by16(sk), wide_of(qk_ms[:, 16:20], DH), ALU.mult)
                kd_v = kd.rearrange("p t (g u d) -> p (t g) u d", g=SW_KV, u=2)
                for u in range(2):
                    tt(kd_v[:, :, u, :], by16(sk), p_("k_gain").unsqueeze(1).to_broadcast([P, 4, DH]), ALU.mult)
                tt(by16(sq), by16(sq), p_("q_gain").unsqueeze(1).to_broadcast([P, 16, DH]),
                   ALU.mult).then_inc(S["qk_normed"], 1)
                dve.wait_ge(S["tk"], l + 1)
                dve.run(V.tensor_copy, skT.rearrange("p g n -> p (g n)"), PS[:, 1, :]).then_inc(S["skT"], 1)
                dve.wait_ge(S["ml_cols_ps"], l + 1)
                dve.run(V.tensor_copy, ml_cols[:, 0, :, :], PS[:, 0, 0:8].rearrange("p (t h) -> p t h", t=NT)).then_inc(
                    S["ml_a"], 1)

                for h in range(SW_H):
                    dve.wait_ge(S["sw_sc"], l * SW_H + h + 1)
                    if h == 0:
                        dve.wait_ge(S["band_full"], 16)
                    else:
                        if h >= 2:
                            dve.wait_ge(S["sw_t"], l * SW_H + h - 1)
                    stt(sw_s[:, h % 2, 0:TOK], PS[:, h % 2, 0:TOK], DH ** -0.5, band[:, h, :], ALU.mult, ALU.add)
                    stt(sw_s[:, h % 2, TOK:3 * P], PS[:, h % 2, TOK:3 * P], DH ** -0.5, band[:, h, P:TOK],
                        ALU.mult, ALU.add)
                    dve.run(V.reduce_max, sw_stat[:, 0, h, 1:2], sw_s[:, h % 2, 0:TOK], AX.X)
                    dve.run(V.reduce_max, sw_stat[:, 0, h, 0:1], sw_s[:, h % 2, TOK:3 * P], AX.X)
                    ts(sw_stat[:, 0, h, :], sw_stat[:, 0, h, :], p_("sink")[:, h:h + 1], -1.0, ALU.max,
                       ALU.mult).then_inc(S["sw_scores"], 1)
                tt(sw_stat[:, 2, :, :], sw_stat[:, 0, :, :], wide_of(p_("sink"), NT), ALU.add).then_inc(
                    S["sink_arg"], 1)
                for h in range(ML_H):
                    if h % 2 == 0:
                        dve.wait_ge(S["neg_m"], l * 2 + h // 2 + 1)
                    m_h = PS[:, 4 + h // 2, (h % 2) * TOK:(h % 2) * TOK + TOK]
                    last = tt(ml_w[:, h, :].rearrange("p (s n) -> p s n", s=NT),
                              con("causal", NT), m_h.unsqueeze(1).to_broadcast([P, NT, TOK]), ALU.add)
                    last.then_inc(S["ml_arg"], 1)
                dve.wait_ge(S["sink_exp"], l + 1)
                tt(sw_stat[:, 3, :, :], sw_stat[:, 1, :, :], sw_stat[:, 2, :, :], ALU.add)
                dve.run(V.reciprocal, sw_stat[:, 3, :, :], sw_stat[:, 3, :, :])
                dve.wait_ge(S["sw_av"], (l + 1) * SW_H)
                tt(heads(hn[:, :, HALF:D], SW_H), heads(PS[:, 6:8, :], SW_H),
                   wide_of(sw_stat[:, 3, :, :].rearrange("p h t -> p t h"), DH), ALU.mult).then_inc(S["h_b"], 1)
                for h in range(ML_H):
                    dve.wait_ge(S["ml_exp"], l * ML_H + h + 1)
                    dve.wait_ge(S["ml_s"], l * ML_H + h + 1)
                    stt(ml_w[:, h, :], ml_w[:, h, :], 64 ** -0.5, PS[:, h, :], ALU.mult, ALU.mult).then_inc(
                        S["ml_w"], 1)
                dve.wait_ge(S["ml_av"], (l + 1) * ML_H)
                dve.wait_ge(S["exp_minus_m"], l + 1)
                den = ml_den.rearrange("p (t h) -> p t h", t=NT)
                num = lambda t, pair: PS[:, 6 + t - 2 * pair, 0:2 * (ML_DV + 1)].rearrange("p (h n) -> p h n", h=2)
                parts = [(t, pair) for t in range(NT) for pair in range(2)]
                den_of = lambda t, pair: den[:, t, 2 * pair:2 * pair + 2].unsqueeze(2)
                for t, pair in parts:
                    ts(den_of(t, pair), num(t, pair)[:, :, ML_DV:ML_DV + 1], -1.0, None, ALU.mult)
                for t, pair in parts:
                    tt(den_of(t, pair), den_of(t, pair), num(t, pair)[:, :, ML_DV:ML_DV + 1], ALU.max)
                tt(den, den, ml_cols[:, 1, :, :], ALU.max)
                dve.run(V.reciprocal, ml_den, ml_den)
                h_a = heads(hn[:, :, 0:HALF], ML_H)
                for t, pair in parts:
                        tt(h_a[:, t, 2 * pair:2 * pair + 2, :], num(t, pair)[:, :, 0:ML_DV],
                           wide_of(den[:, t, 2 * pair:2 * pair + 2], ML_DV), ALU.mult)
                stt(heads(sq, ML_H), h_a, 1.0 / ML_DV, h_a, ALU.mult, ALU.mult)
                dve.run(V.reduce_sum, by_head(head_ms[:, :]), heads(sq, ML_H), AX.X).then_inc(S["ms_ha"], 1)
                dve.wait_ge(S["mo"], l + 1)
                for t in range(NT):
                    stt(mo[:, t, :], mo[:, t, :], 1.0, p_("ml_gain"), ALU.add, ALU.mult)
                dve.wait_ge(S["head_roots"], l + 2)
                tt(h_a, h_a, wide_of(by_head(head_ms[:, :]), ML_DV), ALU.mult)
                tt(hn[:, :, 0:HALF], hn[:, :, 0:HALF], mo, ALU.mult).then_inc(S["h_a"], 1)
                dve.wait_ge(S["g_copied"], 8 * (l + 1))
                dve.wait_ge(S["slot_used"], before + used(POS_LAYER + OFF_WA + 2))
                for t in range(NT):
                    last = stt(ga[:, t, :], ga[:, t, :], 1.0, PS[:, 4 + 2 * t:6 + 2 * t, :].rearrange("p b n -> p (b n)"),
                               ALU.add, ALU.mult)
                last.then_inc(S["ya_read"], 1)
                dve.wait_ge(S["slot_used"], before + used(POS_LAYER + OFF_WB + 2))
                for t in range(NT):
                    stt(gb[:, t, :], gb[:, t, :], 1.0, PS[:, 2 * t:2 * t + 2, :].rearrange("p b n -> p (b n)"),
                        ALU.add, ALU.mult)
                    stt(hn[:, t, :], ga[:, t, :], 0.5, gb[:, t, :], ALU.mult, ALU.add).then_inc(S["hn"], 1)
                for b in (1, 3):
                    dve.wait_ge(S["turned"], 4 * turned_turn("mixed", l) + (b + 1))
                    dve.run(V.tensor_copy, hT[:, 2 * b:2 * b + 2, :].rearrange("p k n -> p (k n)"),
                                  PS[:, 4 + b, :]).then_inc(S["hT"], 1)
                dve.wait_ge(S["slot_used"], before + used(POS_LAYER + OFF_WO + 4))
                add_rows(0.5, "x_mix")
                norm("ffn2", l)
                norm_T("ffn2", l)
                ffn_hidden(l * 2 * FFN_SUBS + FFN_SUBS)
                dve.wait_ge(S["slot_used"], before + used(POS_LAYER + OFF_FFN2 + FFN_SLOTS))
                add_rows(0.25, "x_ffn2")
                norm("ple", l)
                norm_T("ple", l)
                dve.wait_ge(S["ple_tanh"], NT * (l + 1))
                dve.wait_ge(S["ple_up"], l + 1)
                for t in range(NT):
                    stt(ga[:, t, :], ga[:, t, :], 1.0, PS[:, 4 + 2 * t:6 + 2 * t, :].rearrange("p b n -> p (b n)"),
                        ALU.add, ALU.mult)
                for t in range(NT):
                    last = stt(x[:, t, :], ga[:, t, :], 0.5, x[:, t, :], ALU.mult, ALU.add)
                last.then_inc(S["x_layer"], 1)

        @block.tensor
        def _(pe):
            mm = nc.tensor.matmul

            def full(pos, fills=0):
                pe.wait_ge(S[f"slot{pos % R}_full"], fills + 16 * (pos // R + 1))

            def transpose_rows(name, base, l=0, also=None):
                pe.wait_ge(S["hn"], NT * (turned_turn(name, l) + 1))
                for k in range(KT):
                    for t in range(NT):
                        last = nc.tensor.transpose(PS[:, base + k // 2, (k % 2) * TOK + t * P:(k % 2) * TOK + (t + 1) * P],
                                                   hn[:, t, k:D:KT], ident)
                        if also and k + t == 0:
                            last.then_inc(*also)
                    if k % 2 == 1:
                        last.then_inc(S["turned"], 1)

            def rows_product(pos, slots, per_slot, banks, fills, lhs, signal=True):
                n_k = slots * per_slot
                for s in range(slots):
                    full(pos + s, fills)
                    w = slot(pos + s, per_slot, D)
                    for i in range(per_slot):
                        k = s * per_slot + i
                        for t in range(NT):
                            for n in range(2):
                                last = mm(PS[:, banks + 2 * t + n, :], lhs(k, t), w[:, i, 512 * n:512 * n + 512],
                                          start=(k == 0), stop=(k == n_k - 1))
                    last.then_inc(S["slot_used"], 1)

            hT_tile = lambda k, t: hT[:, k, t * P:(t + 1) * P]

            pe.wait_ge(S["const_full"], 16)
            pe.wait_ge(S["relb_full"], 16)
            pe.wait_ge(S["bucket_full"], 16)
            for h in range(SW_H):
                last = mm(PS[:, h, 0:3 * P], relb[:, h:h + 1].to_broadcast([BUCKETS + 1, P]),
                          bucket[0:BUCKETS + 1, :], start=True, stop=True)
            last.then_inc(S["rep"], 1)
            pe.wait_ge(S["rep_copied"], 1)
            pe.wait_ge(S["ones"], 1)
            pe.wait_ge(S["zeros"], 1)
            pe.wait_ge(S["b_rows_full"], 64)
            pe.wait_ge(S["c_wide"], 1)

            for j in range(ADA_CHUNKS):
                if j >= 2:
                    pe.wait_ge(S["ada_copied"], j - 1)
                g = 32 * (j // 3)
                last = mm(PS[:, 6 + j % 2, :], ones[g:g + 1, :], b_rows[g:g + 1, 512 * (j % 3):512 * (j % 3) + 512],
                          start=True, stop=False)
                if j >= 1:
                    last.then_inc(S["slot_used"], 2)
                for k in range(KT):
                    if k % 4 == 0:
                        full(POS_ADA + 2 * j + k // 4)
                    last = mm(PS[:, 6 + j % 2, :], c_wide[:, k, :], slot(POS_ADA + 2 * j + k // 4, 4, 512)[:, k % 4, :],
                              start=False, stop=(k == KT - 1))
                last.then_inc(S["ada"], 1)
            transpose_rows("pre", 0, also=(S["slot_used"], 2))
            pe.wait_ge(S["hT"], 4 * (turned_turn("pre") + 1))
            for j in range(6):
                pos = POS_WIN + 2 * j
                full(pos)
                full(pos + 1)
                b = 2 * (j % 3)
                if j >= 3:
                    pe.wait_ge(S[f"piece{j - 3}_copied"], 1)
                w = [slot(pos + k // 4, 4, 512)[:, k % 4, :] for k in range(KT)]
                for part in range(4 if j in (0, 3, 4) else NT):
                    for k in range(KT):
                        if j in (0, 3, 4):
                            last = mm(PS[:, b + part // 2, (part % 2) * TOK:(part % 2) * TOK + TOK],
                                      w[k][:, part * P:(part + 1) * P], hT[:, k, :], start=(k == 0), stop=(k == 7))
                        else:
                            last = mm(PS[:, b + part, :], hT_tile(k, part), w[k], start=(k == 0), stop=(k == 7))
                last.then_inc(S["slot_used"], 2)
            pe.wait_ge(S["piece0_copied"], 1)
            pe.wait_ge(S["piece3_copied"], 1)
            pe.wait_ge(S["piece4_copied"], 1)
            for h in range(RET_H):
                lo = 64 * (h % 2)
                for st in range(NT):
                    last = mm(PS[:, h, st * TOK:(st + 1) * TOK], qkT[lo:lo + 64, 2 + h // 2, st * P:(st + 1) * P],
                              qkT[lo:lo + 64, h // 2, :], start=True, stop=True)
                last.then_inc(S["ret_s"], 1)

            def att_s(h):
                lo = 64 * (h % 2)
                for t in range(NT):
                    last = mm(PS[:, 4 + h % 2, t * TOK:(t + 1) * TOK], aqT[lo:lo + 64, h // 2, t * P:(t + 1) * P],
                              akT[lo:lo + 64, h // 2, :], start=True, stop=True)
                last.then_inc(S["att_s"], 1)

            def att_av(h):
                pe.wait_ge(S["att_pT"], h + 1)
                for t in range(NT):
                    for st in range(NT):
                        last = mm(PS[:, 2 + t, h * DH:(h + 1) * DH],
                                  scores[:, 2 + h % 2, st * TOK + t * P:st * TOK + (t + 1) * P],
                                  av[:, st, h * DH:(h + 1) * DH], start=(st == 0), stop=(st == NT - 1))
                last.then_inc(S["att_av"], 1)

            pe.wait_ge(S["piece5_copied"], 1)
            att_s(0)
            att_s(1)
            pe.wait_ge(S["ret_w"], RET_H)
            for t in range(NT):
                for h in range(RET_H):
                    for st in range(NT):
                        last = mm(PS[:, t, h * P:(h + 1) * P], scores[:, h, st * TOK + t * P:st * TOK + (t + 1) * P],
                                  rv[:, st, h * P:(h + 1) * P], start=(st == 0), stop=(st == NT - 1))
            last.then_inc(S["ret_y"], 1)
            pe.wait_ge(S["gn_read"], 1)
            for h in range(ATT_H):
                pe.wait_ge(S["att_p"], h + 1)
                if h >= 2:
                    pe.wait_ge(S["att_pT"], h - 1)
                for st in range(NT):
                    for t in range(NT):
                        last = nc.tensor.transpose(PS[:, h % 2, st * TOK + t * P:st * TOK + (t + 1) * P],
                                                   scores[:, h % 2, t * TOK + st * P:t * TOK + (st + 1) * P], ident)
                last.then_inc(S["att_t"], 1)
                if h + 2 < ATT_H:
                    att_s(h + 2)
                if h >= 1:
                    att_av(h - 1)
            att_av(ATT_H - 1)
            transpose_rows("y", 4)
            pe.wait_ge(S["hT"], 4 * (turned_turn("y") + 1))
            rows_product(POS_WOUT, 4, 2, 0, 0, hT_tile)

            transpose_rows("moe", 4)
            pe.wait_ge(S["hT"], 4 * (turned_turn("moe") + 1))
            pe.wait_ge(S["router_full"], 16)
            for t in range(NT):
                for k in range(KT):
                    last = mm(PS[:, 0, t * NE:(t + 1) * NE], hT_tile(k, t), w_router[:, k, :], start=(k == 0),
                              stop=(k == KT - 1))
            last.then_inc(S["logits"], 1)
            pe.wait_ge(S["aff"], 1)
            for t in range(NT):
                last = nc.tensor.transpose(PS[0:NE, 1, t * P:(t + 1) * P], aff[:, t, :], ident)
            last.then_inc(S["affT_ps"], 1)
            pe.wait_ge(S["place_rows"], 1)
            for t in range(NT):
                last = nc.tensor.transpose(PS[:, 2, t * NE:(t + 1) * NE], affT[0:NE, t * P:(t + 1) * P],
                                           ident[0:NE, 0:NE])
            last.then_inc(S["place_ps"], 1)
            pe.wait_ge(S["onehot"], 1)
            for k in range(KT):
                for t in range(NT):
                    last = mm(PS[:, k, :], hn[:, t, k:D:KT], onehot[:, t, :, :].rearrange("p e c -> p (e c)"),
                              start=(t == 0), stop=(t == NT - 1))
                last.then_inc(S["gathered"], 1)
            pe.wait_ge(S["xeT"], KT)
            for q in range(NQ):
                for t in range(NT):
                    last = nc.tensor.transpose(
                        PS[:, q // 2, (q % 2) * TOK + t * P:(q % 2) * TOK + (t + 1) * P],
                        gated[:, t, GROUP * q:GROUP * q + GROUP, :].rearrange("p e c -> p (e c)"), ident)
            last.then_inc(S["GT_ps"], 1)

            with pe.Fori(0, NQ) as q:
                fills = q * (GROUP_SLOTS // R * 16)
                for r in range(GROUP):
                    e = q * GROUP + r
                    pos = POS_MOE + r * EXPERT_SLOTS
                    pe.wait_ge(S["xe"], e + 1)
                    for part in range(2):
                        for k in range(KT):
                            at = pos + part * KT + k
                            full(at, fills)
                            for g in range(4):
                                last = mm(PS[32 * g:32 * g + 32, 2 + part, :], xe[:, k, :],
                                          slot(at, SLOT)[:, 512 * g:512 * g + 512],
                                          start=(k == 0), stop=(k == KT - 1), tile_position=(0, 32 * g))
                            last.then_inc(S["slot_used"], 1)
                    pe.wait_ge(S["e_hid"], e + 1)
                    for s in range(4):
                        last = nc.tensor.transpose(PS[:, 4, s * P:(s + 1) * P], e_hid[:, s:512:4], ident)
                        if s == 0:
                            last.then_inc(S["xe_free"], 1)
                    last.then_inc(S["e_tr"], 1)
                    pe.wait_ge(S["e_hT"], e + 1)
                    pe.wait_ge(S["y_copied"], e + 1)
                    for j in range(4):
                        for s in range(4):
                            at = pos + 2 * KT + 2 * j + s // 2
                            if s % 2 == 0:
                                full(at, fills)
                            for g in range(4):
                                last = mm(PS[32 * g:32 * g + 32, 5, 0:256], e_hT[:, s, 32 * j:32 * j + 32],
                                          slot(at, 2, D)[:, s % 2, 256 * g:256 * g + 256],
                                          start=(j == 0 and s == 0), stop=(j == 3 and s == 3),
                                          tile_position=(0, 32 * g))
                            if s % 2 == 1:
                                last.then_inc(S["slot_used"], 1)
            pe.wait_ge(S["GT"], 1)
            pe.wait_ge(S["y_copied"], NE + 1)
            for t in range(NT):
                for n in range(2):
                    for q in range(NQ):
                        last = mm(PS[:, 2 * t + n, :], GT[:, q, t * P:(t + 1) * P], Y[:, q, 512 * n:512 * n + 512],
                                  start=(q == 0), stop=(q == NQ - 1))
            last.then_inc(S["combined"], 1)

            with pe.Fori(0, LAYERS) as l:
                layer_fills = l * (LAYER_SLOTS // R * 16)

                def ffn(pos, base):
                    for b in range(4):
                        mm(PS[:, b, 0:2], zeros[0:1, 0:P], zeros[0:1, 0:2], start=True, stop=False,
                           skip_group_check=True)

                    def up(c, fills):
                        i, u = c // 2, c % 2
                        for part in range(2):
                            at = pos + 3 * i + part
                            if u == 0:
                                full(at, fills)
                            w = slot(at, KT, FFN_STEP)
                            for k in range(KT):
                                last = mm(PS[:, 4 + c % 4, part * TOK:(part + 1) * TOK],
                                          w[:, k, u * P:(u + 1) * P], hT[:, k, :],
                                          start=(k == 0), stop=(k == KT - 1))
                            if part == 0 and u == 1:
                                last.then_inc(S["slot_used"], 1)
                        last.then_inc(S["gate_up"], 1)

                    def down(c, fills, turn):
                        i, u = c // 2, c % 2
                        pe.wait_ge(S["f_hid"], turn + c + 1)
                        if u == 0:
                            full(pos + 3 * i + 2, fills)
                        w = slot(pos + 3 * i + 2, 2, D)
                        for t in range(NT):
                            for n in range(2):
                                last = mm(PS[:, 2 * t + n, :], f_hid[:, c % 2, t * P:(t + 1) * P],
                                          w[:, u, 512 * n:512 * n + 512], start=False, stop=False,
                                          skip_group_check=True)
                                if t == 0 and n == 0 and (c + 1) % 2 == 1 and c + 1 < FFN_SUBS:
                                    last.then_inc(S["slot_used"], 1)
                        if u == 1:
                            last.then_inc(S["slot_used"], 1)

                    up(0, layer_fills)
                    with pe.Fori(0, FFN_STEPS // 4) as b:
                        for c in range(8):
                            up(c + 1, layer_fills + b * 16)
                            down(c, layer_fills + b * 16, base + b * 8)
                    for c in range(FFN_STEPS // 4 * 8, FFN_SUBS):
                        if c + 1 < FFN_SUBS:
                            up(c + 1, layer_fills)
                        down(c, layer_fills, base)

                transpose_rows("ffn1", 4, l)
                pe.wait_ge(S["hT"], 4 * (turned_turn("ffn1", l) + 1))
                ffn(POS_LAYER + OFF_FFN1, l * 2 * FFN_SUBS)
                transpose_rows("mix", 4, l)
                pe.wait_ge(S["hT"], 4 * (turned_turn("mix", l) + 1))

                zpos = POS_LAYER + OFF_Z

                def z_weights(j):
                    full(zpos + 2 * j, layer_fills)
                    full(zpos + 2 * j + 1, layer_fills)
                    width = Z_PIECES[j][1]
                    return [slot(zpos + 2 * j + k // 4, 4, width)[:, k % 4, :] for k in range(KT)]

                def z_rows(j, t, bank, w, lo, hi):
                    for k in range(KT):
                        last = mm(PS[:, bank, 0:hi - lo], hT_tile(k, t), w[k][:, lo:hi], start=(k == 0),
                                  stop=(k == KT - 1))
                    return last

                w = z_weights(0)
                for part in range(4):
                    for k in range(KT):
                        last = mm(PS[:, 6 + part // 2, (part % 2) * TOK:(part % 2) * TOK + TOK],
                                  w[k][:, part * P:(part + 1) * P], hT[:, k, :], start=(k == 0), stop=(k == KT - 1))
                last.then_inc(S["slot_used"], 2)
                w = z_weights(1)
                for g in range(2):
                    for k in range(KT):
                        mm(PS[0:ML_H, 2, g * TOK:(g + 1) * TOK], w[k][:, ML_H * g:ML_H * g + ML_H], hT[:, k, :],
                           start=(k == 0), stop=(k == KT - 1))
                for t in range(NT):
                    last = z_rows(1, t, t, w, 2 * ML_H, 2 * ML_H + 384)
                last.then_inc(S["slot_used"], 2)
                w = z_weights(2)
                for t in range(NT):
                    last = z_rows(2, t, 4 + t, w, 0, 384)
                last.then_inc(S["slot_used"], 2)
                w = z_weights(3)
                pe.wait_ge(S["sq_copied"], l + 1)
                for t in range(NT):
                    last = z_rows(3, t, t, w, 0, 512)
                last.then_inc(S["slot_used"], 2)
                w = z_weights(4)
                pe.wait_ge(S["gate_i"], l + 1)
                pe.wait_ge(S["gate_f"], l + 1)
                for t in range(NT):
                    last = z_rows(4, t, 2 + t, w, 0, 512)
                last.then_inc(S["slot_used"], 2)
                pe.wait_ge(S["mqkT"], l + 1)
                pe.wait_ge(S["qk_normed"], l + 1)
                for j in range(4):
                    for t in range(NT):
                        last = nc.tensor.transpose(PS[:, 6 + j // 2, (j % 2) * TOK + t * P:(j % 2) * TOK + (t + 1) * P],
                                                   sq[:, t, j * P:(j + 1) * P], ident)
                last.then_inc(S["tq"], 1)
                pe.wait_ge(S["scan"], l + 1)
                pe.wait_ge(S["mva"], l + 1)
                for g in range(SW_KV):
                    for t in range(NT):
                        last = nc.tensor.transpose(PS[:, 1, g * TOK + t * P:g * TOK + (t + 1) * P],
                                                   kd[:, t, g * P:(g + 1) * P], ident)
                last.then_inc(S["tk"], 1)
                for which, at in ((7, 0), (2, 8)):
                    for t in range(NT):
                        last = nc.tensor.transpose(PS[:, 0, at + ML_H * t:at + ML_H * t + ML_H],
                                                   gates[0:ML_H, which, t * P:(t + 1) * P], ident[0:ML_H, 0:ML_H])
                last.then_inc(S["ml_cols_ps"], 1)
                pe.wait_ge(S["sqT"], l + 1)
                pe.wait_ge(S["skT"], l + 1)
                pe.wait_ge(S["ml_a"], l + 1)
                pe.wait_ge(S["exp_minus_m"], l + 1)

                def sw_s_(h):
                    lo, g = 64 * (h % 2), h // (SW_H // SW_KV)
                    q_h, k_h = sqT[lo:lo + 64, h // 2, :], skT[lo:lo + 64, g, :]
                    mm(PS[:, h % 2, 0:TOK], q_h[:, P:TOK], k_h, start=True, stop=True)
                    mm(PS[:, h % 2, TOK:3 * P], q_h[:, 0:P], k_h[:, 0:P], start=True, stop=True).then_inc(
                        S["sw_sc"], 1)

                def sw_av(h):
                    g = h // (SW_H // SW_KV)
                    v = lambda st: sv[:, st, g * DH:(g + 1) * DH]
                    pe.wait_ge(S["sw_pT"], l * SW_H + h + 1)
                    mm(PS[:, 6, h * DH:(h + 1) * DH], sw_pT[:, h % 2, TOK:3 * P], v(0), start=True, stop=True)
                    mm(PS[:, 7, h * DH:(h + 1) * DH], sw_pT[:, h % 2, 0:P], v(0), start=True, stop=False)
                    mm(PS[:, 7, h * DH:(h + 1) * DH], sw_pT[:, h % 2, P:TOK], v(1), start=False, stop=True).then_inc(
                        S["sw_av"], 1)

                sw_s_(0)
                sw_s_(1)
                pe.wait_ge(S["mo"], l + 1)
                pe.wait_ge(S["sk_copied"], l + 1)
                for h in range(SW_H):
                    j, t = h // 2, h % 2
                    if t == 0:
                        w = z_weights(5 + j)
                    if h >= 2:
                        pe.wait_ge(S["g_copied"], l * 8 + h - 1)
                    last = z_rows(5 + j, t, 4 + t, w, 0, 512)
                    if t == 0:
                        last.then_inc(S["g_first"], 1)
                    else:
                        last.then_inc(S["slot_used"], 2)
                    pe.wait_ge(S["sw_p"], l * SW_H + h + 1)
                    if h >= 2:
                        pe.wait_ge(S["sw_pT"], l * SW_H + h - 1)
                    for at in (0, P, TOK):
                        last = nc.tensor.transpose(PS[:, 2 + h % 2, at:at + P], sw_s[:, h % 2, at:at + P], ident)
                    last.then_inc(S["sw_t"], 1)
                    if h + 2 < SW_H:
                        sw_s_(h + 2)
                    if h >= 1:
                        sw_av(h - 1)
                sw_av(SW_H - 1)
                pe.wait_ge(S["g_copied"], 8 * (l + 1))
                for h in range(ML_H):
                    last = mm(PS[:, 4 + h // 2, (h % 2) * TOK:(h % 2) * TOK + TOK],
                              con("minus_row")[0:ML_H, h * P:(h + 1) * P], gates[0:ML_H, 1, :], start=True, stop=True)
                    if h % 2 == 1:
                        last.then_inc(S["neg_m"], 1)
                for h in range(ML_H):
                    lo = 64 * (h % 2)
                    for st in range(NT):
                        last = mm(PS[:, h, st * TOK:(st + 1) * TOK], mqkT[lo:lo + 64, 2 + h // 2, st * P:(st + 1) * P],
                                  mqkT[lo:lo + 64, h // 2, :], start=True, stop=True)
                    last.then_inc(S["ml_s"], 1)
                pe.wait_ge(S["h_b"], l + 1)
                for h in range(ML_H):
                    if h == 2:
                        pe.wait_ge(S["ml_arg"], ML_H * (l + 1))
                    pe.wait_ge(S["ml_w"], l * ML_H + h + 1)
                    for t in range(NT):
                        for st in range(t + 1):
                            last = mm(PS[:, 6 + t - 2 * (h // 2), (h % 2) * (ML_DV + 1):(h % 2 + 1) * (ML_DV + 1)],
                                      ml_w[:, h, st * TOK + t * P:st * TOK + (t + 1) * P],
                                      mva[:, st, h, :], start=(st == 0), stop=(st == t))
                    last.then_inc(S["ml_av"], 1)

                def branch_T(lo, bank, signal):
                    for k in range(4):
                        for t in range(NT):
                            last = nc.tensor.transpose(
                                PS[:, bank + k // 2, (k % 2) * TOK + t * P:(k % 2) * TOK + (t + 1) * P],
                                hn[:, t, lo + k:lo + HALF:4], ident)
                    last.then_inc(S[signal], 1)

                branch_T(HALF, 2, "tr_b")
                pe.wait_ge(S["h_a"], l + 1)
                branch_T(0, 0, "tr_a")
                pe.wait_ge(S["hT_a"], l + 1)
                rows_product(POS_LAYER + OFF_WA, 2, 2, 4, layer_fills, hT_tile)
                pe.wait_ge(S["hT_b"], l + 1)
                rows_product(POS_LAYER + OFF_WB, 2, 2, 0, layer_fills, lambda k, t: hT_tile(4 + k, t))
                pe.wait_ge(S["ya_read"], l + 1)
                transpose_rows("mixed", 4, l)
                pe.wait_ge(S["hT"], 4 * (turned_turn("mixed", l) + 1))
                rows_product(POS_LAYER + OFF_WO, 4, 2, 0, layer_fills, hT_tile)
                transpose_rows("ffn2", 4, l)
                pe.wait_ge(S["hT"], 4 * (turned_turn("ffn2", l) + 1))
                ffn(POS_LAYER + OFF_FFN2, l * 2 * FFN_SUBS + FFN_SUBS)
                transpose_rows("ple", 4, l)
                pe.wait_ge(S["ple_full"], 32 * (l + 1))
                for j in range(2):
                    for t in range(NT):
                        last = nc.tensor.transpose(PS[:, 0, j * TOK + t * P:j * TOK + (t + 1) * P],
                                                   p_rows[:, t, j * P:(j + 1) * P], ident)
                last.then_inc(S["pT_ps"], 1)
                pe.wait_ge(S["hT"], 4 * (turned_turn("ple", l) + 1))
                pe.wait_ge(S["pT"], l + 1)
                for j in range(2):
                    for t in range(NT):
                        for n in range(2):
                            last = mm(PS[:, 4 + 2 * t + n, :], pT[:, j, t * P:(t + 1) * P],
                                      w_ple[:, j, 512 * n:512 * n + 512], start=(j == 0), stop=(j == 1))
                last.then_inc(S["ple_up"], 1)
                rows_product(POS_LAYER + OFF_PLE, 4, 2, 0, layer_fills, hT_tile)


_INS = [
    "x", "c", "w_ada", "b_ada", "g_pre_mix", "g_post_mix", "g_pre_ffn", "g_post_ffn", "w_in", "ret_decay_fwd",
    "ret_decay_bwd", "w_out", "w_router", "w_gate_e", "w_up_e", "w_down_e", "p_2", "ffn1_norm_2", "ffn1_wi_2",
    "ffn1_wo_2", "mix_norm_2", "w_in_2", "b_igate_2", "b_fgate_2", "ml_out_norm_2", "q_norm_2", "k_norm_2",
    "sinks_2", "rel_bias_2", "w_a_2", "w_b_2", "w_out_2", "ffn2_norm_2", "ffn2_wi_2", "ffn2_wo_2", "ple_norm_2",
    "w_ple_gate_2", "w_ple_2"]


def shape_constants():
    c = {name: np.zeros((P, n), np.float32) for name, n in CONST_PARTS}
    c["ident"][:] = np.eye(P)
    tile = lambda f: np.concatenate([f(i * P + np.arange(P)[:, None], np.arange(TOK)[None, :]) for i in range(NT)], 1)
    c["rel_pos"][:] = tile(lambda s, t: np.maximum(t - s, 0))
    c["rel_neg"][:] = tile(lambda s, t: np.maximum(s - t, 0))
    c["dist"][:] = tile(lambda i, j: np.abs(i - j))
    c["causal"][:] = tile(lambda s, t: np.where(s <= t, 0.0, MASKED))

    def count(i, j):
        n = np.zeros(np.broadcast(i, j).shape)
        for window, d in ((128, 1), (512, 4), (2048, 16)):
            n += ((i - j) % d == 0) & (np.abs(i - j) // d <= window // (2 * d))
        return np.where(n > 0, np.log(np.maximum(n, 1)), MASKED)

    c["ln_count"][:] = tile(count)
    c["cap_iota"][:] = np.arange(CAP)
    for h in range(ML_H):
        c["minus_row"][h, h * P:(h + 1) * P] = -1.0
    dist = 2 * P - np.arange(3 * P)
    exact = BUCKETS // 2
    d = np.maximum(dist, 0)
    large = exact + (np.log(np.maximum(d, 1) / exact) / np.log(128 / exact) * (BUCKETS - exact)).astype(np.int32)
    bucket = np.where(d < exact, d, np.minimum(large, BUCKETS - 1))
    bucket = np.where((dist >= 0) & (dist < WINDOW), bucket, BUCKETS)
    c["bucket"][bucket, np.arange(3 * P)] = 1.0
    return np.ascontiguousarray(np.concatenate([c[name] for name, _ in CONST_PARTS], 1))


def kernel(**inputs):
    import concourse.bacc as bacc
    from concourse.bass_utils import run_bass_kernel_spmd

    nc = bacc.Bacc("TRN2", target_bir_lowering=False, num_devices=1)
    arrays, args = {}, {}
    for name in _INS:
        v = np.ascontiguousarray(inputs[name])
        arrays[f"in_{name}"] = v
        args[name] = nc.dram_tensor(f"in_{name}", v.shape, mybir.dt.from_np(v.dtype), kind="ExternalInput").ap()
    arrays["shape_constants"] = shape_constants()
    const = nc.dram_tensor("shape_constants", (P, NCONST), F32, kind="ExternalInput").ap()
    skew = nc.dram_tensor("skew", (SW_H, P, 3 * P), F32, kind="Internal").ap()
    out = nc.dram_tensor("out", (1, TOK, D), F32, kind="ExternalOutput").ap()
    build(nc, args, const, skew, out)
    r = run_bass_kernel_spmd(nc, [arrays], core_ids=[0])
    return r.results[0]["out"]
```

```python
import numpy as np
import concourse.bass as bass
from concourse import mybir
from contextlib import ExitStack

F32 = mybir.dt.float32
ROUNDED = mybir.dt.float32r
ALU = mybir.AluOpType
ACT = mybir.ActivationFunctionType
AX = mybir.AxisListType

P = 128
D = 1024
TOK = 256
NT = TOK // P
KT = D // P
MASKED = -1e30

RET_H, RET_DK, RET_DV = 4, 64, 128
ATT_H, DH = 8, 64
NE, CAP, FE = 16, 32, 2048
GROUP = 4
NQ = NE // GROUP
DFF = 2816
ML_H, ML_DV = 4, 128
SW_H, SW_KV = 8, 2
LAYERS = 2
BUCKETS, WINDOW = 32, 128
HALF = D // 2

R = 6
SLOT = 2048
ADA_WIDTH = 4 * 512
ADA_SLOTS = 6 * D // ADA_WIDTH * KT
WIN_PIECES = 6
pos_win = lambda j: KT + 5 * j
pos_ada = lambda i: i if i < KT else pos_win((i - KT) // 3) + 2 + (i - KT) % 3
POS_WOUT = pos_ada(ADA_SLOTS - 1) + 1
POS_MOE = POS_WOUT + 4
EXPERT_SLOTS = 24
GROUP_SLOTS = GROUP * EXPERT_SLOTS
POS_LAYER = POS_MOE + NE * EXPERT_SLOTS
FFN_STEP = 256
FFN_STEPS = DFF // FFN_STEP
FFN_SUBS = 2 * FFN_STEPS
FFN_SLOTS = 3 * FFN_STEPS
FFN_PAIRS = FFN_STEPS // 2
FFN_UNITS = 3 * FFN_SUBS
UNIT = 1024
UNIT_BUFFERS = 4
Z_QK, Z_V, Z_O, Z_IF, Z_SK, Z_GA, Z_GB = 0, 512, 1024, 1536, 1928, 2312, 3336
Z_PIECES = [(Z_QK, 512), (Z_IF, Z_SK - Z_IF), (Z_SK, Z_GA - Z_SK), (Z_V, 512), (Z_O, 512),
            (Z_GA, 512), (Z_GA + 512, 512), (Z_GB, 512), (Z_GB + 512, 512)]
OFF_FFN1 = 0
OFF_Z = OFF_FFN1 + FFN_SLOTS
OFF_WA = OFF_Z + 2 * len(Z_PIECES)
OFF_WB = OFF_WA + 2
OFF_WO = OFF_WB + 2
OFF_FFN2 = OFF_WO + 4
OFF_PLE = OFF_FFN2 + FFN_SLOTS
LAYER_SLOTS = OFF_PLE + 4
assert LAYER_SLOTS % R == 0 and GROUP_SLOTS % R == 0 and 2 * 3 == R and FFN_STEPS % 2 == 1

CONST_PARTS = [("ident", P), ("causal", NT * TOK), ("cap_iota", CAP), ("minus_row", ML_H * P),
               ("rel_pos", NT * TOK), ("rel_neg", NT * TOK), ("ln_count", NT * TOK),
               ("dist", NT * TOK), ("bucket", 3 * P)]
CONST_AT, _n = {}, 0
for _name, _width in CONST_PARTS:
    CONST_AT[_name] = (_n, _width)
    _n += _width
NCONST = _n
NKEPT = CONST_AT["rel_pos"][0]

ARENA = 14488
PAR_PARTS = [("ffn1", KT), ("mix", KT), ("ffn2", KT), ("ple", KT), ("b_i", 1), ("b_f", 1),
             ("ml_gain", ML_H * ML_DV), ("q_gain", DH), ("k_gain", DH), ("sink", SW_H)]
PAR_AT, _n = {}, 0
for _name, _width in PAR_PARTS:
    PAR_AT[_name] = (_n, _width)
    _n += _width
NPAR = _n
NORMS = ("ffn1", "mix", "ffn2", "ple")


def gate_unit(c):
    return 3 * c - 1 if c else 0


def down_unit(c):
    return 3 * c + 4 if c < FFN_SUBS - 1 else FFN_UNITS - 1


def norm_turn(name, l=0):
    first = ("pre", "post", "moe", "last")
    if name in first:
        return first.index(name) + 1
    return l * len(NORMS) + (len(first) + NORMS.index(name) + 1)


def turned_turn(name, l=0):
    first, layer = ("pre", "y", "moe"), ("ffn1", "mix", "mixed", "ffn2", "ple")
    if name in first:
        return first.index(name)
    return l * len(layer) + (len(first) + layer.index(name))


class Signals:

    def __init__(self, nc, ctx):
        self.nc, self.ctx, self.by_name = nc, ctx, {}

    def __getitem__(self, name):
        if name not in self.by_name:
            self.by_name[name] = self.ctx.enter_context(self.nc.semaphore(name))
        return self.by_name[name]


class InOrder:

    def __init__(self, engine, program):
        self.engine, self.program, self.open = engine, program, False

    def settle(self):
        if self.open:
            self.engine.drain()
            self.open = False

    def wait_ge(self, signal, value):
        self.settle()
        self.program.wait_ge(signal, value)

    def run(self, instruction, *args, **kwargs):
        self.settle()
        self.open = True
        return instruction(*args, **kwargs)

    def loop(self, turns):
        self.settle()
        with self.program.Fori(0, turns) as i:
            yield i
            self.settle()


def build(nc, a, const, skew, out):
    ctx = ExitStack()
    with ctx:
        S = Signals(nc, ctx)

        def sb(name, shape):
            return ctx.enter_context(nc.sbuf_tensor(name, shape, F32))

        def sb_rounded(name, shape):
            return ctx.enter_context(nc.sbuf_tensor(name, shape, ROUNDED))

        ring = sb("ring", [P, R, SLOT])
        units = sb_rounded("units", [P, 2, UNIT_BUFFERS, UNIT])
        hT_split = sb_rounded("hT_split", [P, 2, KT, TOK])
        hid_split = sb_rounded("hid_split", [P, 2, 2, TOK])
        cst = sb("cst", [P, NKEPT])
        x = sb("x", [P, NT, D])
        hn = sb("hn", [P, NT, D])
        hT = sb("hT", [P, KT, TOK])
        zeros = sb("zeros", [P, TOK])
        halves = sb("halves", [P, 24])
        eps_rms = sb("eps_rms", [P, 24])
        eps_group = sb("eps_group", [P, 8])
        spare = sb("spare", [P, 4])
        ms = sb("ms", [P, NT])
        ms_post = sb("ms_post", [P, NT])
        head_ms = sb("head_ms", [P, 8])
        head_mean = sb("head_mean", [P, 8])
        cur = sb("cur", [P, NPAR])
        relb = sb("relb", [BUCKETS + 1, SW_H])
        wide = sb("wide", [P, 4, D])
        p_rows = sb("p_rows", [P, NT, TOK])
        arena = sb("arena", [P, ARENA])
        PS = ctx.enter_context(nc.psum_tensor("PS", [P, 8, 512], F32))

        class Region:

            def __init__(self, at):
                self.at = at

            def take(self, *dims):
                n = int(np.prod(dims))
                v = arena[:, self.at:self.at + n]
                self.at += n
                assert self.at <= ARENA, self.at
                if len(dims) == 2:
                    v = v.rearrange("p (a b) -> p a b", a=dims[0])
                elif len(dims) == 3:
                    v = v.rearrange("p (a b c) -> p a b c", a=dims[0], b=dims[1])
                return v

        def con(name, a_=None):
            at, n = CONST_AT[name]
            v = cst[:, at:at + n]
            return v.rearrange("p (a b) -> p a b", a=a_) if a_ else v

        def p_(name):
            at, n = PAR_AT[name]
            return cur[:, at:at + n]

        ident = con("ident")

        def slot(pos, *dims):
            n = int(np.prod(dims))
            v = ring[:, pos % R, 0:n]
            return v.rearrange("p (a b) -> p a b", a=dims[0]) if len(dims) == 2 else v

        first = Region(0)
        mod = first.take(6, D)
        moe_start = 5 * D
        g_pre, g_post, g_pre_f, g_post_f = (wide[:, i, :] for i in range(4))
        small = first.take(64)
        c_col, c_tanh, silu_c = small[:, 0:8], small[:, 8:16], small[:, 16:24]
        lgt, lg_m, lg_a, lg = small[:, 24:32], small[:, 32:40], small[:, 40:48], small[:, 48:56]
        bucket = Region(first.at).take(3 * P)
        ada = Region(2 * D)
        c_wide = ada.take(KT, 32)
        b_rows = ada.take(512)
        b_late = Region(3 * D).take(2, 512)
        ada_rows = [hn[:, 0, 0:512]] + [hT[:, 2 * i:2 * i + 2, :].rearrange("p k n -> p (k n)") for i in (1, 2)]
        qkT = first.take(4, TOK)
        rv = first.take(NT, HALF)
        rg = first.take(NT, HALF)
        aqT = first.take(4, TOK)
        akT = first.take(4, TOK)
        av = first.take(NT, HALF)
        scores = first.take(4, NT * TOK)
        att_bias = hT[:, 0:NT, :]
        att_stat = first.take(3, ATT_H, NT)
        decay = arena[:, 0:RET_H * NT * TOK].rearrange("p (h n) -> p h n", h=RET_H)

        rg_tanh = qkT.rearrange("p a n -> p (a n)").rearrange("p (t n) -> p t n", t=NT)

        rel = scores[:, 0:2, :]
        ln_count, dist = cur[:, 0:NT * TOK], p_rows.rearrange("p t n -> p (t n)")
        router = Region(0)
        w_router = router.take(KT, NE)
        GT = router.take(NQ, TOK)
        onehot = router.take(NT, NE * CAP).rearrange("p t (e c) -> p t e c", e=NE)
        gated = router.take(NT, NE * CAP).rearrange("p t (e c) -> p t e c", e=NE)
        xe = router.take(KT, CAP)
        aff = router.take(NT, NE)
        place = router.take(NT, NE)
        rt_stat = router.take(3, NT)
        top8 = router.take(8)
        affT = router.take(TOK)
        chosen = router.take(TOK)
        count = router.take(TOK)
        e_act = router.take(512)
        assert router.at <= 5 * D
        gate_f = mod[:, 5, :]
        e_tanh = onehot[:, 0, :, :].rearrange("p e c -> p (e c)")
        e_hid = onehot[:, 1, :, :].rearrange("p e c -> p (e c)")
        e_hT = gated[:, 0, :, :].rearrange("p e c -> p (e c)").rearrange("p (s n) -> p s n", s=4)
        moe = Region(6 * D)
        xeT = moe.take(KT, NE * CAP)
        Y = moe.take(NQ, D)

        ffn = Region(0)
        f_tanh = ffn.take(2, TOK)
        f_act = ffn.take(2, TOK)
        lay = Region(0)
        gates = lay.take(8, TOK)
        mqkT = lay.take(4, TOK)
        mva = lay.take(NT, ML_H, ML_DV + 1)
        mo = lay.take(NT, HALF)
        sq = lay.take(NT, HALF)
        sk = lay.take(NT, P)
        sv = lay.take(NT, P)
        sqT = hn[:, 0, :].rearrange("p (a n) -> p a n", a=4)
        skT = lay.take(2, TOK)
        ga = lay.take(NT, D)
        gb = lay.take(NT, D)
        sw_s = hn[:, 1, 0:6 * P].rearrange("p (a n) -> p a n", a=2)
        sw_pT = lay.take(2, 3 * P)
        kd = sw_pT.rearrange("p a n -> p (a n)")[:, 0:NT * 2 * P].rearrange("p (t n) -> p t n", t=NT)
        ml_w = lay.take(ML_H, NT * TOK)
        qk_ms = lay.take(20)
        ml_cols = lay.take(2, NT, ML_H)
        ml_den = lay.take(8)
        sw_stat = lay.take(4, SW_H, NT)
        band = wide[:, 0:2, :].rearrange("p a (h n) -> p (a h) n", h=4)
        w_ple = wide[:, 2:4, :]
        pT = sq[:, 0, :].rearrange("p (j n) -> p j n", j=2)

        def gate_up_weights(pos, c, part):
            return slot(pos + 3 * (c // 2) + part, KT, FFN_STEP)[:, :, (c % 2) * P:(c % 2 + 1) * P]

        def down_weights(pos, c):
            return slot(pos + 3 * (c // 2) + 2, 2, D)[:, c % 2, :]

        def unit(part, n, *dims):
            v = units[:, part, n % UNIT_BUFFERS, :]
            return v.rearrange("p (k n) -> p k n", k=KT) if dims else v

        block = ctx.enter_context(nc.Block())
        FILLS = LAYER_SLOTS // R

        @block.sync
        def _(sp):
            def fill(pos, src, before=0):
                if pos >= R:
                    sp.wait_ge(S["slot_used"], before + (pos - R + 1))
                n = 1
                for s in src.shape[1:]:
                    n *= s
                dst = slot(pos, *src.shape[1:])
                sp.dma_start(dst, src).then_inc(S[f"slot{pos % R}_full"], 16)

            w_ada = a["w_ada"][0].rearrange("(p k) n -> p k n", k=KT)
            w_in = a["w_in"][0].rearrange("(p k) n -> p k n", k=KT)
            w_out = a["w_out"][0].rearrange("(p k) n -> p k n", k=KT)

            def columns(pos, w, col, width):
                for half in range(2):
                    fill(pos + half, w[:, 4 * half:4 * half + 4, col:col + width])

            def ada_fill(i):
                fill(pos_ada(i), w_ada[:, i % KT, ADA_WIDTH * (i // KT):ADA_WIDTH * (i // KT + 1)])

            for i in range(KT):
                ada_fill(i)
            for j in range(WIN_PIECES):
                columns(pos_win(j), w_in, 512 * j, 512)
                for i in range(KT + 3 * j, min(KT + 3 * j + 3, ADA_SLOTS)):
                    ada_fill(i)
            for i in range(4):
                fill(POS_WOUT + i, w_out[:, 2 * i:2 * i + 2, :])

            with sp.Fori(0, NQ) as q:
                for r in range(GROUP):
                    pos = POS_MOE + r * EXPERT_SLOTS
                    for w, at in (("w_gate_e", 0), ("w_up_e", KT)):
                        rows = a[w][0, q * GROUP + r].rearrange("(p k) n -> p k n", k=KT)
                        for k in range(KT):
                            fill(pos + at + k, rows[:, k, :], q * GROUP_SLOTS)
                    rows = a["w_down_e"][0, q * GROUP + r].rearrange("(j p s) n -> p j s n", j=4, s=4)
                    for j in range(4):
                        for s in range(2):
                            fill(pos + 2 * KT + 2 * j + s, rows[:, j, 2 * s:2 * s + 2, :], q * GROUP_SLOTS)

            with sp.Fori(0, LAYERS) as l:
                def ffn(pos, wi, wo):
                    wi_l = a[wi][l].rearrange("(p k) n -> p k n", k=KT)

                    def step(i, at, before):
                        for part in range(2):
                            fill(at + part, wi_l[:, :, bass.ds(i * FFN_STEP + part * DFF, FFN_STEP)], before)
                        fill(at + 2, a[wo][l, bass.ds(i * FFN_STEP, FFN_STEP), :].rearrange(
                            "(u p) n -> p u n", u=2), before)

                    with sp.Fori(0, FFN_PAIRS) as b:
                        for i in range(2):
                            step(b * 2 + i, pos + 3 * i, l * LAYER_SLOTS + b * R)
                    step(FFN_STEPS - 1, pos + 3 * (FFN_STEPS - 1), l * LAYER_SLOTS)

                def rows_of(w, pos, k):
                    w_l = a[w][l].rearrange("(p k) n -> p k n", k=k)
                    for i in range(k // 2):
                        fill(pos + i, w_l[:, 2 * i:2 * i + 2, :], l * LAYER_SLOTS)

                ffn(POS_LAYER + OFF_FFN1, "ffn1_wi_2", "ffn1_wo_2")
                z = a["w_in_2"][l].rearrange("(p k) n -> p k n", k=KT)
                for j, (col, width) in enumerate(Z_PIECES):
                    for half in range(2):
                        fill(POS_LAYER + OFF_Z + 2 * j + half, z[:, 4 * half:4 * half + 4, col:col + width],
                             l * LAYER_SLOTS)
                rows_of("w_a_2", POS_LAYER + OFF_WA, 4)
                rows_of("w_b_2", POS_LAYER + OFF_WB, 4)
                rows_of("w_out_2", POS_LAYER + OFF_WO, KT)
                ffn(POS_LAYER + OFF_FFN2, "ffn2_wi_2", "ffn2_wo_2")
                rows_of("w_ple_gate_2", POS_LAYER + OFF_PLE, KT)

            sp.wait_ge(S["x_layer"], LAYERS + 1)
            sp.dma_start(out[0].rearrange("(t p) d -> p t d", p=P), x[:, :, :]).then_inc(S["stored"], 16)
            sp.wait_ge(S["stored"], 16)

        @block.gpsimd
        def _(pool):
            nc.gpsimd.memset(zeros[:, :], 0.0).then_inc(S["zeros"], 1)
            nc.gpsimd.memset(halves[:, :], -0.5).then_inc(S["halves"], 1)
            nc.gpsimd.memset(eps_rms[:, :], 1e-6).then_inc(S["halves"], 1)
            nc.gpsimd.memset(eps_group[:, :], 1e-5).then_inc(S["halves"], 1)
            nc.gpsimd.memset(relb[:, :], MASKED).then_inc(S["relb_masked"], 1)
            nc.gpsimd.memset(spare[:, 0:1], 0.0).then_inc(S["xe_free"], 1)
            nc.gpsimd.memset(spare[:, 1:2], 0.0).then_inc(S["y_copied"], 1)

            def inverse_root(need, turn, src, eps, signal):
                pool.wait_ge(S[need], turn)
                n = src.shape[1]
                nc.gpsimd.tensor_tensor(src, src, eps[:, 0:n], ALU.add)
                nc.gpsimd.drain()
                nc.gpsimd.tensor_tensor(src, src, halves[:, 0:n], ALU.pow).then_inc(S[signal], 1)

            def row_root(name, l=0):
                into = ms_post if name in ("post", "last") else ms
                inverse_root("mean_squares", norm_turn(name, l), into[:, :], eps_rms, "row_roots")

            pool.wait_ge(S["halves"], 3)
            row_root("pre")
            inverse_root("var_ret", 1, head_ms[:, :], eps_group, "head_roots")
            row_root("post")
            row_root("moe")
            row_root("last")
            with pool.Fori(0, LAYERS) as l:
                row_root("ffn1", l)
                row_root("mix", l)
                inverse_root("ms_qk", l + 1, qk_ms, eps_rms, "qk_roots")
                inverse_root("ms_ha", l + 1, head_ms[:, :], eps_rms, "head_roots")
                row_root("ffn2", l)
                row_root("ple", l)

        used = lambda pos: pos

        @block.scalar
        def _(program):
            act = InOrder(nc.scalar, program)
            activation = lambda *args, **kwargs: act.run(nc.scalar.activation, *args, **kwargs)

            def row(src):
                return src.partition_broadcast(P)

            program.dma_start(cst[:, :], const[:, 0:NKEPT]).then_inc(S["const_full"], 16)
            program.dma_start(x[:, :, :], a["x"][0].rearrange("(t p) d -> p t d", p=P)).then_inc(S["x_full"], 16)
            program.dma_start(c_col, a["c"][0].rearrange("(p k) -> p k", k=KT)).then_inc(S["c_full"], 16)
            for g in range(4):
                program.dma_start(b_rows[32 * g:32 * g + 32], a["b_ada"][0, 512 * g:512 * (g + 1)].partition_broadcast(
                    32)).then_inc(S["b_rows_full"], 16)
            act.wait_ge(S["relb_masked"], 1)
            program.dma_start(relb[0:BUCKETS, :], a["rel_bias_2"]).then_inc(S["relb_full"], 16)
            for name, dst in (("bucket", bucket), ("rel_pos", rel[:, 0, :]), ("rel_neg", rel[:, 1, :]),
                              ("dist", dist), ("ln_count", ln_count)):
                at, n = CONST_AT[name]
                program.dma_start(dst, const[:, at:at + n]).then_inc(S[name + "_full"], 16)
            for i, name in enumerate(("g_pre_mix", "g_post_mix", "g_pre_ffn", "g_post_ffn")):
                program.dma_start(wide[:, i, :], row(a[name][0])).then_inc(S["gains_full"], 16)
            for i, name in enumerate(("ret_decay_fwd", "ret_decay_bwd")):
                program.dma_start(lgt[:, 4 * i:4 * i + 4], row(a[name][0])).then_inc(S["decay_full"], 16)

            def square_sums(rows, into, need, values, scale=1.0 / 32):
                for t in range(NT):
                    act.wait_ge(S[need], values[t])
                    last = activation(hn[:, t, :], rows(t), ACT.Square, scale=scale,
                                        accum_out=into[:, t:t + 1])
                last.then_inc(S["mean_squares"], 1)

            def two_banks(b):
                return PS[:, b:b + 2, :].rearrange("p b n -> p (b n)")

            act.wait_ge(S["c_full"], 16)
            activation(c_tanh, c_col, ACT.Tanh, scale=0.5).then_inc(S["c_tanh"], 1)
            square_sums(lambda t: x[:, t, :], ms, "x_full", (16, 16))
            act.wait_ge(S["rep"], 1)
            rep = arena[:, 3 * D:6 * D].rearrange("p (h n) -> p h n", h=SW_H)
            activation(rep, PS[:, 0:8, 0:3 * P], ACT.Copy).then_inc(S["rep_copied"], 1)
            act.wait_ge(S["rep_copied"], 1)
            program.dma_start(skew.rearrange("h p n -> p h n"), rep).then_inc(S["skew_written"], 16)

            act.wait_ge(S["ada"], 1)
            activation(mod[:, 0, :], two_banks(0), ACT.Copy).then_inc(S["ada_copied"], 1)

            def ada_copy(h):
                act.wait_ge(S["ada"], h + 2)
                activation(mod[:, 2 + h // 2, 512 * (h % 2):512 * (h % 2) + 512], PS[:, 6 + h % 2, :],
                           ACT.Copy).then_inc(S["ada_copied"], 1)

            def plain_hT(name, base):
                for b in (0, 2):
                    act.wait_ge(S["turned"], 4 * turned_turn(name) + b + 1)
                    activation(hT[:, 2 * b:2 * b + 2, :], PS[:, base + b, :], ACT.Copy).then_inc(S["hT"], 1)

            act.wait_ge(S["lg_abs"], 1)
            activation(lg_a, lg_a, ACT.Exp, scale=-1.0)
            activation(lg_a, lg_a, ACT.Ln, bias=1.0).then_inc(S["lg_ln"], 1)
            act.wait_ge(S["skew_written"], 16)
            for g in range(4):
                program.dma_start(b_late[32 * g:32 * g + 32], a["b_ada"][0, ADA_WIDTH:3 * ADA_WIDTH].rearrange(
                    "(i g n) -> g i n", i=2, g=4)[g].partition_broadcast(32)).then_inc(S["b_late_full"], 16)
            plain_hT("pre", 0)
            for h in range(RET_H):
                act.wait_ge(S["decay_arg"], h + 1)
                activation(decay[:, h, :], decay[:, h, :], ACT.Exp).then_inc(S["decay"], 1)
            for j, dst in ((0, qkT), (2, rg), (4, akT)):
                act.wait_ge(S["slot_used"], used(pos_win(j) + 2))
                activation(dst.rearrange("p a n -> p (a n)"), two_banks(2 * (j % 3)), ACT.Copy).then_inc(
                    S[f"piece{j}_copied"], 1)
            act.wait_ge(S["ret_s"], RET_H)
            activation(rg_tanh, rg, ACT.Tanh, scale=0.5).then_inc(S["rg_tanh"], 1)

            def att_exp(h):
                act.wait_ge(S["att_scores"], h + 1)
                for t in range(NT):
                    last = activation(scores[:, h % 2, t * TOK:(t + 1) * TOK], scores[:, h % 2, t * TOK:(t + 1) * TOK],
                                        ACT.Exp, bias=att_stat[:, 0, h, t:t + 1],
                                        accum_out=att_stat[:, 1, h, t:t + 1])
                last.then_inc(S["att_p"], 1)

            def att_copy(h):
                act.wait_ge(S["att_t"], h + 1)
                if h >= 2:
                    act.wait_ge(S["att_av"], h - 1)
                activation(scores[:, 2 + h % 2, :], PS[:, h % 2, :], ACT.Copy).then_inc(S["att_pT"], 1)

            att_exp(0)
            for h in range(ATT_H):
                if h + 1 < ATT_H:
                    att_exp(h + 1)
                att_copy(h)
                ada_copy(h)
            plain_hT("y", 4)
            square_sums(lambda t: two_banks(2 * t), ms_post, "slot_used",
                        (used(POS_WOUT + 4),) * 2)
            act.wait_ge(S["x_mid"], 1)
            program.dma_start(w_router, a["w_router"][0].rearrange("(p k) e -> p k e", k=KT)).then_inc(
                S["router_full"], 16)
            square_sums(lambda t: x[:, t, :], ms, "x_mid", (1, 1))
            plain_hT("moe", 4)
            act.wait_ge(S["logits"], 1)
            act.wait_ge(S["logits_max"], 1)
            for t in range(NT):
                last = activation(aff[:, t, :], PS[:, 0, NE * t:NE * t + NE], ACT.Exp,
                                    bias=rt_stat[:, 0, t:t + 1], accum_out=rt_stat[:, 1, t:t + 1])
            last.then_inc(S["aff_exp"], 1)
            for k in range(0, KT, 2):
                act.wait_ge(S["gathered"], k + 1)
                activation(xeT[:, k, :], PS[:, k, :], ACT.Copy).then_inc(S["xeT"], 1)
            act.wait_ge(S["GT_ps"], 1)
            activation(GT.rearrange("p q n -> p (q n)"), two_banks(0), ACT.Copy).then_inc(S["GT"], 1)

            for q in act.loop(NQ):
                for r in range(GROUP):
                    pos = POS_MOE + r * EXPERT_SLOTS
                    before = q * GROUP_SLOTS
                    act.wait_ge(S["slot_used"], before + used(pos + KT))
                    activation(e_tanh, PS[:, 2, :], ACT.Tanh, scale=0.5).then_inc(S["e_tanh"], 1)
                    act.wait_ge(S["e_tr"], q * GROUP + r + 1)
                    activation(e_hT.rearrange("p s n -> p (s n)"), PS[:, 4, :], ACT.Copy).then_inc(S["e_hT"], 1)
                    act.wait_ge(S["slot_used"], before + used(pos + EXPERT_SLOTS))
                    for g in range(4):
                        last = activation(Y[32 * r:32 * r + 32, bass.ds(q, 1), 256 * g:256 * g + 256],
                                            PS[32 * g:32 * g + 32, 5, 0:256], ACT.Copy)
                    last.then_inc(S["y_copied"], 1)
            square_sums(lambda t: two_banks(2 * t), ms_post, "combined", (1, 1))

            act.wait_ge(S["x_layer"], 1)
            act.wait_ge(S["skew_written"], 16)
            program.dma_start(band, bass.AP(skew.tensor, P, [[3 * P - 1, P], [3 * P * P, SW_H], [1, TOK]])).then_inc(
                S["band_full"], 16)

            def split_hi(n, out, weights, slot_pos, c, base, fills):
                if n >= UNIT_BUFFERS:
                    act.wait_ge(S["unit_used"], base + (n - UNIT_BUFFERS + 1))
                if c % 2 == 0:
                    act.wait_ge(S[f"slot{slot_pos % R}_full"], fills + 16 * (slot_pos // R + 1))
                activation(out, weights, ACT.Copy).then_inc(S["unit_hi"], 1)

            def gate_up_hi(pos, c, base, fills):
                for part in range(2):
                    n = gate_unit(c) + part
                    split_hi(n, unit(0, n, KT), gate_up_weights(pos, c, part), pos + 3 * (c // 2) + part, c,
                             base, fills)

            def down_hi(pos, c, base, fills):
                n = down_unit(c)
                split_hi(n, unit(0, n), down_weights(pos, c), pos + 3 * (c // 2) + 2, c, base, fills)

            def norm(name, need, values, l):
                square_sums(lambda t: x[:, t, :], ms, need, values)
                act.wait_ge(S["row_roots"], norm_turn(name, l))
                activation(hn[:, 0, :], x[:, 0, :], ACT.Copy, scale=ms[:, 0:1]).then_inc(S["hn"], 1)

            def norm_T(name, l):
                for b in (0, 2):
                    act.wait_ge(S["turned"], 4 * turned_turn(name, l) + (b + 1))
                    for k in (2 * b, 2 * b + 1):
                        last = activation(hT[:, k, :], PS[:, 4 + b, (k % 2) * TOK:(k % 2) * TOK + TOK], ACT.Copy,
                                            scale=p_(name)[:, k:k + 1])
                    last.then_inc(S["hT"], 1)

            def norm_T_hi(name, l):
                for b in range(4):
                    act.wait_ge(S["turned"], 4 * turned_turn(name, l) + (b + 1))
                    for k in (2 * b, 2 * b + 1):
                        last = activation(hT_split[:, 0, k, :], PS[:, 4 + b, (k % 2) * TOK:(k % 2) * TOK + TOK],
                                          ACT.Copy, scale=p_(name)[:, k:k + 1])
                    last.then_inc(S["hT_hi"], 1)

            def ffn_tanh(pos, base, fills):
                def sub(c, base, fills):
                    act.wait_ge(S["unit_used"], base + (gate_unit(c) + 2))
                    activation(f_tanh[:, c % 2, :], PS[:, 4 + c % 4, 0:TOK], ACT.Tanh,
                                 scale=0.5).then_inc(S["f_tanh"], 1)
                    if c + 2 < FFN_SUBS:
                        gate_up_hi(pos, c + 2, base, fills)
                    if c + 1 < FFN_SUBS:
                        down_hi(pos, c + 1, base, fills)

                down_hi(pos, 0, base, fills)
                for b in act.loop(FFN_PAIRS):
                    for c in range(4):
                        sub(c, base + b * 12, fills + b * 16)
                for c in range(4 * FFN_PAIRS, FFN_SUBS):
                    sub(c, base, fills)

            for l in act.loop(LAYERS):
                before = l * LAYER_SLOTS
                act.wait_ge(S["x_layer"], l + 1)
                for name in NORMS:
                    program.dma_start(p_(name), a[{"mix": "mix_norm_2", "ple": "ple_norm_2"}.get(
                        name, name + "_norm_2")][l].rearrange("(p k) -> p k", k=KT)).then_inc(S["par_full"], 16)
                for name, src in (("b_i", "b_igate_2"), ("b_f", "b_fgate_2")):
                    program.dma_start(p_(name)[0:ML_H, :], a[src][l].rearrange("(h o) -> h o", o=1)).then_inc(
                        S["par_full"], 16)
                program.dma_start(p_("ml_gain"), row(a["ml_out_norm_2"][l].rearrange("h d -> (h d)"))).then_inc(
                    S["par_full"], 16)
                for name, src in (("q_gain", "q_norm_2"), ("k_gain", "k_norm_2"), ("sink", "sinks_2")):
                    program.dma_start(p_(name), row(a[src][l])).then_inc(S["par_full"], 16)
                program.dma_start(w_ple, a["w_ple_2"][l].rearrange("(j p) n -> p j n", p=P)).then_inc(S["ple_full"], 16)
                program.dma_start(p_rows[:, :, :], a["p_2"][l, 0].rearrange("(t p) n -> p t n", p=P)).then_inc(
                    S["ple_full"], 16)
                layer_fills = l * (LAYER_SLOTS // R * 16)
                norm("ffn1", "x_layer", (l + 1, l + 1), l)
                act.wait_ge(S["par_full"], (l + 1) * 16 * 10)
                norm_T_hi("ffn1", l)
                for c in range(2):
                    gate_up_hi(POS_LAYER + OFF_FFN1, c, l * 2 * FFN_UNITS, layer_fills)
                ffn_tanh(POS_LAYER + OFF_FFN1, l * 2 * FFN_UNITS, layer_fills)
                norm("mix", "x_ffn1", (2 * l + 1, 2 * l + 2), l)
                norm_T("mix", l)

                zpos = POS_LAYER + OFF_Z
                act.wait_ge(S["slot_used"], before + used(zpos + 2))
                activation(mqkT.rearrange("p a n -> p (a n)"), two_banks(6), ACT.Copy).then_inc(S["mqkT"], 1)
                act.wait_ge(S["slot_used"], before + used(zpos + 4))
                act.wait_ge(S["gate_f"], l + 1)
                activation(gates[0:ML_H, 0, :], PS[0:ML_H, 2, 0:TOK], ACT.Identity,
                             bias=p_("b_i")[0:ML_H, :]).then_inc(S["gate_i"], 1)
                activation(sq[:, :, 0:384], PS[:, 0:2, 0:384], ACT.Copy).then_inc(S["sq_copied"], 1)
                act.wait_ge(S["f_abs"], l + 1)
                activation(gates[0:ML_H, 4, :], gates[0:ML_H, 3, :], ACT.Exp, scale=-1.0)
                activation(gates[0:ML_H, 4, :], gates[0:ML_H, 4, :], ACT.Ln, bias=1.0).then_inc(S["f_ln"], 1)
                act.wait_ge(S["slot_used"], before + used(zpos + 10))
                activation(mo.rearrange("p t n -> p (t n)"), two_banks(2), ACT.Tanh, scale=0.5).then_inc(
                    S["mo"], 1)
                act.wait_ge(S["tq"], l + 1)
                activation(sqT.rearrange("p a n -> p (a n)"), two_banks(6), ACT.Copy).then_inc(S["sqT"], 1)
                act.wait_ge(S["ml_cols_ps"], l + 1)
                act.wait_ge(S["ml_a"], l + 1)
                activation(ml_cols[:, 1, :, :], PS[:, 0, 8:16].rearrange("p (t h) -> p t h", t=NT), ACT.Exp,
                             scale=-1.0).then_inc(S["exp_minus_m"], 1)

                def sw_exp(h):
                    act.wait_ge(S["sw_scores"], l * SW_H + h + 1)
                    for t, (lo, hi) in ((1, (0, TOK)), (0, (TOK, 3 * P))):
                        last = activation(sw_s[:, h % 2, lo:hi], sw_s[:, h % 2, lo:hi], ACT.Exp,
                                            bias=sw_stat[:, 0, h, t:t + 1], accum_out=sw_stat[:, 1, h, t:t + 1])
                    last.then_inc(S["sw_p"], 1)

                def sw_copy(h):
                    act.wait_ge(S["sw_t"], l * SW_H + h + 1)
                    if h >= 2:
                        act.wait_ge(S["sw_av"], l * SW_H + h - 1)
                    activation(sw_pT[:, h % 2, :], PS[:, 2 + h % 2, 0:3 * P], ACT.Copy).then_inc(S["sw_pT"], 1)

                def g_half(i):
                    j, t = i // 2, i % 2
                    if t == 0:
                        act.wait_ge(S["g_first"], l * 4 + j + 1)
                    else:
                        act.wait_ge(S["slot_used"], before + used(zpos + 10 + 2 * j + 2))
                    activation((ga, gb)[j // 2][:, t, 512 * (j % 2):512 * (j % 2) + 512], PS[:, 4 + t, :],
                                 ACT.Tanh, scale=0.5).then_inc(S["g_copied"], 1)

                sw_exp(0)
                for h in range(SW_H):
                    if h + 1 < SW_H:
                        sw_exp(h + 1)
                    sw_copy(h)
                    g_half(h)
                act.wait_ge(S["sink_arg"], l + 1)
                activation(sw_stat[:, 2, :, :], sw_stat[:, 2, :, :], ACT.Exp).then_inc(S["sink_exp"], 1)
                for h in range(ML_H):
                    act.wait_ge(S["ml_arg"], l * ML_H + h + 1)
                    for st in range(NT):
                        last = activation(ml_w[:, h, st * TOK:(st + 1) * TOK], ml_w[:, h, st * TOK:(st + 1) * TOK],
                                            ACT.Exp, bias=ml_cols[:, 0, st, h:h + 1])
                    last.then_inc(S["ml_exp"], 1)
                act.wait_ge(S["tr_b"], l + 1)
                activation(hT[:, 4:8, :].rearrange("p k n -> p (k n)"), two_banks(2), ACT.Copy).then_inc(S["hT_b"], 1)
                act.wait_ge(S["tr_a"], l + 1)
                activation(hT[:, 0:4, :].rearrange("p k n -> p (k n)"), two_banks(0), ACT.Copy).then_inc(S["hT_a"], 1)
                for b in (0, 2):
                    act.wait_ge(S["turned"], 4 * turned_turn("mixed", l) + (b + 1))
                    activation(hT[:, 2 * b:2 * b + 2, :].rearrange("p k n -> p (k n)"), PS[:, 4 + b, :],
                                 ACT.Copy).then_inc(S["hT"], 1)
                for c in range(2):
                    gate_up_hi(POS_LAYER + OFF_FFN2, c, l * 2 * FFN_UNITS + FFN_UNITS, layer_fills)
                norm("ffn2", "x_mix", (2 * l + 1, 2 * l + 2), l)
                norm_T_hi("ffn2", l)
                ffn_tanh(POS_LAYER + OFF_FFN2, l * 2 * FFN_UNITS + FFN_UNITS, layer_fills)
                norm("ple", "x_ffn2", (2 * l + 1, 2 * l + 2), l)
                norm_T("ple", l)
                act.wait_ge(S["pT_ps"], l + 1)
                activation(pT, PS[:, 0, :].rearrange("p (j n) -> p j n", j=2), ACT.Copy).then_inc(S["pT"], 1)
                act.wait_ge(S["slot_used"], before + used(POS_LAYER + OFF_PLE + 4))
                for t in range(NT):
                    activation(ga[:, t, :], two_banks(2 * t), ACT.Tanh, scale=0.5).then_inc(S["ple_tanh"], 1)

        @block.vector
        def _(program):
            V = nc.vector
            dve = InOrder(V, program)
            tt = lambda *args, **kwargs: dve.run(V.tensor_tensor, *args, **kwargs)
            ts = lambda *args, **kwargs: dve.run(V.tensor_scalar, *args, **kwargs)
            stt = lambda *args, **kwargs: dve.run(V.scalar_tensor_tensor, *args, **kwargs)

            def wide_of(v, n):
                return v.unsqueeze(len(v.shape)).to_broadcast(list(v.shape) + [n])

            def heads(v, h):
                return v.rearrange("p t (h d) -> p t h d", h=h)

            dve.wait_ge(S["c_tanh"], 1)
            dve.wait_ge(S["c_full"], 16)
            stt(silu_c, c_tanh, 1.0, c_col, ALU.add, ALU.mult)
            ts(c_wide, wide_of(silu_c, 32), 0.5, None, ALU.mult).then_inc(S["c_wide"], 1)
            dve.wait_ge(S["decay_full"], 32)
            ts(lg_m, lgt, 0.0, None, ALU.min)
            stt(lg_a, lg_m, -2.0, lgt, ALU.mult, ALU.add).then_inc(S["lg_abs"], 1)
            def ada_row(chunk, bias):
                dve.wait_ge(S["slot_used"], used(pos_ada(KT * (chunk + 1) - 1) + 1))
                tt(ada_rows[chunk], PS[:, (7, 6, 7)[chunk], :], bias, ALU.add).then_inc(S["ada_row"], 1)

            dve.wait_ge(S["b_rows_full"], 64)
            ada_row(0, b_rows)
            dve.wait_ge(S["gains_full"], 64)
            dve.wait_ge(S["ada"], 1)
            stt(mod[:, 1, :], PS[:, 2:4, :].rearrange("p b n -> p (b n)"), 1.0, g_pre, ALU.add, ALU.mult)
            dve.wait_ge(S["ada_copied"], 1)
            dve.wait_ge(S["row_roots"], norm_turn("pre"))
            dve.wait_ge(S["x_full"], 16)
            for t in range(NT):
                stt(hn[:, t, :], x[:, t, :], ms[:, t:t + 1], mod[:, 1, :], ALU.mult, ALU.mult)
            for t in range(NT):
                last = tt(hn[:, t, :], hn[:, t, :], mod[:, 0, :], ALU.add)
            last.then_inc(S["hn"], NT)

            def plain_hT(name, base):
                for b in (1, 3):
                    dve.wait_ge(S["turned"], 4 * turned_turn(name) + b + 1)
                    dve.run(V.tensor_copy, hT[:, 2 * b:2 * b + 2, :].rearrange("p k n -> p (k n)"),
                                  PS[:, base + b, :]).then_inc(S["hT"], 1)

            plain_hT("pre", 0)
            dve.wait_ge(S["lg_ln"], 1)
            tt(lg, lg_m, lg_a, ALU.subtract)
            dve.wait_ge(S["const_full"], 16)
            dve.wait_ge(S["rel_pos_full"], 16)
            dve.wait_ge(S["rel_neg_full"], 16)
            for h in range(RET_H):
                backward = hn[:, 0, 0:NT * TOK]
                ts(backward, rel[:, 1, :], lg[:, 4 + h:5 + h], None, ALU.mult)
                stt(decay[:, h, :], rel[:, 0, :], lg[:, h:h + 1], backward,
                    ALU.mult, ALU.add).then_inc(S["decay_arg"], 1)
            for j, dst in ((1, rv), (3, aqT), (5, av)):
                dve.wait_ge(S["slot_used"], used(pos_win(j) + 2))
                b = 2 * (j % 3)
                dve.run(V.tensor_copy, dst.rearrange("p a n -> p (a n)"),
                              PS[:, b:b + 2, :].rearrange("p b n -> p (b n)")).then_inc(S[f"piece{j}_copied"], 1)
            dve.wait_ge(S["b_late_full"], 64)
            for i in range(2):
                ada_row(1 + i, b_late[:, i, :])
            for h in range(RET_H):
                dve.wait_ge(S["ret_s"], h + 1)
                dve.wait_ge(S["decay"], h + 1)
                stt(scores[:, h, :], PS[:, h, :], RET_DK ** -0.5, decay[:, h, :], ALU.mult,
                    ALU.mult).then_inc(S["ret_w"], 1)
            dve.wait_ge(S["rg_tanh"], 1)
            dve.wait_ge(S["piece2_copied"], 1)
            stt(rg, rg_tanh, 1.0, rg, ALU.add, ALU.mult)
            dve.wait_ge(S["ret_y"], 1)
            ret_out = PS[:, 0:2, :].rearrange("p t (h d) -> p t h d", h=RET_H)
            by_head = lambda v: v.rearrange("p (t h) -> p t h", t=NT)
            dve.run(V.reduce_sum, by_head(head_mean[:, :]), ret_out, AX.X)
            ts(head_mean[:, :], head_mean[:, :], -1.0 / RET_DV, None, ALU.mult)
            yc = heads(hn[:, :, 0:HALF], RET_H)
            tt(yc, ret_out, wide_of(by_head(head_mean[:, :]), RET_DV), ALU.add).then_inc(S["gn_read"], 1)
            stt(heads(hn[:, :, HALF:D], RET_H), yc, 1.0 / RET_DV, yc, ALU.mult, ALU.mult)
            dve.run(V.reduce_sum, by_head(head_ms[:, :]), heads(hn[:, :, HALF:D], RET_H), AX.X).then_inc(S["var_ret"], 1)
            dve.wait_ge(S["head_roots"], 1)
            tt(yc, yc, wide_of(by_head(head_ms[:, :]), RET_DV), ALU.mult)
            stt(hn[:, :, 0:HALF], hn[:, :, 0:HALF], 0.5, rg, ALU.mult, ALU.mult)

            dve.wait_ge(S["dist_full"], 16)
            dve.wait_ge(S["ln_count_full"], 16)
            for h in range(ATT_H):
                slope = 2.0 ** (-8.0 * (h + 1) / ATT_H)
                stt(att_bias.rearrange("p a b -> p (a b)"), dist, -slope, ln_count, ALU.mult, ALU.add)
                dve.wait_ge(S["att_s"], h + 1)
                if h >= 2:
                    dve.wait_ge(S["att_t"], h - 1)
                s_h = scores[:, h % 2, :].rearrange("p (t n) -> p t n", t=NT)
                stt(s_h, PS[:, 4 + h % 2, :].rearrange("p (t n) -> p t n", t=NT), DH ** -0.5, att_bias,
                    ALU.mult, ALU.add)
                dve.run(V.tensor_reduce, att_stat[:, 0, h, :], s_h, AX.X, ALU.max, negate=True).then_inc(S["att_scores"], 1)
            dve.wait_ge(S["att_p"], ATT_H)
            dve.run(V.reciprocal, att_stat[:, 2, :, :], att_stat[:, 1, :, :])
            dve.wait_ge(S["att_av"], ATT_H)
            tt(heads(hn[:, :, HALF:D], ATT_H), heads(PS[:, 2:4, :], ATT_H),
               wide_of(att_stat[:, 2, :, :].rearrange("p h t -> p t h"), DH), ALU.mult).then_inc(S["hn"], NT)
            plain_hT("y", 4)
            dve.wait_ge(S["ada_copied"], 1 + ATT_H)
            tt(mod[:, 2, :], mod[:, 2, :], g_post, ALU.mult)
            stt(mod[:, 4, :], mod[:, 4, :], 1.0, g_pre_f, ALU.add, ALU.mult)
            tt(mod[:, 5, :], mod[:, 5, :], g_post_f, ALU.mult)

            def add_normed(gate, signal, name):
                dve.wait_ge(S["row_roots"], norm_turn(name))
                for t in range(NT):
                    stt(hn[:, t, :], PS[:, 2 * t:2 * t + 2, :].rearrange("p b n -> p (b n)"), ms_post[:, t:t + 1],
                        gate, ALU.mult, ALU.mult)
                for t in range(NT):
                    last = tt(x[:, t, :], x[:, t, :], hn[:, t, :], ALU.add)
                last.then_inc(S[signal], 1)

            add_normed(mod[:, 2, :], "x_mid", "post")
            dve.wait_ge(S["row_roots"], norm_turn("moe"))
            for t in range(NT):
                stt(hn[:, t, :], x[:, t, :], ms[:, t:t + 1], mod[:, 4, :], ALU.mult, ALU.mult)
            for t in range(NT):
                last = tt(hn[:, t, :], hn[:, t, :], mod[:, 3, :], ALU.add)
            last.then_inc(S["hn"], NT)
            plain_hT("moe", 4)
            dve.wait_ge(S["logits"], 1)
            dve.run(V.tensor_reduce, rt_stat[:, 0, :], PS[:, 0, 0:NT * NE].rearrange("p (t e) -> p t e", t=NT), AX.X, ALU.max,
                            negate=True).then_inc(S["logits_max"], 1)
            dve.wait_ge(S["aff_exp"], 1)
            dve.run(V.reciprocal, rt_stat[:, 2, :], rt_stat[:, 1, :])
            tt(aff, aff, wide_of(rt_stat[:, 2, :], NE), ALU.mult).then_inc(S["aff"], 1)
            dve.wait_ge(S["affT_ps"], 1)
            dve.run(V.tensor_copy, affT[0:NE, :], PS[0:NE, 1, 0:TOK])
            for i in range(CAP // 8):
                dve.run(V.max, top8[0:NE, :], affT[0:NE, :])
                dve.run(V.match_replace, affT[0:NE, :], top8[0:NE, :], affT[0:NE, :], -1.0)
            ts(chosen[0:NE, :], affT[0:NE, :], -1.0, None, ALU.is_equal)
            dve.run(V.tensor_tensor_scan, count[0:NE, :], chosen[0:NE, :], zeros[0:NE, :], 0.0, ALU.add, ALU.add)
            tt(count[0:NE, :], count[0:NE, :], chosen[0:NE, :], ALU.mult)
            ts(affT[0:NE, :], count[0:NE, :], 1.0, None, ALU.subtract).then_inc(S["place_rows"], 1)
            dve.wait_ge(S["place_ps"], 1)
            dve.run(V.tensor_copy, place.rearrange("p t e -> p (t e)"), PS[:, 2, 0:NT * NE])
            for t in range(NT):
                tt(onehot[:, t, :, :], con("cap_iota").unsqueeze(1).to_broadcast([P, NE, CAP]),
                   wide_of(place[:, t, :], CAP), ALU.is_equal)
            for t in range(NT):
                last = tt(gated[:, t, :, :], onehot[:, t, :, :], wide_of(aff[:, t, :], CAP), ALU.mult)
            last.then_inc(S["onehot"], 1)
            for k in range(1, KT, 2):
                dve.wait_ge(S["gathered"], k + 1)
                dve.run(V.tensor_copy, xeT[:, k, :], PS[:, k, :]).then_inc(S["xeT"], 1)
            dve.wait_ge(S["xeT"], KT)

            for q in dve.loop(NQ):
                for r in range(GROUP):
                    e = q * GROUP + r
                    pos = POS_MOE + r * EXPERT_SLOTS
                    dve.wait_ge(S["xe_free"], e + 1)
                    dve.run(V.tensor_copy, xe, xeT[:, :, bass.ds(e * CAP, CAP)]).then_inc(S["xe"], 1)
                    dve.wait_ge(S["e_tanh"], e + 1)
                    stt(e_act, e_tanh, 1.0, PS[:, 2, :], ALU.add, ALU.mult)
                    dve.wait_ge(S["slot_used"], q * GROUP_SLOTS + used(pos + 2 * KT))
                    stt(e_hid, e_act, 0.5, PS[:, 3, :], ALU.mult, ALU.mult).then_inc(S["e_hid"], 1)
            add_normed(gate_f, "x_layer", "last")

            def norm(name, l):
                dve.wait_ge(S["row_roots"], norm_turn(name, l))
                ts(hn[:, 1, :], x[:, 1, :], ms[:, 1:2], None, ALU.mult).then_inc(S["hn"], 1)

            def norm_T(name, l):
                for b in (1, 3):
                    dve.wait_ge(S["turned"], 4 * turned_turn(name, l) + (b + 1))
                    tt(hT[:, 2 * b:2 * b + 2, :], PS[:, 4 + b, :].rearrange("p (k n) -> p k n", k=2),
                       wide_of(p_(name)[:, 2 * b:2 * b + 2], TOK), ALU.mult).then_inc(S["hT"], 1)

            def norm_T_rest(name, turn, l):
                for b in range(4):
                    dve.wait_ge(S["hT_hi"], 4 * turn + (b + 1))
                    for k in (2 * b, 2 * b + 1):
                        last = stt(hT_split[:, 1, k, :], PS[:, 4 + b, (k % 2) * TOK:(k % 2) * TOK + TOK],
                                   p_(name)[:, k:k + 1], hT_split[:, 0, k, :].bitcast(F32), ALU.mult, ALU.subtract)
                    last.then_inc(S["hT"], 1)

            def gate_up_rest(pos, c, base):
                for part in range(2):
                    n = gate_unit(c) + part
                    dve.wait_ge(S["unit_hi"], base + (n + 1))
                    tt(unit(1, n, KT), gate_up_weights(pos, c, part), unit(0, n, KT).bitcast(F32),
                       ALU.subtract).then_inc(S["unit_split"], 1)

            def down_rest(pos, c, base):
                n = down_unit(c)
                dve.wait_ge(S["unit_hi"], base + (n + 1))
                tt(unit(1, n), down_weights(pos, c), unit(0, n).bitcast(F32), ALU.subtract).then_inc(
                    S["unit_split"], 1)

            def ffn_hidden(pos, hidden, base):
                def sub(c, hidden, base):
                    dve.wait_ge(S["f_tanh"], hidden + (c + 1))
                    act_ = f_act[:, c % 2, :]
                    stt(act_, f_tanh[:, c % 2, :], 1.0, PS[:, 4 + c % 4, 0:TOK], ALU.add, ALU.mult)
                    tt(act_, act_, PS[:, 4 + c % 4, TOK:2 * TOK], ALU.mult)
                    dve.run(V.tensor_copy, hid_split[:, 0, c % 2, :], act_)
                    tt(hid_split[:, 1, c % 2, :], act_, hid_split[:, 0, c % 2, :].bitcast(F32),
                       ALU.subtract).then_inc(S["f_hid"], 1)
                    if c + 2 < FFN_SUBS:
                        gate_up_rest(pos, c + 2, base)
                    if c + 1 < FFN_SUBS:
                        down_rest(pos, c + 1, base)

                down_rest(pos, 0, base)
                for b in dve.loop(FFN_PAIRS):
                    for c in range(4):
                        sub(c, hidden + b * 4, base + b * 12)
                for c in range(4 * FFN_PAIRS, FFN_SUBS):
                    sub(c, hidden, base)

            def add_rows(scale, signal):
                for t in range(NT):
                    stt(x[:, t, :], PS[:, 2 * t:2 * t + 2, :].rearrange("p b n -> p (b n)"), scale, x[:, t, :],
                        ALU.mult, ALU.add).then_inc(S[signal], 1)

            for l in dve.loop(LAYERS):
                before = l * LAYER_SLOTS
                norm("ffn1", l)
                dve.wait_ge(S["par_full"], (l + 1) * 16 * 10)
                norm_T_rest("ffn1", 2 * l, l)
                for c in range(2):
                    gate_up_rest(POS_LAYER + OFF_FFN1, c, l * 2 * FFN_UNITS)
                ffn_hidden(POS_LAYER + OFF_FFN1, l * 2 * FFN_SUBS, l * 2 * FFN_UNITS)
                dve.wait_ge(S["unit_used"], l * 2 * FFN_UNITS + FFN_UNITS)
                add_rows(0.25, "x_ffn1")
                norm("mix", l)
                norm_T("mix", l)

                zpos = POS_LAYER + OFF_Z
                dve.run(V.memset, mva[:, :, :, ML_DV:ML_DV + 1], 1.0)
                dve.wait_ge(S["slot_used"], before + used(zpos + 4))
                G = lambda i: gates[0:ML_H, i, :]
                ts(G(1), PS[0:ML_H, 2, TOK:2 * TOK], p_("b_f")[0:ML_H, :], None, ALU.add).then_inc(S["gate_f"], 1)
                ts(G(2), G(1), 0.0, None, ALU.min)
                stt(G(3), G(2), -2.0, G(1), ALU.mult, ALU.add).then_inc(S["f_abs"], 1)
                dve.wait_ge(S["slot_used"], before + used(zpos + 6))
                dve.run(V.tensor_copy, sq[:, :, 384:512], PS[:, 4:6, 0:P])
                dve.run(V.tensor_copy, sk, PS[:, 4:6, P:2 * P])
                dve.run(V.tensor_copy, sv, PS[:, 4:6, 2 * P:3 * P]).then_inc(S["sk_copied"], 1)
                dve.wait_ge(S["f_ln"], l + 1)
                tt(G(5), G(2), G(4), ALU.subtract)
                dve.run(V.tensor_tensor_scan, G(6), G(5), zeros[0:ML_H, :], 0.0, ALU.add, ALU.add)
                dve.wait_ge(S["gate_i"], l + 1)
                tt(G(7), G(0), G(6), ALU.subtract)
                dve.run(V.tensor_tensor_scan, G(1), G(7), G(7), 0.0, ALU.max, ALU.max)
                tt(G(2), G(6), G(1), ALU.add).then_inc(S["scan"], 1)
                dve.wait_ge(S["sq_copied"], l + 1)
                by16 = lambda v: v.rearrange("p t (h d) -> p (t h) d", d=DH)
                tmp = hn[:, 0, :].rearrange("p (h d) -> p h d", d=DH)
                tmp_k = hn[:, 1, 0:TOK].rearrange("p (h d) -> p h d", d=DH)
                stt(tmp, by16(sq), 1.0 / DH, by16(sq), ALU.mult, ALU.mult)
                stt(tmp_k, by16(sk), 1.0 / DH, by16(sk), ALU.mult, ALU.mult)
                dve.run(V.reduce_sum, qk_ms[:, 0:16], tmp, AX.X)
                dve.run(V.reduce_sum, qk_ms[:, 16:20], tmp_k, AX.X).then_inc(S["ms_qk"], 1)
                dve.wait_ge(S["slot_used"], before + used(zpos + 8))
                dve.run(V.tensor_copy, mva[:, :, :, 0:ML_DV], heads(PS[:, 0:2, :], ML_H)).then_inc(S["mva"], 1)
                dve.wait_ge(S["qk_roots"], l + 1)
                tt(by16(sq), by16(sq), wide_of(qk_ms[:, 0:16], DH), ALU.mult)
                tt(by16(sk), by16(sk), wide_of(qk_ms[:, 16:20], DH), ALU.mult)
                kd_v = kd.rearrange("p t (g u d) -> p (t g) u d", g=SW_KV, u=2)
                for u in range(2):
                    tt(kd_v[:, :, u, :], by16(sk), p_("k_gain").unsqueeze(1).to_broadcast([P, 4, DH]), ALU.mult)
                tt(by16(sq), by16(sq), p_("q_gain").unsqueeze(1).to_broadcast([P, 16, DH]),
                   ALU.mult).then_inc(S["qk_normed"], 1)
                dve.wait_ge(S["tk"], l + 1)
                dve.run(V.tensor_copy, skT.rearrange("p g n -> p (g n)"), PS[:, 1, :]).then_inc(S["skT"], 1)
                dve.wait_ge(S["ml_cols_ps"], l + 1)
                dve.run(V.tensor_copy, ml_cols[:, 0, :, :], PS[:, 0, 0:8].rearrange("p (t h) -> p t h", t=NT)).then_inc(
                    S["ml_a"], 1)

                for h in range(SW_H):
                    dve.wait_ge(S["sw_sc"], l * SW_H + h + 1)
                    if h == 0:
                        dve.wait_ge(S["band_full"], 16)
                    else:
                        if h >= 2:
                            dve.wait_ge(S["sw_t"], l * SW_H + h - 1)
                    stt(sw_s[:, h % 2, 0:TOK], PS[:, h % 2, 0:TOK], DH ** -0.5, band[:, h, :], ALU.mult, ALU.add)
                    stt(sw_s[:, h % 2, TOK:3 * P], PS[:, h % 2, TOK:3 * P], DH ** -0.5, band[:, h, P:TOK],
                        ALU.mult, ALU.add)
                    dve.run(V.reduce_max, sw_stat[:, 0, h, 1:2], sw_s[:, h % 2, 0:TOK], AX.X)
                    dve.run(V.reduce_max, sw_stat[:, 0, h, 0:1], sw_s[:, h % 2, TOK:3 * P], AX.X)
                    ts(sw_stat[:, 0, h, :], sw_stat[:, 0, h, :], p_("sink")[:, h:h + 1], -1.0, ALU.max,
                       ALU.mult).then_inc(S["sw_scores"], 1)
                tt(sw_stat[:, 2, :, :], sw_stat[:, 0, :, :], wide_of(p_("sink"), NT), ALU.add).then_inc(
                    S["sink_arg"], 1)
                for h in range(ML_H):
                    if h % 2 == 0:
                        dve.wait_ge(S["neg_m"], l * 2 + h // 2 + 1)
                    m_h = PS[:, 4 + h // 2, (h % 2) * TOK:(h % 2) * TOK + TOK]
                    last = tt(ml_w[:, h, :].rearrange("p (s n) -> p s n", s=NT),
                              con("causal", NT), m_h.unsqueeze(1).to_broadcast([P, NT, TOK]), ALU.add)
                    last.then_inc(S["ml_arg"], 1)
                dve.wait_ge(S["sink_exp"], l + 1)
                tt(sw_stat[:, 3, :, :], sw_stat[:, 1, :, :], sw_stat[:, 2, :, :], ALU.add)
                dve.run(V.reciprocal, sw_stat[:, 3, :, :], sw_stat[:, 3, :, :])
                dve.wait_ge(S["sw_av"], (l + 1) * SW_H)
                tt(heads(hn[:, :, HALF:D], SW_H), heads(PS[:, 6:8, :], SW_H),
                   wide_of(sw_stat[:, 3, :, :].rearrange("p h t -> p t h"), DH), ALU.mult).then_inc(S["h_b"], 1)
                for h in range(ML_H):
                    dve.wait_ge(S["ml_exp"], l * ML_H + h + 1)
                    dve.wait_ge(S["ml_s"], l * ML_H + h + 1)
                    stt(ml_w[:, h, :], ml_w[:, h, :], 64 ** -0.5, PS[:, h, :], ALU.mult, ALU.mult).then_inc(
                        S["ml_w"], 1)
                dve.wait_ge(S["ml_av"], (l + 1) * ML_H)
                dve.wait_ge(S["exp_minus_m"], l + 1)
                den = ml_den.rearrange("p (t h) -> p t h", t=NT)
                num = lambda t, pair: PS[:, 6 + t - 2 * pair, 0:2 * (ML_DV + 1)].rearrange("p (h n) -> p h n", h=2)
                parts = [(t, pair) for t in range(NT) for pair in range(2)]
                den_of = lambda t, pair: den[:, t, 2 * pair:2 * pair + 2].unsqueeze(2)
                for t, pair in parts:
                    ts(den_of(t, pair), num(t, pair)[:, :, ML_DV:ML_DV + 1], -1.0, None, ALU.mult)
                for t, pair in parts:
                    tt(den_of(t, pair), den_of(t, pair), num(t, pair)[:, :, ML_DV:ML_DV + 1], ALU.max)
                tt(den, den, ml_cols[:, 1, :, :], ALU.max)
                dve.run(V.reciprocal, ml_den, ml_den)
                h_a = heads(hn[:, :, 0:HALF], ML_H)
                for t, pair in parts:
                        tt(h_a[:, t, 2 * pair:2 * pair + 2, :], num(t, pair)[:, :, 0:ML_DV],
                           wide_of(den[:, t, 2 * pair:2 * pair + 2], ML_DV), ALU.mult)
                stt(heads(sq, ML_H), h_a, 1.0 / ML_DV, h_a, ALU.mult, ALU.mult)
                dve.run(V.reduce_sum, by_head(head_ms[:, :]), heads(sq, ML_H), AX.X).then_inc(S["ms_ha"], 1)
                dve.wait_ge(S["mo"], l + 1)
                for t in range(NT):
                    stt(mo[:, t, :], mo[:, t, :], 1.0, p_("ml_gain"), ALU.add, ALU.mult)
                dve.wait_ge(S["head_roots"], l + 2)
                tt(h_a, h_a, wide_of(by_head(head_ms[:, :]), ML_DV), ALU.mult)
                tt(hn[:, :, 0:HALF], hn[:, :, 0:HALF], mo, ALU.mult).then_inc(S["h_a"], 1)
                dve.wait_ge(S["g_copied"], 8 * (l + 1))
                dve.wait_ge(S["slot_used"], before + used(POS_LAYER + OFF_WA + 2))
                for t in range(NT):
                    last = stt(ga[:, t, :], ga[:, t, :], 1.0, PS[:, 4 + 2 * t:6 + 2 * t, :].rearrange("p b n -> p (b n)"),
                               ALU.add, ALU.mult)
                last.then_inc(S["ya_read"], 1)
                dve.wait_ge(S["slot_used"], before + used(POS_LAYER + OFF_WB + 2))
                for t in range(NT):
                    stt(gb[:, t, :], gb[:, t, :], 1.0, PS[:, 2 * t:2 * t + 2, :].rearrange("p b n -> p (b n)"),
                        ALU.add, ALU.mult)
                    stt(hn[:, t, :], ga[:, t, :], 0.5, gb[:, t, :], ALU.mult, ALU.add).then_inc(S["hn"], 1)
                for b in (1, 3):
                    dve.wait_ge(S["turned"], 4 * turned_turn("mixed", l) + (b + 1))
                    dve.run(V.tensor_copy, hT[:, 2 * b:2 * b + 2, :].rearrange("p k n -> p (k n)"),
                                  PS[:, 4 + b, :]).then_inc(S["hT"], 1)
                for c in range(2):
                    gate_up_rest(POS_LAYER + OFF_FFN2, c, l * 2 * FFN_UNITS + FFN_UNITS)
                dve.wait_ge(S["slot_used"], before + used(POS_LAYER + OFF_WO + 4))
                add_rows(0.5, "x_mix")
                norm("ffn2", l)
                norm_T_rest("ffn2", 2 * l + 1, l)
                ffn_hidden(POS_LAYER + OFF_FFN2, l * 2 * FFN_SUBS + FFN_SUBS, l * 2 * FFN_UNITS + FFN_UNITS)
                dve.wait_ge(S["unit_used"], (l + 1) * 2 * FFN_UNITS)
                add_rows(0.25, "x_ffn2")
                norm("ple", l)
                norm_T("ple", l)
                dve.wait_ge(S["ple_tanh"], NT * (l + 1))
                dve.wait_ge(S["ple_up"], l + 1)
                for t in range(NT):
                    stt(ga[:, t, :], ga[:, t, :], 1.0, PS[:, 4 + 2 * t:6 + 2 * t, :].rearrange("p b n -> p (b n)"),
                        ALU.add, ALU.mult)
                for t in range(NT):
                    last = stt(x[:, t, :], ga[:, t, :], 0.5, x[:, t, :], ALU.mult, ALU.add)
                last.then_inc(S["x_layer"], 1)

        @block.tensor
        def _(pe):
            mm = nc.tensor.matmul

            def full(pos, fills=0):
                pe.wait_ge(S[f"slot{pos % R}_full"], fills + 16 * (pos // R + 1))

            def transpose_rows(name, base, l=0, also=None):
                pe.wait_ge(S["hn"], NT * (turned_turn(name, l) + 1))
                for k in range(KT):
                    for t in range(NT):
                        last = nc.tensor.transpose(PS[:, base + k // 2, (k % 2) * TOK + t * P:(k % 2) * TOK + (t + 1) * P],
                                                   hn[:, t, k:D:KT], ident)
                        if also and k + t == 0:
                            last.then_inc(*also)
                    if k % 2 == 1:
                        last.then_inc(S["turned"], 1)

            def rows_product(pos, slots, per_slot, banks, fills, lhs, signal=True):
                n_k = slots * per_slot
                for s in range(slots):
                    full(pos + s, fills)
                    w = slot(pos + s, per_slot, D)
                    for i in range(per_slot):
                        k = s * per_slot + i
                        for t in range(NT):
                            for n in range(2):
                                last = mm(PS[:, banks + 2 * t + n, :], lhs(k, t), w[:, i, 512 * n:512 * n + 512],
                                          start=(k == 0), stop=(k == n_k - 1))
                    last.then_inc(S["slot_used"], 1)

            hT_tile = lambda k, t: hT[:, k, t * P:(t + 1) * P]

            pe.wait_ge(S["const_full"], 16)
            pe.wait_ge(S["relb_full"], 16)
            pe.wait_ge(S["bucket_full"], 16)
            for h in range(SW_H):
                last = mm(PS[:, h, 0:3 * P], relb[:, h:h + 1].to_broadcast([BUCKETS + 1, P]),
                          bucket[0:BUCKETS + 1, :], start=True, stop=True)
            last.then_inc(S["rep"], 1)
            pe.wait_ge(S["rep_copied"], 1)
            pe.wait_ge(S["c_wide"], 1)

            def ada_product(i):
                chunk, k = i // KT, i % KT
                full(pos_ada(i))
                for g in range(4):
                    last = mm(PS[32 * g:32 * g + 32, (7, 6, 7)[chunk], :], c_wide[:, k, :],
                              slot(pos_ada(i), SLOT)[:, 512 * g:512 * g + 512], start=(k == 0), stop=(k == KT - 1),
                              tile_position=(0, 32 * g))
                last.then_inc(S["slot_used"], 1)

            def ada_to_all(chunk, g, bank):
                return mm(PS[:, bank, :], ident[:, 32 * g:32 * g + 1].to_broadcast([P, P]), ada_rows[chunk],
                          start=True, stop=True)

            for i in range(KT):
                ada_product(i)
            pe.wait_ge(S["ada_row"], 1)
            for g in range(4):
                last = ada_to_all(0, g, g)
            last.then_inc(S["ada"], 1)
            transpose_rows("pre", 0)
            pe.wait_ge(S["hT"], 4 * (turned_turn("pre") + 1))
            for j in range(WIN_PIECES):
                pos = pos_win(j)
                full(pos)
                full(pos + 1)
                b = 2 * (j % 3)
                if j >= 3:
                    pe.wait_ge(S[f"piece{j - 3}_copied"], 1)
                w = [slot(pos + k // 4, 4, 512)[:, k % 4, :] for k in range(KT)]
                for part in range(4 if j in (0, 3, 4) else NT):
                    for k in range(KT):
                        if j in (0, 3, 4):
                            last = mm(PS[:, b + part // 2, (part % 2) * TOK:(part % 2) * TOK + TOK],
                                      w[k][:, part * P:(part + 1) * P], hT[:, k, :], start=(k == 0), stop=(k == 7))
                        else:
                            last = mm(PS[:, b + part, :], hT_tile(k, part), w[k], start=(k == 0), stop=(k == 7))
                last.then_inc(S["slot_used"], 2)
                for i in range(KT + 3 * j, min(KT + 3 * j + 3, ADA_SLOTS)):
                    ada_product(i)
            pe.wait_ge(S["piece0_copied"], 1)
            pe.wait_ge(S["piece3_copied"], 1)
            pe.wait_ge(S["piece4_copied"], 1)
            for h in range(RET_H):
                lo = 64 * (h % 2)
                for st in range(NT):
                    last = mm(PS[:, h, st * TOK:(st + 1) * TOK], qkT[lo:lo + 64, 2 + h // 2, st * P:(st + 1) * P],
                              qkT[lo:lo + 64, h // 2, :], start=True, stop=True)
                last.then_inc(S["ret_s"], 1)

            def att_s(h):
                lo = 64 * (h % 2)
                for t in range(NT):
                    last = mm(PS[:, 4 + h % 2, t * TOK:(t + 1) * TOK], aqT[lo:lo + 64, h // 2, t * P:(t + 1) * P],
                              akT[lo:lo + 64, h // 2, :], start=True, stop=True)
                last.then_inc(S["att_s"], 1)

            def att_av(h):
                pe.wait_ge(S["att_pT"], h + 1)
                for t in range(NT):
                    for st in range(NT):
                        last = mm(PS[:, 2 + t, h * DH:(h + 1) * DH],
                                  scores[:, 2 + h % 2, st * TOK + t * P:st * TOK + (t + 1) * P],
                                  av[:, st, h * DH:(h + 1) * DH], start=(st == 0), stop=(st == NT - 1))
                last.then_inc(S["att_av"], 1)

            pe.wait_ge(S["piece5_copied"], 1)
            att_s(0)
            att_s(1)
            pe.wait_ge(S["ret_w"], RET_H)
            for t in range(NT):
                for h in range(RET_H):
                    for st in range(NT):
                        last = mm(PS[:, t, h * P:(h + 1) * P], scores[:, h, st * TOK + t * P:st * TOK + (t + 1) * P],
                                  rv[:, st, h * P:(h + 1) * P], start=(st == 0), stop=(st == NT - 1))
            last.then_inc(S["ret_y"], 1)
            pe.wait_ge(S["gn_read"], 1)
            for h in range(ATT_H):
                pe.wait_ge(S["att_p"], h + 1)
                if h >= 2:
                    pe.wait_ge(S["att_pT"], h - 1)
                for st in range(NT):
                    for t in range(NT):
                        last = nc.tensor.transpose(PS[:, h % 2, st * TOK + t * P:st * TOK + (t + 1) * P],
                                                   scores[:, h % 2, t * TOK + st * P:t * TOK + (st + 1) * P], ident)
                last.then_inc(S["att_t"], 1)
                if h + 2 < ATT_H:
                    att_s(h + 2)
                if h >= 1:
                    att_av(h - 1)
                if h == 0:
                    pe.wait_ge(S["ada_row"], 3)
                if h >= 2:
                    pe.wait_ge(S["ada_copied"], h)
                ada_to_all(1 + h // 4, h % 4, 6 + h % 2).then_inc(S["ada"], 1)
            att_av(ATT_H - 1)
            pe.wait_ge(S["ada_copied"], 1 + ATT_H)
            transpose_rows("y", 4)
            pe.wait_ge(S["hT"], 4 * (turned_turn("y") + 1))
            rows_product(POS_WOUT, 4, 2, 0, 0, hT_tile)

            transpose_rows("moe", 4)
            pe.wait_ge(S["hT"], 4 * (turned_turn("moe") + 1))
            pe.wait_ge(S["router_full"], 16)
            for t in range(NT):
                for k in range(KT):
                    last = mm(PS[:, 0, t * NE:(t + 1) * NE], hT_tile(k, t), w_router[:, k, :], start=(k == 0),
                              stop=(k == KT - 1))
            last.then_inc(S["logits"], 1)
            pe.wait_ge(S["aff"], 1)
            for t in range(NT):
                last = nc.tensor.transpose(PS[0:NE, 1, t * P:(t + 1) * P], aff[:, t, :], ident)
            last.then_inc(S["affT_ps"], 1)
            pe.wait_ge(S["place_rows"], 1)
            for t in range(NT):
                last = nc.tensor.transpose(PS[:, 2, t * NE:(t + 1) * NE], affT[0:NE, t * P:(t + 1) * P],
                                           ident[0:NE, 0:NE])
            last.then_inc(S["place_ps"], 1)
            pe.wait_ge(S["onehot"], 1)
            for k in range(KT):
                for t in range(NT):
                    last = mm(PS[:, k, :], hn[:, t, k:D:KT], onehot[:, t, :, :].rearrange("p e c -> p (e c)"),
                              start=(t == 0), stop=(t == NT - 1))
                last.then_inc(S["gathered"], 1)
            pe.wait_ge(S["xeT"], KT)
            for q in range(NQ):
                for t in range(NT):
                    last = nc.tensor.transpose(
                        PS[:, q // 2, (q % 2) * TOK + t * P:(q % 2) * TOK + (t + 1) * P],
                        gated[:, t, GROUP * q:GROUP * q + GROUP, :].rearrange("p e c -> p (e c)"), ident)
            last.then_inc(S["GT_ps"], 1)

            with pe.Fori(0, NQ) as q:
                fills = q * (GROUP_SLOTS // R * 16)
                for r in range(GROUP):
                    e = q * GROUP + r
                    pos = POS_MOE + r * EXPERT_SLOTS
                    pe.wait_ge(S["xe"], e + 1)
                    for part in range(2):
                        for k in range(KT):
                            at = pos + part * KT + k
                            full(at, fills)
                            for g in range(4):
                                last = mm(PS[32 * g:32 * g + 32, 2 + part, :], xe[:, k, :],
                                          slot(at, SLOT)[:, 512 * g:512 * g + 512],
                                          start=(k == 0), stop=(k == KT - 1), tile_position=(0, 32 * g))
                            last.then_inc(S["slot_used"], 1)
                    pe.wait_ge(S["e_hid"], e + 1)
                    for s in range(4):
                        last = nc.tensor.transpose(PS[:, 4, s * P:(s + 1) * P], e_hid[:, s:512:4], ident)
                        if s == 0:
                            last.then_inc(S["xe_free"], 1)
                    last.then_inc(S["e_tr"], 1)
                    pe.wait_ge(S["e_hT"], e + 1)
                    pe.wait_ge(S["y_copied"], e + 1)
                    for j in range(4):
                        for s in range(4):
                            at = pos + 2 * KT + 2 * j + s // 2
                            if s % 2 == 0:
                                full(at, fills)
                            for g in range(4):
                                last = mm(PS[32 * g:32 * g + 32, 5, 0:256], e_hT[:, s, 32 * j:32 * j + 32],
                                          slot(at, 2, D)[:, s % 2, 256 * g:256 * g + 256],
                                          start=(j == 0 and s == 0), stop=(j == 3 and s == 3),
                                          tile_position=(0, 32 * g))
                            if s % 2 == 1:
                                last.then_inc(S["slot_used"], 1)
            pe.wait_ge(S["GT"], 1)
            pe.wait_ge(S["y_copied"], NE + 1)
            for t in range(NT):
                for n in range(2):
                    for q in range(NQ):
                        last = mm(PS[:, 2 * t + n, :], GT[:, q, t * P:(t + 1) * P], Y[:, q, 512 * n:512 * n + 512],
                                  start=(q == 0), stop=(q == NQ - 1))
            last.then_inc(S["combined"], 1)

            with pe.Fori(0, LAYERS) as l:
                layer_fills = l * (LAYER_SLOTS // R * 16)

                def ffn(pos, hidden, base):
                    for b in range(4):
                        mm(PS[:, b, 0:2], zeros[0:1, 0:P], zeros[0:1, 0:2], start=True, stop=False,
                           skip_group_check=True)

                    def split_mm(out, lhs, rhs, start, stop, **flags):
                        passes = [mm(out, lhs[i], rhs[j], start=start and i + j == 0, stop=stop and i == 1, **flags)
                                  for i, j in ((0, 0), (0, 1), (1, 0))]
                        return passes[0], passes[-1]

                    def up(c, base):
                        for part in range(2):
                            n = gate_unit(c) + part
                            pe.wait_ge(S["unit_split"], base + (n + 1))
                            for k in range(KT):
                                first, last = split_mm(PS[:, 4 + c % 4, part * TOK:(part + 1) * TOK],
                                                       [unit(i, n, KT)[:, k, :] for i in range(2)],
                                                       [hT_split[:, i, k, :] for i in range(2)],
                                                       start=(k == 0), stop=(k == KT - 1))
                                if k == 0 and c % 2 == 1:
                                    first.then_inc(S["slot_used"], 1)
                            last.then_inc(S["unit_used"], 1)

                    def down(c, hidden, base):
                        n = down_unit(c)
                        pe.wait_ge(S["f_hid"], hidden + (c + 1))
                        pe.wait_ge(S["unit_split"], base + (n + 1))
                        for t in range(NT):
                            for half in range(2):
                                first, last = split_mm(
                                    PS[:, 2 * t + half, :],
                                    [hid_split[:, i, c % 2, t * P:(t + 1) * P] for i in range(2)],
                                    [unit(i, n)[:, 512 * half:512 * half + 512] for i in range(2)],
                                    start=False, stop=False, skip_group_check=True)
                                if t + half == 0 and c % 2 == 1:
                                    first.then_inc(S["slot_used"], 1)
                        last.then_inc(S["unit_used"], 1)

                    up(0, base)
                    with pe.Fori(0, FFN_PAIRS) as b:
                        for c in range(4):
                            up(c + 1, base + b * 12)
                            down(c, hidden + b * 4, base + b * 12)
                    for c in range(4 * FFN_PAIRS, FFN_SUBS):
                        if c + 1 < FFN_SUBS:
                            up(c + 1, base)
                        down(c, hidden, base)

                transpose_rows("ffn1", 4, l)
                pe.wait_ge(S["hT"], 4 * (turned_turn("ffn1", l) + 1))
                ffn(POS_LAYER + OFF_FFN1, l * 2 * FFN_SUBS, l * 2 * FFN_UNITS)
                transpose_rows("mix", 4, l)
                pe.wait_ge(S["hT"], 4 * (turned_turn("mix", l) + 1))

                zpos = POS_LAYER + OFF_Z

                def z_weights(j):
                    full(zpos + 2 * j, layer_fills)
                    full(zpos + 2 * j + 1, layer_fills)
                    width = Z_PIECES[j][1]
                    return [slot(zpos + 2 * j + k // 4, 4, width)[:, k % 4, :] for k in range(KT)]

                def z_rows(j, t, bank, w, lo, hi):
                    for k in range(KT):
                        last = mm(PS[:, bank, 0:hi - lo], hT_tile(k, t), w[k][:, lo:hi], start=(k == 0),
                                  stop=(k == KT - 1))
                    return last

                w = z_weights(0)
                for part in range(4):
                    for k in range(KT):
                        last = mm(PS[:, 6 + part // 2, (part % 2) * TOK:(part % 2) * TOK + TOK],
                                  w[k][:, part * P:(part + 1) * P], hT[:, k, :], start=(k == 0), stop=(k == KT - 1))
                last.then_inc(S["slot_used"], 2)
                w = z_weights(1)
                for g in range(2):
                    for k in range(KT):
                        mm(PS[0:ML_H, 2, g * TOK:(g + 1) * TOK], w[k][:, ML_H * g:ML_H * g + ML_H], hT[:, k, :],
                           start=(k == 0), stop=(k == KT - 1))
                for t in range(NT):
                    last = z_rows(1, t, t, w, 2 * ML_H, 2 * ML_H + 384)
                last.then_inc(S["slot_used"], 2)
                w = z_weights(2)
                for t in range(NT):
                    last = z_rows(2, t, 4 + t, w, 0, 384)
                last.then_inc(S["slot_used"], 2)
                w = z_weights(3)
                pe.wait_ge(S["sq_copied"], l + 1)
                for t in range(NT):
                    last = z_rows(3, t, t, w, 0, 512)
                last.then_inc(S["slot_used"], 2)
                w = z_weights(4)
                pe.wait_ge(S["gate_i"], l + 1)
                pe.wait_ge(S["gate_f"], l + 1)
                for t in range(NT):
                    last = z_rows(4, t, 2 + t, w, 0, 512)
                last.then_inc(S["slot_used"], 2)
                pe.wait_ge(S["mqkT"], l + 1)
                pe.wait_ge(S["qk_normed"], l + 1)
                for j in range(4):
                    for t in range(NT):
                        last = nc.tensor.transpose(PS[:, 6 + j // 2, (j % 2) * TOK + t * P:(j % 2) * TOK + (t + 1) * P],
                                                   sq[:, t, j * P:(j + 1) * P], ident)
                last.then_inc(S["tq"], 1)
                pe.wait_ge(S["scan"], l + 1)
                pe.wait_ge(S["mva"], l + 1)
                for g in range(SW_KV):
                    for t in range(NT):
                        last = nc.tensor.transpose(PS[:, 1, g * TOK + t * P:g * TOK + (t + 1) * P],
                                                   kd[:, t, g * P:(g + 1) * P], ident)
                last.then_inc(S["tk"], 1)
                for which, at in ((7, 0), (2, 8)):
                    for t in range(NT):
                        last = nc.tensor.transpose(PS[:, 0, at + ML_H * t:at + ML_H * t + ML_H],
                                                   gates[0:ML_H, which, t * P:(t + 1) * P], ident[0:ML_H, 0:ML_H])
                last.then_inc(S["ml_cols_ps"], 1)
                pe.wait_ge(S["sqT"], l + 1)
                pe.wait_ge(S["skT"], l + 1)
                pe.wait_ge(S["ml_a"], l + 1)
                pe.wait_ge(S["exp_minus_m"], l + 1)

                def sw_s_(h):
                    lo, g = 64 * (h % 2), h // (SW_H // SW_KV)
                    q_h, k_h = sqT[lo:lo + 64, h // 2, :], skT[lo:lo + 64, g, :]
                    mm(PS[:, h % 2, 0:TOK], q_h[:, P:TOK], k_h, start=True, stop=True)
                    mm(PS[:, h % 2, TOK:3 * P], q_h[:, 0:P], k_h[:, 0:P], start=True, stop=True).then_inc(
                        S["sw_sc"], 1)

                def sw_av(h):
                    g = h // (SW_H // SW_KV)
                    v = lambda st: sv[:, st, g * DH:(g + 1) * DH]
                    pe.wait_ge(S["sw_pT"], l * SW_H + h + 1)
                    mm(PS[:, 6, h * DH:(h + 1) * DH], sw_pT[:, h % 2, TOK:3 * P], v(0), start=True, stop=True)
                    mm(PS[:, 7, h * DH:(h + 1) * DH], sw_pT[:, h % 2, 0:P], v(0), start=True, stop=False)
                    mm(PS[:, 7, h * DH:(h + 1) * DH], sw_pT[:, h % 2, P:TOK], v(1), start=False, stop=True).then_inc(
                        S["sw_av"], 1)

                sw_s_(0)
                sw_s_(1)
                pe.wait_ge(S["mo"], l + 1)
                pe.wait_ge(S["sk_copied"], l + 1)
                for h in range(SW_H):
                    j, t = h // 2, h % 2
                    if t == 0:
                        w = z_weights(5 + j)
                    if h >= 2:
                        pe.wait_ge(S["g_copied"], l * 8 + h - 1)
                    last = z_rows(5 + j, t, 4 + t, w, 0, 512)
                    if t == 0:
                        last.then_inc(S["g_first"], 1)
                    else:
                        last.then_inc(S["slot_used"], 2)
                    pe.wait_ge(S["sw_p"], l * SW_H + h + 1)
                    if h >= 2:
                        pe.wait_ge(S["sw_pT"], l * SW_H + h - 1)
                    for at in (0, P, TOK):
                        last = nc.tensor.transpose(PS[:, 2 + h % 2, at:at + P], sw_s[:, h % 2, at:at + P], ident)
                    last.then_inc(S["sw_t"], 1)
                    if h + 2 < SW_H:
                        sw_s_(h + 2)
                    if h >= 1:
                        sw_av(h - 1)
                sw_av(SW_H - 1)
                pe.wait_ge(S["g_copied"], 8 * (l + 1))
                for h in range(ML_H):
                    last = mm(PS[:, 4 + h // 2, (h % 2) * TOK:(h % 2) * TOK + TOK],
                              con("minus_row")[0:ML_H, h * P:(h + 1) * P], gates[0:ML_H, 1, :], start=True, stop=True)
                    if h % 2 == 1:
                        last.then_inc(S["neg_m"], 1)
                for h in range(ML_H):
                    lo = 64 * (h % 2)
                    for st in range(NT):
                        last = mm(PS[:, h, st * TOK:(st + 1) * TOK], mqkT[lo:lo + 64, 2 + h // 2, st * P:(st + 1) * P],
                                  mqkT[lo:lo + 64, h // 2, :], start=True, stop=True)
                    last.then_inc(S["ml_s"], 1)
                pe.wait_ge(S["h_b"], l + 1)
                for h in range(ML_H):
                    if h == 2:
                        pe.wait_ge(S["ml_arg"], ML_H * (l + 1))
                    pe.wait_ge(S["ml_w"], l * ML_H + h + 1)
                    for t in range(NT):
                        for st in range(t + 1):
                            last = mm(PS[:, 6 + t - 2 * (h // 2), (h % 2) * (ML_DV + 1):(h % 2 + 1) * (ML_DV + 1)],
                                      ml_w[:, h, st * TOK + t * P:st * TOK + (t + 1) * P],
                                      mva[:, st, h, :], start=(st == 0), stop=(st == t))
                    last.then_inc(S["ml_av"], 1)

                def branch_T(lo, bank, signal):
                    for k in range(4):
                        for t in range(NT):
                            last = nc.tensor.transpose(
                                PS[:, bank + k // 2, (k % 2) * TOK + t * P:(k % 2) * TOK + (t + 1) * P],
                                hn[:, t, lo + k:lo + HALF:4], ident)
                    last.then_inc(S[signal], 1)

                branch_T(HALF, 2, "tr_b")
                pe.wait_ge(S["h_a"], l + 1)
                branch_T(0, 0, "tr_a")
                pe.wait_ge(S["hT_a"], l + 1)
                rows_product(POS_LAYER + OFF_WA, 2, 2, 4, layer_fills, hT_tile)
                pe.wait_ge(S["hT_b"], l + 1)
                rows_product(POS_LAYER + OFF_WB, 2, 2, 0, layer_fills, lambda k, t: hT_tile(4 + k, t))
                pe.wait_ge(S["ya_read"], l + 1)
                transpose_rows("mixed", 4, l)
                pe.wait_ge(S["hT"], 4 * (turned_turn("mixed", l) + 1))
                rows_product(POS_LAYER + OFF_WO, 4, 2, 0, layer_fills, hT_tile)
                transpose_rows("ffn2", 4, l)
                pe.wait_ge(S["hT"], 4 * (turned_turn("ffn2", l) + 1))
                ffn(POS_LAYER + OFF_FFN2, l * 2 * FFN_SUBS + FFN_SUBS, l * 2 * FFN_UNITS + FFN_UNITS)
                transpose_rows("ple", 4, l)
                pe.wait_ge(S["ple_full"], 32 * (l + 1))
                for j in range(2):
                    for t in range(NT):
                        last = nc.tensor.transpose(PS[:, 0, j * TOK + t * P:j * TOK + (t + 1) * P],
                                                   p_rows[:, t, j * P:(j + 1) * P], ident)
                last.then_inc(S["pT_ps"], 1)
                pe.wait_ge(S["hT"], 4 * (turned_turn("ple", l) + 1))
                pe.wait_ge(S["pT"], l + 1)
                for j in range(2):
                    for t in range(NT):
                        for n in range(2):
                            last = mm(PS[:, 4 + 2 * t + n, :], pT[:, j, t * P:(t + 1) * P],
                                      w_ple[:, j, 512 * n:512 * n + 512], start=(j == 0), stop=(j == 1))
                last.then_inc(S["ple_up"], 1)
                rows_product(POS_LAYER + OFF_PLE, 4, 2, 0, layer_fills, hT_tile)


_INS = [
    "x", "c", "w_ada", "b_ada", "g_pre_mix", "g_post_mix", "g_pre_ffn", "g_post_ffn", "w_in", "ret_decay_fwd",
    "ret_decay_bwd", "w_out", "w_router", "w_gate_e", "w_up_e", "w_down_e", "p_2", "ffn1_norm_2", "ffn1_wi_2",
    "ffn1_wo_2", "mix_norm_2", "w_in_2", "b_igate_2", "b_fgate_2", "ml_out_norm_2", "q_norm_2", "k_norm_2",
    "sinks_2", "rel_bias_2", "w_a_2", "w_b_2", "w_out_2", "ffn2_norm_2", "ffn2_wi_2", "ffn2_wo_2", "ple_norm_2",
    "w_ple_gate_2", "w_ple_2"]


def shape_constants():
    c = {name: np.zeros((P, n), np.float32) for name, n in CONST_PARTS}
    c["ident"][:] = np.eye(P)
    tile = lambda f: np.concatenate([f(i * P + np.arange(P)[:, None], np.arange(TOK)[None, :]) for i in range(NT)], 1)
    c["rel_pos"][:] = tile(lambda s, t: np.maximum(t - s, 0))
    c["rel_neg"][:] = tile(lambda s, t: np.maximum(s - t, 0))
    c["dist"][:] = tile(lambda i, j: np.abs(i - j))
    c["causal"][:] = tile(lambda s, t: np.where(s <= t, 0.0, MASKED))

    def count(i, j):
        n = np.zeros(np.broadcast(i, j).shape)
        for window, d in ((128, 1), (512, 4), (2048, 16)):
            n += ((i - j) % d == 0) & (np.abs(i - j) // d <= window // (2 * d))
        return np.where(n > 0, np.log(np.maximum(n, 1)), MASKED)

    c["ln_count"][:] = tile(count)
    c["cap_iota"][:] = np.arange(CAP)
    for h in range(ML_H):
        c["minus_row"][h, h * P:(h + 1) * P] = -1.0
    dist = 2 * P - np.arange(3 * P)
    exact = BUCKETS // 2
    d = np.maximum(dist, 0)
    large = exact + (np.log(np.maximum(d, 1) / exact) / np.log(128 / exact) * (BUCKETS - exact)).astype(np.int32)
    bucket = np.where(d < exact, d, np.minimum(large, BUCKETS - 1))
    bucket = np.where((dist >= 0) & (dist < WINDOW), bucket, BUCKETS)
    c["bucket"][bucket, np.arange(3 * P)] = 1.0
    return np.ascontiguousarray(np.concatenate([c[name] for name, _ in CONST_PARTS], 1))


def kernel(**inputs):
    import concourse.bacc as bacc
    from concourse.bass_utils import run_bass_kernel_spmd

    nc = bacc.Bacc("TRN2", target_bir_lowering=False, num_devices=1)
    arrays, args = {}, {}
    for name in _INS:
        v = np.ascontiguousarray(inputs[name])
        arrays[f"in_{name}"] = v
        args[name] = nc.dram_tensor(f"in_{name}", v.shape, mybir.dt.from_np(v.dtype), kind="ExternalInput").ap()
    arrays["shape_constants"] = shape_constants()
    const = nc.dram_tensor("shape_constants", (P, NCONST), F32, kind="ExternalInput").ap()
    skew = nc.dram_tensor("skew", (SW_H, P, 3 * P), F32, kind="Internal").ap()
    out = nc.dram_tensor("out", (1, TOK, D), F32, kind="ExternalOutput").ap()
    build(nc, args, const, skew, out)
    r = run_bass_kernel_spmd(nc, [arrays], core_ids=[0])
    return r.results[0]["out"]
```

```python
import numpy as np
import concourse.bass as bass
from concourse import mybir
from contextlib import ExitStack

F32 = mybir.dt.float32
ROUNDED = mybir.dt.float32r
ALU = mybir.AluOpType
ACT = mybir.ActivationFunctionType
AX = mybir.AxisListType

P = 128
D = 1024
TOK = 256
NT = TOK // P
KT = D // P
MASKED = -1e30

RET_H, RET_DK, RET_DV = 4, 64, 128
ATT_H, DH = 8, 64
NE, CAP, FE = 16, 32, 2048
GROUP = 4
NQ = NE // GROUP
DFF = 2816
ML_H, ML_DV = 4, 128
SW_H, SW_KV = 8, 2
LAYERS = 2
BUCKETS, WINDOW = 32, 128
HALF = D // 2

R = 6
SLOT = 2048
ADA_WIDTH = 4 * 512
ADA_SLOTS = 6 * D // ADA_WIDTH * KT
WIN_PIECES = 6
pos_win = lambda j: KT + 5 * j
pos_ada = lambda i: i if i < KT else pos_win((i - KT) // 3) + 2 + (i - KT) % 3
POS_WOUT = pos_ada(ADA_SLOTS - 1) + 1
POS_MOE = POS_WOUT + 4
EXPERT_SLOTS = 24
GROUP_SLOTS = GROUP * EXPERT_SLOTS
POS_LAYER = POS_MOE + NE * EXPERT_SLOTS
FFN_STEP = 256
FFN_STEPS = DFF // FFN_STEP
FFN_SUBS = 2 * FFN_STEPS
FFN_SLOTS = 3 * FFN_STEPS
FFN_PAIRS = FFN_STEPS // 2
FFN_UNITS = 3 * FFN_SUBS
UNIT = 1024
UNIT_BUFFERS = 4
Z_QK, Z_V, Z_O, Z_IF, Z_SK, Z_GA, Z_GB = 0, 512, 1024, 1536, 1928, 2312, 3336
Z_PIECES = [(Z_QK, 512), (Z_IF, Z_SK - Z_IF), (Z_SK, Z_GA - Z_SK), (Z_V, 512), (Z_O, 512),
            (Z_GA, 512), (Z_GA + 512, 512), (Z_GB, 512), (Z_GB + 512, 512)]
OFF_FFN1 = 0
OFF_Z = OFF_FFN1 + FFN_SLOTS
OFF_WA = OFF_Z + 2 * len(Z_PIECES)
OFF_WB = OFF_WA + 2
OFF_WO = OFF_WB + 2
OFF_FFN2 = OFF_WO + 4
OFF_PLE = OFF_FFN2 + FFN_SLOTS
LAYER_SLOTS = OFF_PLE + 4
LAYER_UNITS = 2 * LAYER_SLOTS
assert LAYER_UNITS % UNIT_BUFFERS == 0 and LAYER_SLOTS % R == 0 and GROUP_SLOTS % R == 0 and 2 * 3 == R and FFN_STEPS % 2 == 1

CONST_PARTS = [("ident", P), ("causal", NT * TOK), ("cap_iota", CAP), ("minus_row", ML_H * P),
               ("rel_pos", NT * TOK), ("rel_neg", NT * TOK), ("ln_count", NT * TOK),
               ("dist", NT * TOK), ("bucket", 3 * P)]
CONST_AT, _n = {}, 0
for _name, _width in CONST_PARTS:
    CONST_AT[_name] = (_n, _width)
    _n += _width
NCONST = _n
NKEPT = CONST_AT["rel_pos"][0]

ARENA = 14488
PAR_PARTS = [("ffn1", KT), ("mix", KT), ("ffn2", KT), ("ple", KT), ("b_i", 1), ("b_f", 1),
             ("ml_gain", ML_H * ML_DV), ("q_gain", DH), ("k_gain", DH), ("sink", SW_H)]
PAR_AT, _n = {}, 0
for _name, _width in PAR_PARTS:
    PAR_AT[_name] = (_n, _width)
    _n += _width
NPAR = _n
NORMS = ("ffn1", "mix", "ffn2", "ple")


def gate_unit(c):
    return 3 * c - 1 if c else 0


def down_unit(c):
    return 3 * c + 4 if c < FFN_SUBS - 1 else FFN_UNITS - 1


def split_turn(name, l):
    return turned_turn(name, l) - turned_turn("ffn1", 0)


def norm_turn(name, l=0):
    first = ("pre", "post", "moe", "last")
    if name in first:
        return first.index(name) + 1
    return l * len(NORMS) + (len(first) + NORMS.index(name) + 1)


def turned_turn(name, l=0):
    first, layer = ("pre", "y", "moe"), ("ffn1", "mix", "mixed", "ffn2", "ple")
    if name in first:
        return first.index(name)
    return l * len(layer) + (len(first) + layer.index(name))


class Signals:

    def __init__(self, nc, ctx):
        self.nc, self.ctx, self.by_name = nc, ctx, {}

    def __getitem__(self, name):
        if name not in self.by_name:
            self.by_name[name] = self.ctx.enter_context(self.nc.semaphore(name))
        return self.by_name[name]


class InOrder:

    def __init__(self, engine, program):
        self.engine, self.program, self.open = engine, program, False

    def settle(self):
        if self.open:
            self.engine.drain()
            self.open = False

    def wait_ge(self, signal, value):
        self.settle()
        self.program.wait_ge(signal, value)

    def run(self, instruction, *args, **kwargs):
        self.settle()
        self.open = True
        return instruction(*args, **kwargs)

    def loop(self, turns):
        self.settle()
        with self.program.Fori(0, turns) as i:
            yield i
            self.settle()


def build(nc, a, const, skew, out):
    ctx = ExitStack()
    with ctx:
        S = Signals(nc, ctx)

        def sb(name, shape):
            return ctx.enter_context(nc.sbuf_tensor(name, shape, F32))

        def sb_rounded(name, shape):
            return ctx.enter_context(nc.sbuf_tensor(name, shape, ROUNDED))

        ring = sb("ring", [P, R, SLOT])
        units = sb_rounded("units", [P, 2, UNIT_BUFFERS, UNIT])
        hT_split = sb_rounded("hT_split", [P, 2, KT, TOK])
        hid_split = sb_rounded("hid_split", [P, 2, 2, TOK])
        cst = sb("cst", [P, NKEPT])
        x = sb("x", [P, NT, D])
        hn = sb("hn", [P, NT, D])
        hT = sb("hT", [P, KT, TOK])
        zeros = sb("zeros", [P, TOK])
        halves = sb("halves", [P, 24])
        eps_rms = sb("eps_rms", [P, 24])
        eps_group = sb("eps_group", [P, 8])
        spare = sb("spare", [P, 4])
        ms = sb("ms", [P, NT])
        ms_post = sb("ms_post", [P, NT])
        head_ms = sb("head_ms", [P, 8])
        head_mean = sb("head_mean", [P, 8])
        cur = sb("cur", [P, NPAR])
        relb = sb("relb", [BUCKETS + 1, SW_H])
        wide = sb("wide", [P, 4, D])
        p_rows = sb("p_rows", [P, NT, TOK])
        arena = sb("arena", [P, ARENA])
        PS = ctx.enter_context(nc.psum_tensor("PS", [P, 8, 512], F32))

        class Region:

            def __init__(self, at):
                self.at = at

            def take(self, *dims):
                n = int(np.prod(dims))
                v = arena[:, self.at:self.at + n]
                self.at += n
                assert self.at <= ARENA, self.at
                if len(dims) == 2:
                    v = v.rearrange("p (a b) -> p a b", a=dims[0])
                elif len(dims) == 3:
                    v = v.rearrange("p (a b c) -> p a b c", a=dims[0], b=dims[1])
                return v

        def con(name, a_=None):
            at, n = CONST_AT[name]
            v = cst[:, at:at + n]
            return v.rearrange("p (a b) -> p a b", a=a_) if a_ else v

        def p_(name):
            at, n = PAR_AT[name]
            return cur[:, at:at + n]

        ident = con("ident")

        def slot(pos, *dims):
            n = int(np.prod(dims))
            v = ring[:, pos % R, 0:n]
            return v.rearrange("p (a b) -> p a b", a=dims[0]) if len(dims) == 2 else v

        first = Region(0)
        mod = first.take(6, D)
        moe_start = 5 * D
        g_pre, g_post, g_pre_f, g_post_f = (wide[:, i, :] for i in range(4))
        small = first.take(64)
        c_col, c_tanh, silu_c = small[:, 0:8], small[:, 8:16], small[:, 16:24]
        lgt, lg_m, lg_a, lg = small[:, 24:32], small[:, 32:40], small[:, 40:48], small[:, 48:56]
        bucket = Region(first.at).take(3 * P)
        ada = Region(2 * D)
        c_wide = ada.take(KT, 32)
        b_rows = ada.take(512)
        b_late = Region(3 * D).take(2, 512)
        ada_rows = [hn[:, 0, 0:512]] + [hT[:, 2 * i:2 * i + 2, :].rearrange("p k n -> p (k n)") for i in (1, 2)]
        qkT = first.take(4, TOK)
        rv = first.take(NT, HALF)
        rg = first.take(NT, HALF)
        aqT = first.take(4, TOK)
        akT = first.take(4, TOK)
        av = first.take(NT, HALF)
        scores = first.take(4, NT * TOK)
        att_bias = hT[:, 0:NT, :]
        att_stat = first.take(3, ATT_H, NT)
        decay = arena[:, 0:RET_H * NT * TOK].rearrange("p (h n) -> p h n", h=RET_H)

        rg_tanh = qkT.rearrange("p a n -> p (a n)").rearrange("p (t n) -> p t n", t=NT)

        rel = scores[:, 0:2, :]
        ln_count, dist = cur[:, 0:NT * TOK], p_rows.rearrange("p t n -> p (t n)")
        router = Region(0)
        w_router = router.take(KT, NE)
        GT = router.take(NQ, TOK)
        onehot = router.take(NT, NE * CAP).rearrange("p t (e c) -> p t e c", e=NE)
        gated = router.take(NT, NE * CAP).rearrange("p t (e c) -> p t e c", e=NE)
        xe = router.take(KT, CAP)
        aff = router.take(NT, NE)
        place = router.take(NT, NE)
        rt_stat = router.take(3, NT)
        top8 = router.take(8)
        affT = router.take(TOK)
        chosen = router.take(TOK)
        count = router.take(TOK)
        e_act = router.take(512)
        assert router.at <= 5 * D
        gate_f = mod[:, 5, :]
        e_tanh = onehot[:, 0, :, :].rearrange("p e c -> p (e c)")
        e_hid = onehot[:, 1, :, :].rearrange("p e c -> p (e c)")
        e_hT = gated[:, 0, :, :].rearrange("p e c -> p (e c)").rearrange("p (s n) -> p s n", s=4)
        moe = Region(6 * D)
        xeT = moe.take(KT, NE * CAP)
        Y = moe.take(NQ, D)

        ffn = Region(0)
        f_tanh = ffn.take(2, TOK)
        f_act = ffn.take(2, TOK)
        lay = Region(0)
        gates = lay.take(8, TOK)
        mqkT = lay.take(4, TOK)
        mva = lay.take(NT, ML_H, ML_DV + 1)
        mo = lay.take(NT, HALF)
        sq = lay.take(NT, HALF)
        sk = lay.take(NT, P)
        sv = lay.take(NT, P)
        sqT = hn[:, 0, :].rearrange("p (a n) -> p a n", a=4)
        skT = lay.take(2, TOK)
        ga = lay.take(NT, D)
        gb = lay.take(NT, D)
        sw_s = hn[:, 1, 0:6 * P].rearrange("p (a n) -> p a n", a=2)
        sw_pT = lay.take(2, 3 * P)
        kd = sw_pT.rearrange("p a n -> p (a n)")[:, 0:NT * 2 * P].rearrange("p (t n) -> p t n", t=NT)
        ml_w = lay.take(ML_H, NT * TOK)
        qk_ms = lay.take(20)
        ml_cols = lay.take(2, NT, ML_H)
        ml_den = lay.take(8)
        sw_stat = lay.take(4, SW_H, NT)
        band = wide[:, 0:2, :].rearrange("p a (h n) -> p (a h) n", h=4)
        w_ple = wide[:, 2:4, :]
        pT = sq[:, 0, :].rearrange("p (j n) -> p j n", j=2)

        def stage_units(off, slots, first=0, last=None):
            return range(2 * off + first, 2 * (off + slots) if last is None else 2 * off + last)

        def gate_up_weights(pos, c, part):
            return slot(pos + 3 * (c // 2) + part, KT, FFN_STEP)[:, :, (c % 2) * P:(c % 2 + 1) * P]

        def down_weights(pos, c):
            return slot(pos + 3 * (c // 2) + 2, 2, D)[:, c % 2, :]

        def unit(part, u, *dims):
            n = int(np.prod(dims)) if dims else UNIT
            v = units[:, part, u % UNIT_BUFFERS, 0:n]
            return v.rearrange("p (k n) -> p k n", k=dims[0]) if len(dims) == 2 else v

        def half_slot(u, width):
            n = 2 * width if width < D else D
            return slot(POS_LAYER + u // 2, 2 * n)[:, (u % 2) * n:(u % 2 + 1) * n], n

        block = ctx.enter_context(nc.Block())
        FILLS = LAYER_SLOTS // R

        @block.sync
        def _(sp):
            def fill(pos, src, before=0):
                if pos >= R:
                    sp.wait_ge(S["slot_used"], before + (pos - R + 1))
                n = 1
                for s in src.shape[1:]:
                    n *= s
                dst = slot(pos, *src.shape[1:])
                sp.dma_start(dst, src).then_inc(S[f"slot{pos % R}_full"], 16)

            w_ada = a["w_ada"][0].rearrange("(p k) n -> p k n", k=KT)
            w_in = a["w_in"][0].rearrange("(p k) n -> p k n", k=KT)
            w_out = a["w_out"][0].rearrange("(p k) n -> p k n", k=KT)

            def columns(pos, w, col, width):
                for half in range(2):
                    fill(pos + half, w[:, 4 * half:4 * half + 4, col:col + width])

            def ada_fill(i):
                fill(pos_ada(i), w_ada[:, i % KT, ADA_WIDTH * (i // KT):ADA_WIDTH * (i // KT + 1)])

            for i in range(KT):
                ada_fill(i)
            for j in range(WIN_PIECES):
                columns(pos_win(j), w_in, 512 * j, 512)
                for i in range(KT + 3 * j, min(KT + 3 * j + 3, ADA_SLOTS)):
                    ada_fill(i)
            for i in range(4):
                fill(POS_WOUT + i, w_out[:, 2 * i:2 * i + 2, :])

            with sp.Fori(0, NQ) as q:
                for r in range(GROUP):
                    pos = POS_MOE + r * EXPERT_SLOTS
                    for w, at in (("w_gate_e", 0), ("w_up_e", KT)):
                        rows = a[w][0, q * GROUP + r].rearrange("(p k) n -> p k n", k=KT)
                        for k in range(KT):
                            fill(pos + at + k, rows[:, k, :], q * GROUP_SLOTS)
                    rows = a["w_down_e"][0, q * GROUP + r].rearrange("(j p s) n -> p j s n", j=4, s=4)
                    for j in range(4):
                        for s in range(2):
                            fill(pos + 2 * KT + 2 * j + s, rows[:, j, 2 * s:2 * s + 2, :], q * GROUP_SLOTS)

            with sp.Fori(0, LAYERS) as l:
                def ffn(pos, wi, wo):
                    wi_l = a[wi][l].rearrange("(p k) n -> p k n", k=KT)

                    def step(i, at, before):
                        for part in range(2):
                            fill(at + part, wi_l[:, :, bass.ds(i * FFN_STEP + part * DFF, FFN_STEP)], before)
                        fill(at + 2, a[wo][l, bass.ds(i * FFN_STEP, FFN_STEP), :].rearrange(
                            "(u p) n -> p u n", u=2), before)

                    with sp.Fori(0, FFN_PAIRS) as b:
                        for i in range(2):
                            step(b * 2 + i, pos + 3 * i, l * LAYER_SLOTS + b * R)
                    step(FFN_STEPS - 1, pos + 3 * (FFN_STEPS - 1), l * LAYER_SLOTS)

                def rows_of(w, pos, k):
                    w_l = a[w][l].rearrange("(p k) n -> p k n", k=k)
                    for i in range(k // 2):
                        fill(pos + i, w_l[:, 2 * i:2 * i + 2, :], l * LAYER_SLOTS)

                ffn(POS_LAYER + OFF_FFN1, "ffn1_wi_2", "ffn1_wo_2")
                z = a["w_in_2"][l].rearrange("(p k) n -> p k n", k=KT)
                for j, (col, width) in enumerate(Z_PIECES):
                    for half in range(2):
                        fill(POS_LAYER + OFF_Z + 2 * j + half, z[:, 4 * half:4 * half + 4, col:col + width],
                             l * LAYER_SLOTS)
                rows_of("w_a_2", POS_LAYER + OFF_WA, 4)
                rows_of("w_b_2", POS_LAYER + OFF_WB, 4)
                rows_of("w_out_2", POS_LAYER + OFF_WO, KT)
                ffn(POS_LAYER + OFF_FFN2, "ffn2_wi_2", "ffn2_wo_2")
                rows_of("w_ple_gate_2", POS_LAYER + OFF_PLE, KT)

            sp.wait_ge(S["x_layer"], NT * (LAYERS + 1))
            sp.dma_start(out[0].rearrange("(t p) d -> p t d", p=P), x[:, :, :]).then_inc(S["stored"], 16)
            sp.wait_ge(S["stored"], 16)

        @block.gpsimd
        def _(pool):
            nc.gpsimd.memset(zeros[:, :], 0.0).then_inc(S["zeros"], 1)
            nc.gpsimd.memset(halves[:, :], -0.5).then_inc(S["halves"], 1)
            nc.gpsimd.memset(eps_rms[:, :], 1e-6).then_inc(S["halves"], 1)
            nc.gpsimd.memset(eps_group[:, :], 1e-5).then_inc(S["halves"], 1)
            nc.gpsimd.memset(relb[:, :], MASKED).then_inc(S["relb_masked"], 1)
            nc.gpsimd.memset(spare[:, 0:1], 0.0).then_inc(S["xe_free"], 1)
            nc.gpsimd.memset(spare[:, 1:2], 0.0).then_inc(S["y_copied"], 1)

            def inverse_root(need, turn, src, eps, signal):
                pool.wait_ge(S[need], turn)
                n = src.shape[1]
                nc.gpsimd.tensor_tensor(src, src, eps[:, 0:n], ALU.add)
                nc.gpsimd.drain()
                nc.gpsimd.tensor_tensor(src, src, halves[:, 0:n], ALU.pow).then_inc(S[signal], 1)

            def row_root(name, l=0):
                into = ms_post if name in ("post", "last") else ms
                inverse_root("mean_squares", norm_turn(name, l), into[:, :], eps_rms, "row_roots")

            pool.wait_ge(S["halves"], 3)
            row_root("pre")
            inverse_root("var_ret", 1, head_ms[:, :], eps_group, "head_roots")
            row_root("post")
            row_root("moe")
            row_root("last")
            with pool.Fori(0, LAYERS) as l:
                row_root("ffn1", l)
                row_root("mix", l)
                inverse_root("ms_qk", l + 1, qk_ms, eps_rms, "qk_roots")
                inverse_root("ms_ha", l + 1, head_ms[:, :], eps_rms, "head_roots")
                row_root("ffn2", l)
                row_root("ple", l)

        used = lambda pos: pos

        @block.scalar
        def _(program):
            act = InOrder(nc.scalar, program)
            activation = lambda *args, **kwargs: act.run(nc.scalar.activation, *args, **kwargs)

            def row(src):
                return src.partition_broadcast(P)

            program.dma_start(c_col, a["c"][0].rearrange("(p k) -> p k", k=KT)).then_inc(S["c_full"], 16)
            program.dma_start(x[:, :, :], a["x"][0].rearrange("(t p) d -> p t d", p=P)).then_inc(S["x_full"], 16)
            program.dma_start(cst[:, :], const[:, 0:NKEPT]).then_inc(S["const_full"], 16)
            for g in range(4):
                program.dma_start(b_rows[32 * g:32 * g + 32], a["b_ada"][0, 512 * g:512 * (g + 1)].partition_broadcast(
                    32)).then_inc(S["b_rows_full"], 16)
            program.dma_start(g_pre, row(a["g_pre_mix"][0])).then_inc(S["g_pre_full"], 16)
            for i, name in enumerate(("ret_decay_fwd", "ret_decay_bwd")):
                program.dma_start(lgt[:, 4 * i:4 * i + 4], row(a[name][0])).then_inc(S["decay_full"], 16)

            def square_sums(rows, into, need, values, scale=1.0 / 32):
                for t in range(NT):
                    act.wait_ge(S[need], values[t])
                    last = activation(hn[:, t, :], rows(t), ACT.Square, scale=scale,
                                        accum_out=into[:, t:t + 1])
                last.then_inc(S["mean_squares"], 1)

            def two_banks(b):
                return PS[:, b:b + 2, :].rearrange("p b n -> p (b n)")

            act.wait_ge(S["c_full"], 16)
            activation(c_tanh, c_col, ACT.Tanh, scale=0.5).then_inc(S["c_tanh"], 1)
            square_sums(lambda t: x[:, t, :], ms, "x_full", (16, 16))
            act.wait_ge(S["ada"], 1)
            activation(mod[:, 0, :], two_banks(0), ACT.Copy).then_inc(S["ada_copied"], 1)
            act.wait_ge(S["relb_masked"], 1)
            program.dma_start(relb[0:BUCKETS, :], a["rel_bias_2"]).then_inc(S["relb_full"], 16)
            for name, dst in (("bucket", bucket), ("rel_pos", rel[:, 0, :]), ("rel_neg", rel[:, 1, :]),
                              ("dist", dist), ("ln_count", ln_count)):
                at, n = CONST_AT[name]
                program.dma_start(dst, const[:, at:at + n]).then_inc(S[name + "_full"], 16)
            for i, name in enumerate(("g_post_mix", "g_pre_ffn", "g_post_ffn")):
                program.dma_start(wide[:, i + 1, :], row(a[name][0])).then_inc(S["gains_full"], 16)

            def ada_copy(h):
                act.wait_ge(S["ada"], h + 2)
                activation(mod[:, 2 + h // 2, 512 * (h % 2):512 * (h % 2) + 512], PS[:, 6 + h % 2, :],
                           ACT.Copy).then_inc(S["ada_copied"], 1)

            def plain_hT(name, base):
                for b in (0, 2):
                    act.wait_ge(S["turned"], 4 * turned_turn(name) + b + 1)
                    activation(hT[:, 2 * b:2 * b + 2, :], PS[:, base + b, :], ACT.Copy).then_inc(S["hT"], 1)

            act.wait_ge(S["lg_abs"], 1)
            activation(lg_a, lg_a, ACT.Exp, scale=-1.0)
            activation(lg_a, lg_a, ACT.Ln, bias=1.0).then_inc(S["lg_ln"], 1)
            plain_hT("pre", 0)
            act.wait_ge(S["rep"], 1)
            rep = arena[:, 3 * D:6 * D].rearrange("p (h n) -> p h n", h=SW_H)
            activation(rep, PS[:, 0:8, 0:3 * P], ACT.Copy).then_inc(S["rep_copied"], 1)
            act.wait_ge(S["rep_copied"], 1)
            program.dma_start(skew.rearrange("h p n -> p h n"), rep).then_inc(S["skew_written"], 16)
            for h in range(RET_H):
                act.wait_ge(S["decay_arg"], h + 1)
                activation(decay[:, h, :], decay[:, h, :], ACT.Exp).then_inc(S["decay"], 1)
            for j, dst in ((0, qkT), (2, rg), (4, akT)):
                act.wait_ge(S["slot_used"], used(pos_win(j) + 2))
                activation(dst.rearrange("p a n -> p (a n)"), two_banks(2 * (j % 3)), ACT.Copy).then_inc(
                    S[f"piece{j}_copied"], 1)
                if j == 0:
                    act.wait_ge(S["skew_written"], 16)
                    for g in range(4):
                        program.dma_start(b_late[32 * g:32 * g + 32], a["b_ada"][0, ADA_WIDTH:3 * ADA_WIDTH].rearrange(
                            "(i g n) -> g i n", i=2, g=4)[g].partition_broadcast(32)).then_inc(S["b_late_full"], 16)
            act.wait_ge(S["ret_s"], RET_H)
            activation(rg_tanh, rg, ACT.Tanh, scale=0.5).then_inc(S["rg_tanh"], 1)

            def att_exp(h):
                act.wait_ge(S["att_scores"], h + 1)
                for t in range(NT):
                    last = activation(scores[:, h % 2, t * TOK:(t + 1) * TOK], scores[:, h % 2, t * TOK:(t + 1) * TOK],
                                        ACT.Exp, bias=att_stat[:, 0, h, t:t + 1],
                                        accum_out=att_stat[:, 1, h, t:t + 1])
                last.then_inc(S["att_p"], 1)

            def att_copy(h):
                act.wait_ge(S["att_t"], h + 1)
                if h >= 2:
                    act.wait_ge(S["att_av"], h - 1)
                activation(scores[:, 2 + h % 2, :], PS[:, h % 2, :], ACT.Copy).then_inc(S["att_pT"], 1)

            att_exp(0)
            for h in range(ATT_H):
                if h + 1 < ATT_H:
                    att_exp(h + 1)
                att_copy(h)
                ada_copy(h)
            plain_hT("y", 4)
            square_sums(lambda t: two_banks(2 * t), ms_post, "slot_used",
                        (used(POS_WOUT + 4),) * 2)
            act.wait_ge(S["x_mid"], 1)
            program.dma_start(w_router, a["w_router"][0].rearrange("(p k) e -> p k e", k=KT)).then_inc(
                S["router_full"], 16)
            square_sums(lambda t: x[:, t, :], ms, "x_mid", (1, 2))
            plain_hT("moe", 4)
            act.wait_ge(S["logits"], 1)
            act.wait_ge(S["logits_max"], 1)
            for t in range(NT):
                last = activation(aff[:, t, :], PS[:, 0, NE * t:NE * t + NE], ACT.Exp,
                                    bias=rt_stat[:, 0, t:t + 1], accum_out=rt_stat[:, 1, t:t + 1])
            last.then_inc(S["aff_exp"], 1)
            for k in range(0, KT, 2):
                act.wait_ge(S["gathered"], k + 1)
                activation(xeT[:, k, :], PS[:, k, :], ACT.Copy).then_inc(S["xeT"], 1)
            act.wait_ge(S["GT_ps"], 1)
            activation(GT.rearrange("p q n -> p (q n)"), two_banks(0), ACT.Copy).then_inc(S["GT"], 1)

            for q in act.loop(NQ):
                for r in range(GROUP):
                    pos = POS_MOE + r * EXPERT_SLOTS
                    before = q * GROUP_SLOTS
                    act.wait_ge(S["slot_used"], before + used(pos + KT))
                    activation(e_tanh, PS[:, 2, :], ACT.Tanh, scale=0.5).then_inc(S["e_tanh"], 1)
                    act.wait_ge(S["e_tr"], q * GROUP + r + 1)
                    activation(e_hT.rearrange("p s n -> p (s n)"), PS[:, 4, :], ACT.Copy).then_inc(S["e_hT"], 1)
                    act.wait_ge(S["slot_used"], before + used(pos + EXPERT_SLOTS))
                    for g in range(4):
                        last = activation(Y[32 * r:32 * r + 32, bass.ds(q, 1), 256 * g:256 * g + 256],
                                            PS[32 * g:32 * g + 32, 5, 0:256], ACT.Copy)
                    last.then_inc(S["y_copied"], 1)
            square_sums(lambda t: two_banks(2 * t), ms_post, "combined", (1, 1))

            act.wait_ge(S["x_layer"], NT)
            act.wait_ge(S["skew_written"], 16)
            program.dma_start(band, bass.AP(skew.tensor, P, [[3 * P - 1, P], [3 * P * P, SW_H], [1, TOK]])).then_inc(
                S["band_full"], 16)

            def split_hi(u, weights, slot_pos, first_use, base, fills):
                if u >= UNIT_BUFFERS:
                    act.wait_ge(S["unit_used"], base + (u - UNIT_BUFFERS + 1))
                if first_use:
                    act.wait_ge(S[f"slot{slot_pos % R}_full"], fills + 16 * (slot_pos // R + 1))
                activation(unit(0, u, *weights.shape[1:]), weights, ACT.Copy).then_inc(S["unit_hi"], 1)

            def halves_hi(us, width, base, fills):
                for u in us:
                    split_hi(u, half_slot(u, width)[0], POS_LAYER + u // 2, u % 2 == 0, base, fills)

            def gate_up_hi(off, c, base, fills):
                for part in range(2):
                    split_hi(2 * off + gate_unit(c) + part, gate_up_weights(POS_LAYER + off, c, part),
                             POS_LAYER + off + 3 * (c // 2) + part, c % 2 == 0, base, fills)

            def down_hi(off, c, base, fills):
                split_hi(2 * off + down_unit(c), down_weights(POS_LAYER + off, c),
                         POS_LAYER + off + 3 * (c // 2) + 2, c % 2 == 0, base, fills)

            def norm(name, need, values, l, also=lambda: None):
                square_sums(lambda t: x[:, t, :], ms, need, values)
                also()
                act.wait_ge(S["row_roots"], norm_turn(name, l))
                activation(hn[:, 0, :], x[:, 0, :], ACT.Copy, scale=ms[:, 0:1]).then_inc(S["hn"], 1)

            def norm_T_hi(name, l):
                for b in range(4):
                    act.wait_ge(S["turned"], 4 * turned_turn(name, l) + (b + 1))
                    for k in (2 * b, 2 * b + 1):
                        last = activation(hT_split[:, 0, k, :], PS[:, 4 + b, (k % 2) * TOK:(k % 2) * TOK + TOK],
                                          ACT.Copy, scale=1.0 if name == "mixed" else p_(name)[:, k:k + 1])
                    last.then_inc(S["hT_hi"], 1)

            def ffn_tanh(off, base, fills):
                def sub(c, base, fills):
                    act.wait_ge(S["unit_used"], base + (2 * off + gate_unit(c) + 2))
                    activation(f_tanh[:, c % 2, :], PS[:, 4 + c % 4, 0:TOK], ACT.Tanh,
                                 scale=0.5).then_inc(S["f_tanh"], 1)
                    if c + 2 < FFN_SUBS:
                        gate_up_hi(off, c + 2, base, fills)
                    if c + 1 < FFN_SUBS:
                        down_hi(off, c + 1, base, fills)

                down_hi(off, 0, base, fills)
                for b in act.loop(FFN_PAIRS):
                    for c in range(4):
                        sub(c, base + b * 12, fills + b * 16)
                for c in range(4 * FFN_PAIRS, FFN_SUBS):
                    sub(c, base, fills)

            for l in act.loop(LAYERS):
                before = l * LAYER_UNITS
                layer_fills = l * (LAYER_SLOTS // R * 16)
                norm("ffn1", "x_layer", (NT * l + 1, NT * l + 2), l, lambda: program.dma_start(
                    p_("ffn1"), a["ffn1_norm_2"][l].rearrange("(p k) -> p k", k=KT)).then_inc(S["gain_full"], 16))
                act.wait_ge(S["gain_full"], (l + 1) * 16)
                norm_T_hi("ffn1", l)
                for c in range(2):
                    gate_up_hi(OFF_FFN1, c, before, layer_fills)
                for name in NORMS[1:]:
                    program.dma_start(p_(name), a[{"mix": "mix_norm_2", "ple": "ple_norm_2"}.get(
                        name, name + "_norm_2")][l].rearrange("(p k) -> p k", k=KT)).then_inc(S["par_full"], 16)
                for name, src in (("b_i", "b_igate_2"), ("b_f", "b_fgate_2")):
                    program.dma_start(p_(name)[0:ML_H, :], a[src][l].rearrange("(h o) -> h o", o=1)).then_inc(
                        S["par_full"], 16)
                program.dma_start(p_("ml_gain"), row(a["ml_out_norm_2"][l].rearrange("h d -> (h d)"))).then_inc(
                    S["par_full"], 16)
                for name, src in (("q_gain", "q_norm_2"), ("k_gain", "k_norm_2"), ("sink", "sinks_2")):
                    program.dma_start(p_(name), row(a[src][l])).then_inc(S["par_full"], 16)
                program.dma_start(w_ple, a["w_ple_2"][l].rearrange("(j p) n -> p j n", p=P)).then_inc(S["ple_full"], 16)
                program.dma_start(p_rows[:, :, :], a["p_2"][l, 0].rearrange("(t p) n -> p t n", p=P)).then_inc(
                    S["ple_full"], 16)
                ffn_tanh(OFF_FFN1, before, layer_fills)
                act.wait_ge(S["par_full"], (l + 1) * 16 * 9)

                def piece_hi(j, first=0, last=4):
                    halves_hi(stage_units(OFF_Z + 2 * j, 2, first, last), Z_PIECES[j][1], before, layer_fills)

                def piece_done(j):
                    act.wait_ge(S["unit_used"], before + 2 * (OFF_Z + 2 * j + 2))

                piece_hi(0)
                norm("mix", "x_ffn1", (2 * l + 1, 2 * l + 2), l)
                norm_T_hi("mix", l)
                piece_hi(1)
                piece_done(0)
                activation(mqkT, PS[:, 0:4, 0:TOK], ACT.Copy).then_inc(S["mqkT"], 1)
                piece_hi(2)
                piece_done(1)
                activation(gates[0:ML_H, 0, :], PS[0:ML_H, 6, 0:TOK], ACT.Identity,
                             bias=p_("b_i")[0:ML_H, :]).then_inc(S["gate_i"], 1)
                activation(sq[:, :, 0:384], PS[:, 4:6, 0:384], ACT.Copy).then_inc(S["sq_copied"], 1)
                act.wait_ge(S["f_abs"], l + 1)
                activation(gates[0:ML_H, 4, :], gates[0:ML_H, 3, :], ACT.Exp, scale=-1.0)
                activation(gates[0:ML_H, 4, :], gates[0:ML_H, 4, :], ACT.Ln, bias=1.0).then_inc(S["f_ln"], 1)
                for j in (3, 4, 5):
                    piece_hi(j)
                piece_done(4)
                activation(mo.rearrange("p t n -> p (t n)"), two_banks(4), ACT.Tanh, scale=0.5).then_inc(
                    S["mo"], 1)
                act.wait_ge(S["tq"], l + 1)
                activation(sqT.rearrange("p a n -> p (a n)"), two_banks(6), ACT.Copy).then_inc(S["sqT"], 1)
                act.wait_ge(S["ml_cols_ps"], l + 1)
                act.wait_ge(S["ml_a"], l + 1)
                activation(ml_cols[:, 1, :, :], PS[:, 0, 8:16].rearrange("p (t h) -> p t h", t=NT), ACT.Exp,
                             scale=-1.0).then_inc(S["exp_minus_m"], 1)

                def sw_exp(h):
                    act.wait_ge(S["sw_scores"], l * SW_H + h + 1)
                    for t, (lo, hi) in ((1, (0, TOK)), (0, (TOK, 3 * P))):
                        last = activation(sw_s[:, h % 2, lo:hi], sw_s[:, h % 2, lo:hi], ACT.Exp,
                                            bias=sw_stat[:, 0, h, t:t + 1], accum_out=sw_stat[:, 1, h, t:t + 1])
                    last.then_inc(S["sw_p"], 1)

                def sw_copy(h):
                    act.wait_ge(S["sw_t"], l * SW_H + h + 1)
                    if h >= 2:
                        act.wait_ge(S["sw_av"], l * SW_H + h - 1)
                    activation(sw_pT[:, h % 2, :], PS[:, 1, 0:3 * P], ACT.Copy).then_inc(S["sw_pT"], 1)

                def gate_piece(j):
                    piece_done(5 + j)
                    for t in range(NT):
                        activation((ga, gb)[j // 2][:, t, 512 * (j % 2):512 * (j % 2) + 512],
                                   PS[:, (2, 4, 2, 0)[j] + t, :], ACT.Tanh, scale=0.5).then_inc(S["g_copied"], 1)

                sw_exp(0)
                for h in range(SW_H):
                    if h + 1 < SW_H:
                        sw_exp(h + 1)
                    sw_copy(h)
                    if h % 2 == 1 and h < SW_H - 1:
                        gate_piece(h // 2)
                    if h + 2 < SW_H:
                        piece_hi(6 + h // 2, 2 * (h % 2), 2 * (h % 2) + 2)
                act.wait_ge(S["sink_arg"], l + 1)
                activation(sw_stat[:, 2, :, :], sw_stat[:, 2, :, :], ACT.Exp).then_inc(S["sink_exp"], 1)
                for h in range(ML_H):
                    act.wait_ge(S["ml_arg"], l * ML_H + h + 1)
                    for st in range(NT):
                        last = activation(ml_w[:, h, st * TOK:(st + 1) * TOK], ml_w[:, h, st * TOK:(st + 1) * TOK],
                                            ACT.Exp, bias=ml_cols[:, 0, st, h:h + 1])
                    last.then_inc(S["ml_exp"], 1)
                halves_hi(stage_units(OFF_WA, 2), D, before, layer_fills)
                gate_piece(3)
                act.wait_ge(S["tr_b"], l + 1)
                activation(hT_split[:, 0, 4:8, :].rearrange("p k n -> p (k n)"), two_banks(2), ACT.Copy).then_inc(
                    S["hT_b_hi"], 1)
                act.wait_ge(S["tr_a"], l + 1)
                activation(hT_split[:, 0, 0:4, :].rearrange("p k n -> p (k n)"), two_banks(0), ACT.Copy).then_inc(
                    S["hT_a_hi"], 1)
                halves_hi(stage_units(OFF_WB, 2), D, before, layer_fills)
                halves_hi(stage_units(OFF_WO, 4, 0, 4), D, before, layer_fills)
                norm_T_hi("mixed", l)
                halves_hi(stage_units(OFF_WO, 4, 4), D, before, layer_fills)
                gate_up_hi(OFF_FFN2, 0, before, layer_fills)
                norm("ffn2", "x_mix", (2 * l + 1, 2 * l + 2), l)
                norm_T_hi("ffn2", l)
                gate_up_hi(OFF_FFN2, 1, before, layer_fills)
                ffn_tanh(OFF_FFN2, before, layer_fills)
                halves_hi(stage_units(OFF_PLE, 4, 0, 4), D, before, layer_fills)
                norm("ple", "x_ffn2", (2 * l + 1, 2 * l + 2), l)
                act.wait_ge(S["pT_ps"], l + 1)
                activation(pT, PS[:, 0, :].rearrange("p (j n) -> p j n", j=2), ACT.Copy).then_inc(S["pT"], 1)
                norm_T_hi("ple", l)
                halves_hi(stage_units(OFF_PLE, 4, 4), D, before, layer_fills)
                act.wait_ge(S["unit_used"], before + LAYER_UNITS)
                for t in range(NT):
                    activation(ga[:, t, :], two_banks(2 * t), ACT.Tanh, scale=0.5).then_inc(S["ple_tanh"], 1)

        @block.vector
        def _(program):
            V = nc.vector
            dve = InOrder(V, program)
            tt = lambda *args, **kwargs: dve.run(V.tensor_tensor, *args, **kwargs)
            ts = lambda *args, **kwargs: dve.run(V.tensor_scalar, *args, **kwargs)
            stt = lambda *args, **kwargs: dve.run(V.scalar_tensor_tensor, *args, **kwargs)

            def wide_of(v, n):
                return v.unsqueeze(len(v.shape)).to_broadcast(list(v.shape) + [n])

            def heads(v, h):
                return v.rearrange("p t (h d) -> p t h d", h=h)

            dve.wait_ge(S["c_tanh"], 1)
            dve.wait_ge(S["c_full"], 16)
            stt(silu_c, c_tanh, 1.0, c_col, ALU.add, ALU.mult)
            ts(c_wide, wide_of(silu_c, 32), 0.5, None, ALU.mult).then_inc(S["c_wide"], 1)
            dve.wait_ge(S["decay_full"], 32)
            ts(lg_m, lgt, 0.0, None, ALU.min)
            stt(lg_a, lg_m, -2.0, lgt, ALU.mult, ALU.add).then_inc(S["lg_abs"], 1)
            def ada_row(chunk, bias):
                dve.wait_ge(S["slot_used"], used(pos_ada(KT * (chunk + 1) - 1) + 1))
                tt(ada_rows[chunk], PS[:, (7, 6, 7)[chunk], :], bias, ALU.add).then_inc(S["ada_row"], 1)

            dve.wait_ge(S["b_rows_full"], 64)
            dve.wait_ge(S["mean_squares"], norm_turn("pre"))
            ada_row(0, b_rows)
            dve.wait_ge(S["g_pre_full"], 16)
            dve.wait_ge(S["ada"], 1)
            stt(mod[:, 1, :], PS[:, 2:4, :].rearrange("p b n -> p (b n)"), 1.0, g_pre, ALU.add, ALU.mult)
            dve.wait_ge(S["ada_copied"], 1)
            dve.wait_ge(S["row_roots"], norm_turn("pre"))
            dve.wait_ge(S["x_full"], 16)
            for t in range(NT):
                stt(hn[:, t, :], x[:, t, :], ms[:, t:t + 1], mod[:, 1, :], ALU.mult, ALU.mult)
            for t in range(NT):
                last = tt(hn[:, t, :], hn[:, t, :], mod[:, 0, :], ALU.add)
            last.then_inc(S["hn"], NT)

            def plain_hT(name, base):
                for b in (1, 3):
                    dve.wait_ge(S["turned"], 4 * turned_turn(name) + b + 1)
                    dve.run(V.tensor_copy, hT[:, 2 * b:2 * b + 2, :].rearrange("p k n -> p (k n)"),
                                  PS[:, base + b, :]).then_inc(S["hT"], 1)

            plain_hT("pre", 0)
            dve.wait_ge(S["lg_ln"], 1)
            tt(lg, lg_m, lg_a, ALU.subtract)
            dve.wait_ge(S["const_full"], 16)
            dve.wait_ge(S["rel_pos_full"], 16)
            dve.wait_ge(S["rel_neg_full"], 16)
            for h in range(RET_H):
                backward = hn[:, 0, 0:NT * TOK]
                ts(backward, rel[:, 1, :], lg[:, 4 + h:5 + h], None, ALU.mult)
                stt(decay[:, h, :], rel[:, 0, :], lg[:, h:h + 1], backward,
                    ALU.mult, ALU.add).then_inc(S["decay_arg"], 1)
            for j, dst in ((1, rv), (3, aqT), (5, av)):
                dve.wait_ge(S["slot_used"], used(pos_win(j) + 2))
                b = 2 * (j % 3)
                dve.run(V.tensor_copy, dst.rearrange("p a n -> p (a n)"),
                              PS[:, b:b + 2, :].rearrange("p b n -> p (b n)")).then_inc(S[f"piece{j}_copied"], 1)
            dve.wait_ge(S["b_late_full"], 64)
            for i in range(2):
                ada_row(1 + i, b_late[:, i, :])
            for h in range(RET_H):
                dve.wait_ge(S["ret_s"], h + 1)
                dve.wait_ge(S["decay"], h + 1)
                stt(scores[:, h, :], PS[:, h, :], RET_DK ** -0.5, decay[:, h, :], ALU.mult,
                    ALU.mult).then_inc(S["ret_w"], 1)
            dve.wait_ge(S["rg_tanh"], 1)
            dve.wait_ge(S["piece2_copied"], 1)
            stt(rg, rg_tanh, 1.0, rg, ALU.add, ALU.mult)
            dve.wait_ge(S["ret_y"], 1)
            ret_out = PS[:, 0:2, :].rearrange("p t (h d) -> p t h d", h=RET_H)
            by_head = lambda v: v.rearrange("p (t h) -> p t h", t=NT)
            dve.run(V.reduce_sum, by_head(head_mean[:, :]), ret_out, AX.X)
            ts(head_mean[:, :], head_mean[:, :], -1.0 / RET_DV, None, ALU.mult)
            yc = heads(hn[:, :, 0:HALF], RET_H)
            tt(yc, ret_out, wide_of(by_head(head_mean[:, :]), RET_DV), ALU.add).then_inc(S["gn_read"], 1)
            stt(heads(hn[:, :, HALF:D], RET_H), yc, 1.0 / RET_DV, yc, ALU.mult, ALU.mult)
            dve.run(V.reduce_sum, by_head(head_ms[:, :]), heads(hn[:, :, HALF:D], RET_H), AX.X).then_inc(S["var_ret"], 1)
            dve.wait_ge(S["head_roots"], 1)
            tt(yc, yc, wide_of(by_head(head_ms[:, :]), RET_DV), ALU.mult)
            stt(hn[:, :, 0:HALF], hn[:, :, 0:HALF], 0.5, rg, ALU.mult, ALU.mult)

            dve.wait_ge(S["dist_full"], 16)
            dve.wait_ge(S["ln_count_full"], 16)
            for h in range(ATT_H):
                slope = 2.0 ** (-8.0 * (h + 1) / ATT_H)
                stt(att_bias.rearrange("p a b -> p (a b)"), dist, -slope, ln_count, ALU.mult, ALU.add)
                dve.wait_ge(S["att_s"], h + 1)
                if h >= 2:
                    dve.wait_ge(S["att_t"], h - 1)
                s_h = scores[:, h % 2, :].rearrange("p (t n) -> p t n", t=NT)
                stt(s_h, PS[:, 4 + h % 2, :].rearrange("p (t n) -> p t n", t=NT), DH ** -0.5, att_bias,
                    ALU.mult, ALU.add)
                dve.run(V.tensor_reduce, att_stat[:, 0, h, :], s_h, AX.X, ALU.max, negate=True).then_inc(S["att_scores"], 1)
            dve.wait_ge(S["att_p"], ATT_H)
            dve.run(V.reciprocal, att_stat[:, 2, :, :], att_stat[:, 1, :, :])
            dve.wait_ge(S["att_av"], ATT_H)
            tt(heads(hn[:, :, HALF:D], ATT_H), heads(PS[:, 2:4, :], ATT_H),
               wide_of(att_stat[:, 2, :, :].rearrange("p h t -> p t h"), DH), ALU.mult).then_inc(S["hn"], NT)
            plain_hT("y", 4)
            dve.wait_ge(S["ada_copied"], 1 + ATT_H)
            dve.wait_ge(S["gains_full"], 48)
            tt(mod[:, 2, :], mod[:, 2, :], g_post, ALU.mult)
            stt(mod[:, 4, :], mod[:, 4, :], 1.0, g_pre_f, ALU.add, ALU.mult)
            tt(mod[:, 5, :], mod[:, 5, :], g_post_f, ALU.mult)

            def add_normed(gate, signal, name):
                dve.wait_ge(S["row_roots"], norm_turn(name))
                for t in range(NT):
                    stt(hn[:, t, :], PS[:, 2 * t:2 * t + 2, :].rearrange("p b n -> p (b n)"), ms_post[:, t:t + 1],
                        gate, ALU.mult, ALU.mult)
                for t in range(NT):
                    tt(x[:, t, :], x[:, t, :], hn[:, t, :], ALU.add).then_inc(S[signal], 1)

            add_normed(mod[:, 2, :], "x_mid", "post")
            dve.wait_ge(S["row_roots"], norm_turn("moe"))
            for t in range(NT):
                stt(hn[:, t, :], x[:, t, :], ms[:, t:t + 1], mod[:, 4, :], ALU.mult, ALU.mult)
            for t in range(NT):
                last = tt(hn[:, t, :], hn[:, t, :], mod[:, 3, :], ALU.add)
            last.then_inc(S["hn"], NT)
            plain_hT("moe", 4)
            dve.wait_ge(S["logits"], 1)
            dve.run(V.tensor_reduce, rt_stat[:, 0, :], PS[:, 0, 0:NT * NE].rearrange("p (t e) -> p t e", t=NT), AX.X, ALU.max,
                            negate=True).then_inc(S["logits_max"], 1)
            dve.wait_ge(S["aff_exp"], 1)
            dve.run(V.reciprocal, rt_stat[:, 2, :], rt_stat[:, 1, :])
            tt(aff, aff, wide_of(rt_stat[:, 2, :], NE), ALU.mult).then_inc(S["aff"], 1)
            dve.wait_ge(S["affT_ps"], 1)
            dve.run(V.tensor_copy, affT[0:NE, :], PS[0:NE, 1, 0:TOK])
            for i in range(CAP // 8):
                dve.run(V.max, top8[0:NE, :], affT[0:NE, :])
                dve.run(V.match_replace, affT[0:NE, :], top8[0:NE, :], affT[0:NE, :], -1.0)
            ts(chosen[0:NE, :], affT[0:NE, :], -1.0, None, ALU.is_equal)
            dve.run(V.tensor_tensor_scan, count[0:NE, :], chosen[0:NE, :], zeros[0:NE, :], 0.0, ALU.add, ALU.add)
            tt(count[0:NE, :], count[0:NE, :], chosen[0:NE, :], ALU.mult)
            ts(affT[0:NE, :], count[0:NE, :], 1.0, None, ALU.subtract).then_inc(S["place_rows"], 1)
            dve.wait_ge(S["place_ps"], 1)
            dve.run(V.tensor_copy, place.rearrange("p t e -> p (t e)"), PS[:, 2, 0:NT * NE])
            for t in range(NT):
                tt(onehot[:, t, :, :], con("cap_iota").unsqueeze(1).to_broadcast([P, NE, CAP]),
                   wide_of(place[:, t, :], CAP), ALU.is_equal)
            for t in range(NT):
                last = tt(gated[:, t, :, :], onehot[:, t, :, :], wide_of(aff[:, t, :], CAP), ALU.mult)
            last.then_inc(S["onehot"], 1)
            for k in range(1, KT, 2):
                dve.wait_ge(S["gathered"], k + 1)
                dve.run(V.tensor_copy, xeT[:, k, :], PS[:, k, :]).then_inc(S["xeT"], 1)
            dve.wait_ge(S["xeT"], KT)

            for q in dve.loop(NQ):
                for r in range(GROUP):
                    e = q * GROUP + r
                    pos = POS_MOE + r * EXPERT_SLOTS
                    dve.wait_ge(S["xe_free"], e + 1)
                    dve.run(V.tensor_copy, xe, xeT[:, :, bass.ds(e * CAP, CAP)]).then_inc(S["xe"], 1)
                    dve.wait_ge(S["e_tanh"], e + 1)
                    stt(e_act, e_tanh, 1.0, PS[:, 2, :], ALU.add, ALU.mult)
                    dve.wait_ge(S["slot_used"], q * GROUP_SLOTS + used(pos + 2 * KT))
                    stt(e_hid, e_act, 0.5, PS[:, 3, :], ALU.mult, ALU.mult).then_inc(S["e_hid"], 1)
            add_normed(gate_f, "x_layer", "last")

            def norm(name, l):
                dve.wait_ge(S["row_roots"], norm_turn(name, l))
                ts(hn[:, 1, :], x[:, 1, :], ms[:, 1:2], None, ALU.mult).then_inc(S["hn"], 1)

            def norm_T_rest(name, l):
                for b in range(4):
                    dve.wait_ge(S["hT_hi"], 4 * split_turn(name, l) + (b + 1))
                    for k in (2 * b, 2 * b + 1):
                        last = stt(hT_split[:, 1, k, :], PS[:, 4 + b, (k % 2) * TOK:(k % 2) * TOK + TOK],
                                   1.0 if name == "mixed" else p_(name)[:, k:k + 1],
                                   hT_split[:, 0, k, :].bitcast(F32), ALU.mult, ALU.subtract)
                    last.then_inc(S["hT"], 1)

            def split_rest(u, weights, base):
                dve.wait_ge(S["unit_hi"], base + (u + 1))
                dims = weights.shape[1:]
                tt(unit(1, u, *dims), weights, unit(0, u, *dims).bitcast(F32), ALU.subtract).then_inc(
                    S["unit_split"], 1)

            def halves_rest(us, width, base):
                for u in us:
                    split_rest(u, half_slot(u, width)[0], base)

            def gate_up_rest(off, c, base):
                for part in range(2):
                    split_rest(2 * off + gate_unit(c) + part, gate_up_weights(POS_LAYER + off, c, part), base)

            def down_rest(off, c, base):
                split_rest(2 * off + down_unit(c), down_weights(POS_LAYER + off, c), base)

            def ffn_hidden(off, hidden, base):
                def sub(c, hidden, base):
                    dve.wait_ge(S["f_tanh"], hidden + (c + 1))
                    act_ = f_act[:, c % 2, :]
                    stt(act_, f_tanh[:, c % 2, :], 1.0, PS[:, 4 + c % 4, 0:TOK], ALU.add, ALU.mult)
                    tt(act_, act_, PS[:, 4 + c % 4, TOK:2 * TOK], ALU.mult)
                    dve.run(V.tensor_copy, hid_split[:, 0, c % 2, :], act_)
                    tt(hid_split[:, 1, c % 2, :], act_, hid_split[:, 0, c % 2, :].bitcast(F32),
                       ALU.subtract).then_inc(S["f_hid"], 1)
                    if c + 2 < FFN_SUBS:
                        gate_up_rest(off, c + 2, base)
                    if c + 1 < FFN_SUBS:
                        down_rest(off, c + 1, base)

                down_rest(off, 0, base)
                for b in dve.loop(FFN_PAIRS):
                    for c in range(4):
                        sub(c, hidden + b * 4, base + b * 12)
                for c in range(4 * FFN_PAIRS, FFN_SUBS):
                    sub(c, hidden, base)

            def add_rows(scale, signal):
                for t in range(NT):
                    stt(x[:, t, :], PS[:, 2 * t:2 * t + 2, :].rearrange("p b n -> p (b n)"), scale, x[:, t, :],
                        ALU.mult, ALU.add).then_inc(S[signal], 1)

            for l in dve.loop(LAYERS):
                before = l * LAYER_UNITS
                norm("ffn1", l)
                dve.wait_ge(S["gain_full"], (l + 1) * 16)
                norm_T_rest("ffn1", l)
                for c in range(2):
                    gate_up_rest(OFF_FFN1, c, before)
                ffn_hidden(OFF_FFN1, l * 2 * FFN_SUBS, before)
                dve.wait_ge(S["par_full"], (l + 1) * 16 * 9)

                def piece_rest(j, first=0, last=4):
                    halves_rest(stage_units(OFF_Z + 2 * j, 2, first, last), Z_PIECES[j][1], before)

                def used_to(off):
                    dve.wait_ge(S["unit_used"], before + 2 * off)

                piece_rest(0, 0, 3)
                used_to(OFF_Z)
                add_rows(0.25, "x_ffn1")
                piece_rest(0, 3)
                norm("mix", l)
                norm_T_rest("mix", l)
                piece_rest(1)
                dve.run(V.memset, mva[:, :, :, ML_DV:ML_DV + 1], 1.0)
                piece_rest(2)
                used_to(OFF_Z + 4)
                G = lambda i: gates[0:ML_H, i, :]
                ts(G(1), PS[0:ML_H, 7, 0:TOK], p_("b_f")[0:ML_H, :], None, ALU.add).then_inc(S["gate_f"], 1)
                ts(G(2), G(1), 0.0, None, ALU.min)
                stt(G(3), G(2), -2.0, G(1), ALU.mult, ALU.add).then_inc(S["f_abs"], 1)
                piece_rest(3)
                used_to(OFF_Z + 6)
                dve.run(V.tensor_copy, sq[:, :, 384:512], PS[:, 0:2, 0:P])
                dve.run(V.tensor_copy, sk, PS[:, 0:2, P:2 * P])
                dve.run(V.tensor_copy, sv, PS[:, 0:2, 2 * P:3 * P]).then_inc(S["sk_copied"], 1)
                dve.wait_ge(S["f_ln"], l + 1)
                tt(G(5), G(2), G(4), ALU.subtract)
                dve.run(V.tensor_tensor_scan, G(6), G(5), zeros[0:ML_H, :], 0.0, ALU.add, ALU.add)
                dve.wait_ge(S["gate_i"], l + 1)
                tt(G(7), G(0), G(6), ALU.subtract)
                dve.run(V.tensor_tensor_scan, G(1), G(7), G(7), 0.0, ALU.max, ALU.max)
                tt(G(2), G(6), G(1), ALU.add).then_inc(S["scan"], 1)
                dve.wait_ge(S["sq_copied"], l + 1)
                by16 = lambda v: v.rearrange("p t (h d) -> p (t h) d", d=DH)
                tmp = hn[:, 0, :].rearrange("p (h d) -> p h d", d=DH)
                tmp_k = hn[:, 1, 0:TOK].rearrange("p (h d) -> p h d", d=DH)
                stt(tmp, by16(sq), 1.0 / DH, by16(sq), ALU.mult, ALU.mult)
                stt(tmp_k, by16(sk), 1.0 / DH, by16(sk), ALU.mult, ALU.mult)
                dve.run(V.reduce_sum, qk_ms[:, 0:16], tmp, AX.X)
                dve.run(V.reduce_sum, qk_ms[:, 16:20], tmp_k, AX.X).then_inc(S["ms_qk"], 1)
                piece_rest(4)
                used_to(OFF_Z + 8)
                dve.run(V.tensor_copy, mva[:, :, :, 0:ML_DV], heads(PS[:, 2:4, :], ML_H)).then_inc(S["mva"], 1)
                dve.wait_ge(S["qk_roots"], l + 1)
                tt(by16(sq), by16(sq), wide_of(qk_ms[:, 0:16], DH), ALU.mult)
                tt(by16(sk), by16(sk), wide_of(qk_ms[:, 16:20], DH), ALU.mult)
                kd_v = kd.rearrange("p t (g u d) -> p (t g) u d", g=SW_KV, u=2)
                for u in range(2):
                    tt(kd_v[:, :, u, :], by16(sk), p_("k_gain").unsqueeze(1).to_broadcast([P, 4, DH]), ALU.mult)
                tt(by16(sq), by16(sq), p_("q_gain").unsqueeze(1).to_broadcast([P, 16, DH]),
                   ALU.mult).then_inc(S["qk_normed"], 1)
                piece_rest(5)
                dve.wait_ge(S["tk"], l + 1)
                dve.run(V.tensor_copy, skT.rearrange("p g n -> p (g n)"), PS[:, 1, :]).then_inc(S["skT"], 1)
                dve.wait_ge(S["ml_cols_ps"], l + 1)
                dve.run(V.tensor_copy, ml_cols[:, 0, :, :], PS[:, 0, 0:8].rearrange("p (t h) -> p t h", t=NT)).then_inc(
                    S["ml_a"], 1)

                for h in range(SW_H):
                    dve.wait_ge(S["sw_sc"], l * SW_H + h + 1)
                    if h == 0:
                        dve.wait_ge(S["band_full"], 16)
                    else:
                        if h >= 2:
                            dve.wait_ge(S["sw_t"], l * SW_H + h - 1)
                    stt(sw_s[:, h % 2, 0:TOK], PS[:, 0, 0:TOK], DH ** -0.5, band[:, h, :], ALU.mult, ALU.add)
                    stt(sw_s[:, h % 2, TOK:3 * P], PS[:, 0, TOK:3 * P], DH ** -0.5, band[:, h, P:TOK],
                        ALU.mult, ALU.add)
                    dve.run(V.reduce_max, sw_stat[:, 0, h, 1:2], sw_s[:, h % 2, 0:TOK], AX.X)
                    dve.run(V.reduce_max, sw_stat[:, 0, h, 0:1], sw_s[:, h % 2, TOK:3 * P], AX.X)
                    ts(sw_stat[:, 0, h, :], sw_stat[:, 0, h, :], p_("sink")[:, h:h + 1], -1.0, ALU.max,
                       ALU.mult).then_inc(S["sw_scores"], 1)
                    if 1 <= h < SW_H - 1:
                        piece_rest(5 + (h + 1) // 2, 2 * ((h + 1) % 2), 2 * ((h + 1) % 2) + 2)
                tt(sw_stat[:, 2, :, :], sw_stat[:, 0, :, :], wide_of(p_("sink"), NT), ALU.add).then_inc(
                    S["sink_arg"], 1)
                for h in range(ML_H):
                    if h % 2 == 0:
                        dve.wait_ge(S["neg_m"], l * 2 + h // 2 + 1)
                    m_h = PS[:, 4 + h // 2, (h % 2) * TOK:(h % 2) * TOK + TOK]
                    last = tt(ml_w[:, h, :].rearrange("p (s n) -> p s n", s=NT),
                              con("causal", NT), m_h.unsqueeze(1).to_broadcast([P, NT, TOK]), ALU.add)
                    last.then_inc(S["ml_arg"], 1)
                dve.wait_ge(S["sink_exp"], l + 1)
                tt(sw_stat[:, 3, :, :], sw_stat[:, 1, :, :], sw_stat[:, 2, :, :], ALU.add)
                dve.run(V.reciprocal, sw_stat[:, 3, :, :], sw_stat[:, 3, :, :])
                dve.wait_ge(S["sw_av"], (l + 1) * SW_H)
                tt(heads(hn[:, :, HALF:D], SW_H), heads(PS[:, 6:8, :], SW_H),
                   wide_of(sw_stat[:, 3, :, :].rearrange("p h t -> p t h"), DH), ALU.mult).then_inc(S["h_b"], 1)
                for h in range(ML_H):
                    dve.wait_ge(S["ml_exp"], l * ML_H + h + 1)
                    dve.wait_ge(S["ml_s"], l * ML_H + h + 1)
                    stt(ml_w[:, h, :], ml_w[:, h, :], 64 ** -0.5, PS[:, h, :], ALU.mult, ALU.mult).then_inc(
                        S["ml_w"], 1)
                dve.wait_ge(S["ml_av"], (l + 1) * ML_H)
                dve.wait_ge(S["exp_minus_m"], l + 1)
                den = ml_den.rearrange("p (t h) -> p t h", t=NT)
                num = lambda t, pair: PS[:, 6 + t - 2 * pair, 0:2 * (ML_DV + 1)].rearrange("p (h n) -> p h n", h=2)
                parts = [(t, pair) for t in range(NT) for pair in range(2)]
                den_of = lambda t, pair: den[:, t, 2 * pair:2 * pair + 2].unsqueeze(2)
                for t, pair in parts:
                    ts(den_of(t, pair), num(t, pair)[:, :, ML_DV:ML_DV + 1], -1.0, None, ALU.mult)
                for t, pair in parts:
                    tt(den_of(t, pair), den_of(t, pair), num(t, pair)[:, :, ML_DV:ML_DV + 1], ALU.max)
                tt(den, den, ml_cols[:, 1, :, :], ALU.max)
                dve.run(V.reciprocal, ml_den, ml_den)
                h_a = heads(hn[:, :, 0:HALF], ML_H)
                for t, pair in parts:
                        tt(h_a[:, t, 2 * pair:2 * pair + 2, :], num(t, pair)[:, :, 0:ML_DV],
                           wide_of(den[:, t, 2 * pair:2 * pair + 2], ML_DV), ALU.mult)
                stt(heads(sq, ML_H), h_a, 1.0 / ML_DV, h_a, ALU.mult, ALU.mult)
                dve.run(V.reduce_sum, by_head(head_ms[:, :]), heads(sq, ML_H), AX.X).then_inc(S["ms_ha"], 1)
                dve.wait_ge(S["mo"], l + 1)
                for t in range(NT):
                    stt(mo[:, t, :], mo[:, t, :], 1.0, p_("ml_gain"), ALU.add, ALU.mult)
                dve.wait_ge(S["head_roots"], l + 2)
                tt(h_a, h_a, wide_of(by_head(head_ms[:, :]), ML_DV), ALU.mult)
                tt(hn[:, :, 0:HALF], hn[:, :, 0:HALF], mo, ALU.mult).then_inc(S["h_a"], 1)
                for half, name, bank in ((1, "hT_b", 2), (0, "hT_a", 0)):
                    dve.wait_ge(S[name + "_hi"], l + 1)
                    part = hT_split[:, :, 4 * half:4 * half + 4, :].rearrange("p i k n -> p i (k n)")
                    tt(part[:, 1, :], PS[:, bank:bank + 2, :].rearrange("p b n -> p (b n)"),
                       part[:, 0, :].bitcast(F32), ALU.subtract).then_inc(S[name], 1)
                    halves_rest(stage_units(OFF_WA, 2, 2 - 2 * half, 4 - 2 * half), D, before)
                halves_rest(stage_units(OFF_WB, 2), D, before)
                dve.wait_ge(S["g_copied"], 8 * (l + 1))
                used_to(OFF_WA + 2)
                for t in range(NT):
                    last = stt(ga[:, t, :], ga[:, t, :], 1.0, PS[:, 4 + 2 * t:6 + 2 * t, :].rearrange("p b n -> p (b n)"),
                               ALU.add, ALU.mult)
                last.then_inc(S["ya_read"], 1)
                used_to(OFF_WB + 2)
                for t in range(NT):
                    stt(gb[:, t, :], gb[:, t, :], 1.0, PS[:, 2 * t:2 * t + 2, :].rearrange("p b n -> p (b n)"),
                        ALU.add, ALU.mult)
                    stt(hn[:, t, :], ga[:, t, :], 0.5, gb[:, t, :], ALU.mult, ALU.add).then_inc(S["hn"], 1)
                halves_rest(stage_units(OFF_WO, 4, 0, 2), D, before)
                norm_T_rest("mixed", l)
                halves_rest(stage_units(OFF_WO, 4, 2), D, before)
                gate_up_rest(OFF_FFN2, 0, before)
                used_to(OFF_FFN2)
                add_rows(0.5, "x_mix")
                norm("ffn2", l)
                norm_T_rest("ffn2", l)
                gate_up_rest(OFF_FFN2, 1, before)
                ffn_hidden(OFF_FFN2, l * 2 * FFN_SUBS + FFN_SUBS, before)
                halves_rest(stage_units(OFF_PLE, 4, 0, 3), D, before)
                used_to(OFF_PLE)
                add_rows(0.25, "x_ffn2")
                halves_rest(stage_units(OFF_PLE, 4, 3, 4), D, before)
                norm("ple", l)
                norm_T_rest("ple", l)
                halves_rest(stage_units(OFF_PLE, 4, 4), D, before)
                dve.wait_ge(S["ple_tanh"], NT * (l + 1))
                dve.wait_ge(S["ple_up"], l + 1)
                for t in range(NT):
                    stt(ga[:, t, :], ga[:, t, :], 1.0, PS[:, 4 + 2 * t:6 + 2 * t, :].rearrange("p b n -> p (b n)"),
                        ALU.add, ALU.mult)
                for t in range(NT):
                    stt(x[:, t, :], ga[:, t, :], 0.5, x[:, t, :], ALU.mult, ALU.add).then_inc(S["x_layer"], 1)

        @block.tensor
        def _(pe):
            mm = nc.tensor.matmul

            def full(pos, fills=0):
                pe.wait_ge(S[f"slot{pos % R}_full"], fills + 16 * (pos // R + 1))

            def transpose_rows(name, base, l=0, also=None):
                pe.wait_ge(S["hn"], NT * (turned_turn(name, l) + 1))
                for k in range(KT):
                    for t in range(NT):
                        last = nc.tensor.transpose(PS[:, base + k // 2, (k % 2) * TOK + t * P:(k % 2) * TOK + (t + 1) * P],
                                                   hn[:, t, k:D:KT], ident)
                        if also and k + t == 0:
                            last.then_inc(*also)
                    if k % 2 == 1:
                        last.then_inc(S["turned"], 1)

            def rows_product(pos, slots, per_slot, banks, fills, lhs, signal=True):
                n_k = slots * per_slot
                for s in range(slots):
                    full(pos + s, fills)
                    w = slot(pos + s, per_slot, D)
                    for i in range(per_slot):
                        k = s * per_slot + i
                        for t in range(NT):
                            for n in range(2):
                                last = mm(PS[:, banks + 2 * t + n, :], lhs(k, t), w[:, i, 512 * n:512 * n + 512],
                                          start=(k == 0), stop=(k == n_k - 1))
                    last.then_inc(S["slot_used"], 1)

            hT_tile = lambda k, t: hT[:, k, t * P:(t + 1) * P]

            pe.wait_ge(S["c_wide"], 1)

            def ada_product(i):
                chunk, k = i // KT, i % KT
                full(pos_ada(i))
                for g in range(4):
                    last = mm(PS[32 * g:32 * g + 32, (7, 6, 7)[chunk], :], c_wide[:, k, :],
                              slot(pos_ada(i), SLOT)[:, 512 * g:512 * g + 512], start=(k == 0), stop=(k == KT - 1),
                              tile_position=(0, 32 * g))
                last.then_inc(S["slot_used"], 1)

            def ada_to_all(chunk, g, bank):
                return mm(PS[:, bank, :], ident[:, 32 * g:32 * g + 1].to_broadcast([P, P]), ada_rows[chunk],
                          start=True, stop=True)

            for i in range(KT):
                ada_product(i)
            pe.wait_ge(S["ada_row"], 1)
            pe.wait_ge(S["const_full"], 16)
            for g in range(4):
                last = ada_to_all(0, g, g)
            last.then_inc(S["ada"], 1)
            transpose_rows("pre", 0)
            pe.wait_ge(S["hT"], 4 * (turned_turn("pre") + 1))
            pe.wait_ge(S["relb_full"], 16)
            pe.wait_ge(S["bucket_full"], 16)
            for h in range(SW_H):
                last = mm(PS[:, h, 0:3 * P], relb[:, h:h + 1].to_broadcast([BUCKETS + 1, P]),
                          bucket[0:BUCKETS + 1, :], start=True, stop=True)
            last.then_inc(S["rep"], 1)
            pe.wait_ge(S["rep_copied"], 1)
            for j in range(WIN_PIECES):
                pos = pos_win(j)
                full(pos)
                b = 2 * (j % 3)
                if j >= 3:
                    pe.wait_ge(S[f"piece{j - 3}_copied"], 1)
                w = [slot(pos + k // 4, 4, 512)[:, k % 4, :] for k in range(KT)]
                for part in range(4 if j in (0, 3, 4) else NT):
                    for k in range(KT):
                        if part == 0 and k == KT // 2:
                            full(pos + 1)
                        if j in (0, 3, 4):
                            last = mm(PS[:, b + part // 2, (part % 2) * TOK:(part % 2) * TOK + TOK],
                                      w[k][:, part * P:(part + 1) * P], hT[:, k, :], start=(k == 0), stop=(k == 7))
                        else:
                            last = mm(PS[:, b + part, :], hT_tile(k, part), w[k], start=(k == 0), stop=(k == 7))
                last.then_inc(S["slot_used"], 2)
                for i in range(KT + 3 * j, min(KT + 3 * j + 3, ADA_SLOTS)):
                    ada_product(i)
            pe.wait_ge(S["piece0_copied"], 1)
            pe.wait_ge(S["piece3_copied"], 1)
            pe.wait_ge(S["piece4_copied"], 1)
            for h in range(RET_H):
                lo = 64 * (h % 2)
                for st in range(NT):
                    last = mm(PS[:, h, st * TOK:(st + 1) * TOK], qkT[lo:lo + 64, 2 + h // 2, st * P:(st + 1) * P],
                              qkT[lo:lo + 64, h // 2, :], start=True, stop=True)
                last.then_inc(S["ret_s"], 1)

            def att_s(h):
                lo = 64 * (h % 2)
                for t in range(NT):
                    last = mm(PS[:, 4 + h % 2, t * TOK:(t + 1) * TOK], aqT[lo:lo + 64, h // 2, t * P:(t + 1) * P],
                              akT[lo:lo + 64, h // 2, :], start=True, stop=True)
                last.then_inc(S["att_s"], 1)

            def att_av(h):
                pe.wait_ge(S["att_pT"], h + 1)
                for t in range(NT):
                    for st in range(NT):
                        last = mm(PS[:, 2 + t, h * DH:(h + 1) * DH],
                                  scores[:, 2 + h % 2, st * TOK + t * P:st * TOK + (t + 1) * P],
                                  av[:, st, h * DH:(h + 1) * DH], start=(st == 0), stop=(st == NT - 1))
                last.then_inc(S["att_av"], 1)

            pe.wait_ge(S["piece5_copied"], 1)
            att_s(0)
            att_s(1)
            pe.wait_ge(S["ret_w"], RET_H)
            for t in range(NT):
                for h in range(RET_H):
                    for st in range(NT):
                        last = mm(PS[:, t, h * P:(h + 1) * P], scores[:, h, st * TOK + t * P:st * TOK + (t + 1) * P],
                                  rv[:, st, h * P:(h + 1) * P], start=(st == 0), stop=(st == NT - 1))
            last.then_inc(S["ret_y"], 1)
            pe.wait_ge(S["gn_read"], 1)
            for h in range(ATT_H):
                pe.wait_ge(S["att_p"], h + 1)
                if h >= 2:
                    pe.wait_ge(S["att_pT"], h - 1)
                for st in range(NT):
                    for t in range(NT):
                        last = nc.tensor.transpose(PS[:, h % 2, st * TOK + t * P:st * TOK + (t + 1) * P],
                                                   scores[:, h % 2, t * TOK + st * P:t * TOK + (st + 1) * P], ident)
                last.then_inc(S["att_t"], 1)
                if h + 2 < ATT_H:
                    att_s(h + 2)
                if h >= 1:
                    att_av(h - 1)
                if h == 0:
                    pe.wait_ge(S["ada_row"], 3)
                if h >= 2:
                    pe.wait_ge(S["ada_copied"], h)
                ada_to_all(1 + h // 4, h % 4, 6 + h % 2).then_inc(S["ada"], 1)
            att_av(ATT_H - 1)
            pe.wait_ge(S["ada_copied"], 1 + ATT_H)
            transpose_rows("y", 4)
            pe.wait_ge(S["hT"], 4 * (turned_turn("y") + 1))
            rows_product(POS_WOUT, 4, 2, 0, 0, hT_tile)

            transpose_rows("moe", 4)
            pe.wait_ge(S["hT"], 4 * (turned_turn("moe") + 1))
            pe.wait_ge(S["router_full"], 16)
            for t in range(NT):
                for k in range(KT):
                    last = mm(PS[:, 0, t * NE:(t + 1) * NE], hT_tile(k, t), w_router[:, k, :], start=(k == 0),
                              stop=(k == KT - 1))
            last.then_inc(S["logits"], 1)
            pe.wait_ge(S["aff"], 1)
            for t in range(NT):
                last = nc.tensor.transpose(PS[0:NE, 1, t * P:(t + 1) * P], aff[:, t, :], ident)
            last.then_inc(S["affT_ps"], 1)
            pe.wait_ge(S["place_rows"], 1)
            for t in range(NT):
                last = nc.tensor.transpose(PS[:, 2, t * NE:(t + 1) * NE], affT[0:NE, t * P:(t + 1) * P],
                                           ident[0:NE, 0:NE])
            last.then_inc(S["place_ps"], 1)
            pe.wait_ge(S["onehot"], 1)
            for k in range(KT):
                for t in range(NT):
                    last = mm(PS[:, k, :], hn[:, t, k:D:KT], onehot[:, t, :, :].rearrange("p e c -> p (e c)"),
                              start=(t == 0), stop=(t == NT - 1))
                last.then_inc(S["gathered"], 1)
            pe.wait_ge(S["xeT"], KT)
            for q in range(NQ):
                for t in range(NT):
                    last = nc.tensor.transpose(
                        PS[:, q // 2, (q % 2) * TOK + t * P:(q % 2) * TOK + (t + 1) * P],
                        gated[:, t, GROUP * q:GROUP * q + GROUP, :].rearrange("p e c -> p (e c)"), ident)
            last.then_inc(S["GT_ps"], 1)

            with pe.Fori(0, NQ) as q:
                fills = q * (GROUP_SLOTS // R * 16)
                for r in range(GROUP):
                    e = q * GROUP + r
                    pos = POS_MOE + r * EXPERT_SLOTS
                    pe.wait_ge(S["xe"], e + 1)
                    for part in range(2):
                        for k in range(KT):
                            at = pos + part * KT + k
                            full(at, fills)
                            for g in range(4):
                                last = mm(PS[32 * g:32 * g + 32, 2 + part, :], xe[:, k, :],
                                          slot(at, SLOT)[:, 512 * g:512 * g + 512],
                                          start=(k == 0), stop=(k == KT - 1), tile_position=(0, 32 * g))
                            last.then_inc(S["slot_used"], 1)
                    pe.wait_ge(S["e_hid"], e + 1)
                    for s in range(4):
                        last = nc.tensor.transpose(PS[:, 4, s * P:(s + 1) * P], e_hid[:, s:512:4], ident)
                        if s == 0:
                            last.then_inc(S["xe_free"], 1)
                    last.then_inc(S["e_tr"], 1)
                    pe.wait_ge(S["e_hT"], e + 1)
                    pe.wait_ge(S["y_copied"], e + 1)
                    for j in range(4):
                        for s in range(4):
                            at = pos + 2 * KT + 2 * j + s // 2
                            if s % 2 == 0:
                                full(at, fills)
                            for g in range(4):
                                last = mm(PS[32 * g:32 * g + 32, 5, 0:256], e_hT[:, s, 32 * j:32 * j + 32],
                                          slot(at, 2, D)[:, s % 2, 256 * g:256 * g + 256],
                                          start=(j == 0 and s == 0), stop=(j == 3 and s == 3),
                                          tile_position=(0, 32 * g))
                            if s % 2 == 1:
                                last.then_inc(S["slot_used"], 1)
            pe.wait_ge(S["GT"], 1)
            pe.wait_ge(S["y_copied"], NE + 1)
            for t in range(NT):
                for n in range(2):
                    for q in range(NQ):
                        last = mm(PS[:, 2 * t + n, :], GT[:, q, t * P:(t + 1) * P], Y[:, q, 512 * n:512 * n + 512],
                                  start=(q == 0), stop=(q == NQ - 1))
            last.then_inc(S["combined"], 1)

            with pe.Fori(0, LAYERS) as l:
                layer_fills = l * (LAYER_SLOTS // R * 16)

                def split_mm(out, lhs, rhs, start, stop, **flags):
                    passes = [mm(out, lhs[i], rhs[j], start=start and i + j == 0, stop=stop and i == 1, **flags)
                              for i, j in ((0, 0), (0, 1), (1, 0))]
                    return passes[0], passes[-1]

                def take(u):
                    pe.wait_ge(S["unit_split"], l * LAYER_UNITS + (u + 1))

                def halves_product(us, first_k, n_k, width, outs, turn=None):
                    per_unit = half_slot(0, width)[1] // width
                    for n, u in enumerate(us):
                        take(u)
                        for kk in range(per_unit):
                            k = first_k + n * per_unit + kk
                            if turn is not None and k % 2 == 0:
                                pe.wait_ge(S["hT"], 4 * turn + (k // 2 + 1))
                            w = [unit(i, u, per_unit, width)[:, kk, :] for i in range(2)]
                            for m, (out_, lhs, rhs) in enumerate(outs(w, k)):
                                first, last = split_mm(out_, lhs, rhs, start=(k == 0), stop=(k == n_k - 1))
                                if u % 2 == 1 and kk + m == 0:
                                    first.then_inc(S["slot_used"], 1)
                        last.then_inc(S["unit_used"], 1)

                hT_rows = lambda k, t: [hT_split[:, i, k, t * P:(t + 1) * P] for i in range(2)]
                hT_cols = lambda k: [hT_split[:, i, k, :] for i in range(2)]
                columns = lambda w, lo, hi: [v[:, lo:hi] for v in w]

                def rows_split(off, n_k, banks, k_at=0, turn=None):
                    halves_product(stage_units(off, n_k // 2), 0, n_k, D, lambda w, k: [
                        (PS[:, banks + 2 * t + n, :], hT_rows(k_at + k, t), columns(w, 512 * n, 512 * n + 512))
                        for t in range(NT) for n in range(2)], turn)

                def ffn(off, hidden, base, turn):
                    for b in range(4):
                        mm(PS[:, b, 0:2], zeros[0:1, 0:P], zeros[0:1, 0:2], start=True, stop=False,
                           skip_group_check=True)

                    def up(c, base, turn=None):
                        for part in range(2):
                            n = 2 * off + gate_unit(c) + part
                            pe.wait_ge(S["unit_split"], base + (n + 1))
                            for k in range(KT):
                                if turn is not None and part == 0 and k % 2 == 0:
                                    pe.wait_ge(S["hT"], 4 * turn + (k // 2 + 1))
                                first, last = split_mm(PS[:, 4 + c % 4, part * TOK:(part + 1) * TOK],
                                                       [unit(i, n, KT, P)[:, k, :] for i in range(2)],
                                                       [hT_split[:, i, k, :] for i in range(2)],
                                                       start=(k == 0), stop=(k == KT - 1))
                                if k == 0 and c % 2 == 1:
                                    first.then_inc(S["slot_used"], 1)
                            last.then_inc(S["unit_used"], 1)

                    def down(c, hidden, base):
                        n = 2 * off + down_unit(c)
                        pe.wait_ge(S["f_hid"], hidden + (c + 1))
                        pe.wait_ge(S["unit_split"], base + (n + 1))
                        for t in range(NT):
                            for half in range(2):
                                first, last = split_mm(
                                    PS[:, 2 * t + half, :],
                                    [hid_split[:, i, c % 2, t * P:(t + 1) * P] for i in range(2)],
                                    [unit(i, n)[:, 512 * half:512 * half + 512] for i in range(2)],
                                    start=False, stop=False, skip_group_check=True)
                                if t + half == 0 and c % 2 == 1:
                                    first.then_inc(S["slot_used"], 1)
                        last.then_inc(S["unit_used"], 1)

                    up(0, base, turn)
                    with pe.Fori(0, FFN_PAIRS) as b:
                        for c in range(4):
                            up(c + 1, base + b * 12)
                            down(c, hidden + b * 4, base + b * 12)
                    for c in range(4 * FFN_PAIRS, FFN_SUBS):
                        if c + 1 < FFN_SUBS:
                            up(c + 1, base)
                        down(c, hidden, base)

                transpose_rows("ffn1", 4, l)
                ffn(OFF_FFN1, l * 2 * FFN_SUBS, l * LAYER_UNITS, turned_turn("ffn1", l))
                transpose_rows("mix", 4, l)

                def piece(j, outs, first=0, last=4, turn=None):
                    halves_product(stage_units(OFF_Z + 2 * j, 2, first, last), 2 * first, KT, Z_PIECES[j][1], outs,
                                   turn)

                def z_rows(bank, lo, hi):
                    return lambda w, k: [(PS[:, bank + t, 0:hi - lo], hT_rows(k, t), columns(w, lo, hi))
                                         for t in range(NT)]

                piece(0, lambda w, k: [(PS[:, part, 0:TOK], columns(w, part * P, (part + 1) * P), hT_cols(k))
                                       for part in range(4)], turn=turned_turn("mix", l))
                piece(1, lambda w, k: [(PS[0:ML_H, 6 + g, 0:TOK], columns(w, ML_H * g, ML_H * g + ML_H), hT_cols(k))
                                       for g in range(2)] + z_rows(4, 2 * ML_H, 2 * ML_H + 384)(w, k))
                pe.wait_ge(S["mqkT"], l + 1)
                piece(2, z_rows(0, 0, 384))
                piece(3, z_rows(2, 0, 512))
                pe.wait_ge(S["sq_copied"], l + 1)
                piece(4, z_rows(4, 0, 512))
                pe.wait_ge(S["gate_i"], l + 1)
                pe.wait_ge(S["gate_f"], l + 1)
                pe.wait_ge(S["qk_normed"], l + 1)
                for j in range(4):
                    for t in range(NT):
                        last = nc.tensor.transpose(PS[:, 6 + j // 2, (j % 2) * TOK + t * P:(j % 2) * TOK + (t + 1) * P],
                                                   sq[:, t, j * P:(j + 1) * P], ident)
                last.then_inc(S["tq"], 1)
                pe.wait_ge(S["scan"], l + 1)
                pe.wait_ge(S["sk_copied"], l + 1)
                for g in range(SW_KV):
                    for t in range(NT):
                        last = nc.tensor.transpose(PS[:, 1, g * TOK + t * P:g * TOK + (t + 1) * P],
                                                   kd[:, t, g * P:(g + 1) * P], ident)
                last.then_inc(S["tk"], 1)
                for which, at in ((7, 0), (2, 8)):
                    for t in range(NT):
                        last = nc.tensor.transpose(PS[:, 0, at + ML_H * t:at + ML_H * t + ML_H],
                                                   gates[0:ML_H, which, t * P:(t + 1) * P], ident[0:ML_H, 0:ML_H])
                last.then_inc(S["ml_cols_ps"], 1)
                pe.wait_ge(S["sqT"], l + 1)
                pe.wait_ge(S["skT"], l + 1)
                pe.wait_ge(S["ml_a"], l + 1)
                pe.wait_ge(S["exp_minus_m"], l + 1)

                def sw_s_(h):
                    lo, g = 64 * (h % 2), h // (SW_H // SW_KV)
                    q_h, k_h = sqT[lo:lo + 64, h // 2, :], skT[lo:lo + 64, g, :]
                    mm(PS[:, 0, 0:TOK], q_h[:, P:TOK], k_h, start=True, stop=True)
                    mm(PS[:, 0, TOK:3 * P], q_h[:, 0:P], k_h[:, 0:P], start=True, stop=True).then_inc(
                        S["sw_sc"], 1)

                def sw_av(h):
                    g = h // (SW_H // SW_KV)
                    v = lambda st: sv[:, st, g * DH:(g + 1) * DH]
                    pe.wait_ge(S["sw_pT"], l * SW_H + h + 1)
                    mm(PS[:, 6, h * DH:(h + 1) * DH], sw_pT[:, h % 2, TOK:3 * P], v(0), start=True, stop=True)
                    mm(PS[:, 7, h * DH:(h + 1) * DH], sw_pT[:, h % 2, 0:P], v(0), start=True, stop=False)
                    mm(PS[:, 7, h * DH:(h + 1) * DH], sw_pT[:, h % 2, P:TOK], v(1), start=False, stop=True).then_inc(
                        S["sw_av"], 1)

                sw_s_(0)
                pe.wait_ge(S["mva"], l + 1)
                pe.wait_ge(S["mo"], l + 1)
                for h in range(SW_H):
                    if h + 1 < SW_H:
                        pe.wait_ge(S["sw_scores"], l * SW_H + h + 1)
                        sw_s_(h + 1)
                    pe.wait_ge(S["sw_p"], l * SW_H + h + 1)
                    if h >= 1:
                        pe.wait_ge(S["sw_pT"], l * SW_H + h)
                    for at in (0, P, TOK):
                        last = nc.tensor.transpose(PS[:, 1, at:at + P], sw_s[:, h % 2, at:at + P], ident)
                    last.then_inc(S["sw_t"], 1)
                    if h >= 1:
                        sw_av(h - 1)
                    j = h // 2
                    if j < 3:
                        if j == 2 and h % 2 == 0:
                            pe.wait_ge(S["g_copied"], l * 8 + 2)
                        piece(5 + j, z_rows((2, 4, 2)[j], 0, 512), 2 * (h % 2), 2 * (h % 2) + 2)
                sw_av(SW_H - 1)
                pe.wait_ge(S["g_copied"], l * 8 + 6)
                for h in range(ML_H):
                    last = mm(PS[:, 4 + h // 2, (h % 2) * TOK:(h % 2) * TOK + TOK],
                              con("minus_row")[0:ML_H, h * P:(h + 1) * P], gates[0:ML_H, 1, :], start=True, stop=True)
                    if h % 2 == 1:
                        last.then_inc(S["neg_m"], 1)
                for h in range(ML_H):
                    lo = 64 * (h % 2)
                    for st in range(NT):
                        last = mm(PS[:, h, st * TOK:(st + 1) * TOK], mqkT[lo:lo + 64, 2 + h // 2, st * P:(st + 1) * P],
                                  mqkT[lo:lo + 64, h // 2, :], start=True, stop=True)
                    last.then_inc(S["ml_s"], 1)
                pe.wait_ge(S["h_b"], l + 1)
                for h in range(ML_H):
                    if h == 2:
                        pe.wait_ge(S["ml_arg"], ML_H * (l + 1))
                    pe.wait_ge(S["ml_w"], l * ML_H + h + 1)
                    for t in range(NT):
                        for st in range(t + 1):
                            last = mm(PS[:, 6 + t - 2 * (h // 2), (h % 2) * (ML_DV + 1):(h % 2 + 1) * (ML_DV + 1)],
                                      ml_w[:, h, st * TOK + t * P:st * TOK + (t + 1) * P],
                                      mva[:, st, h, :], start=(st == 0), stop=(st == t))
                    last.then_inc(S["ml_av"], 1)

                def branch_T(lo, bank, signal):
                    for k in range(4):
                        for t in range(NT):
                            last = nc.tensor.transpose(
                                PS[:, bank + k // 2, (k % 2) * TOK + t * P:(k % 2) * TOK + (t + 1) * P],
                                hn[:, t, lo + k:lo + HALF:4], ident)
                    last.then_inc(S[signal], 1)

                piece(8, z_rows(0, 0, 512))
                branch_T(HALF, 2, "tr_b")
                pe.wait_ge(S["g_copied"], 8 * (l + 1))
                pe.wait_ge(S["h_a"], l + 1)
                branch_T(0, 0, "tr_a")
                pe.wait_ge(S["hT_a"], l + 1)
                rows_split(OFF_WA, 4, 4)
                pe.wait_ge(S["hT_b"], l + 1)
                rows_split(OFF_WB, 4, 0, 4)
                pe.wait_ge(S["ya_read"], l + 1)
                transpose_rows("mixed", 4, l)
                rows_split(OFF_WO, KT, 0, turn=turned_turn("mixed", l))
                transpose_rows("ffn2", 4, l)
                ffn(OFF_FFN2, l * 2 * FFN_SUBS + FFN_SUBS, l * LAYER_UNITS, turned_turn("ffn2", l))
                pe.wait_ge(S["ple_full"], 32 * (l + 1))
                pe.wait_ge(S["x_ffn2"], NT * (l + 1))
                for j in range(2):
                    for t in range(NT):
                        last = nc.tensor.transpose(PS[:, 0, j * TOK + t * P:j * TOK + (t + 1) * P],
                                                   p_rows[:, t, j * P:(j + 1) * P], ident)
                last.then_inc(S["pT_ps"], 1)
                transpose_rows("ple", 4, l)
                pe.wait_ge(S["pT"], l + 1)
                rows_split(OFF_PLE, KT, 0, turn=turned_turn("ple", l))
                for j in range(2):
                    for t in range(NT):
                        for n in range(2):
                            last = mm(PS[:, 4 + 2 * t + n, :], pT[:, j, t * P:(t + 1) * P],
                                      w_ple[:, j, 512 * n:512 * n + 512], start=(j == 0), stop=(j == 1))
                last.then_inc(S["ple_up"], 1)


_INS = [
    "x", "c", "w_ada", "b_ada", "g_pre_mix", "g_post_mix", "g_pre_ffn", "g_post_ffn", "w_in", "ret_decay_fwd",
    "ret_decay_bwd", "w_out", "w_router", "w_gate_e", "w_up_e", "w_down_e", "p_2", "ffn1_norm_2", "ffn1_wi_2",
    "ffn1_wo_2", "mix_norm_2", "w_in_2", "b_igate_2", "b_fgate_2", "ml_out_norm_2", "q_norm_2", "k_norm_2",
    "sinks_2", "rel_bias_2", "w_a_2", "w_b_2", "w_out_2", "ffn2_norm_2", "ffn2_wi_2", "ffn2_wo_2", "ple_norm_2",
    "w_ple_gate_2", "w_ple_2"]


def shape_constants():
    c = {name: np.zeros((P, n), np.float32) for name, n in CONST_PARTS}
    c["ident"][:] = np.eye(P)
    tile = lambda f: np.concatenate([f(i * P + np.arange(P)[:, None], np.arange(TOK)[None, :]) for i in range(NT)], 1)
    c["rel_pos"][:] = tile(lambda s, t: np.maximum(t - s, 0))
    c["rel_neg"][:] = tile(lambda s, t: np.maximum(s - t, 0))
    c["dist"][:] = tile(lambda i, j: np.abs(i - j))
    c["causal"][:] = tile(lambda s, t: np.where(s <= t, 0.0, MASKED))

    def count(i, j):
        n = np.zeros(np.broadcast(i, j).shape)
        for window, d in ((128, 1), (512, 4), (2048, 16)):
            n += ((i - j) % d == 0) & (np.abs(i - j) // d <= window // (2 * d))
        return np.where(n > 0, np.log(np.maximum(n, 1)), MASKED)

    c["ln_count"][:] = tile(count)
    c["cap_iota"][:] = np.arange(CAP)
    for h in range(ML_H):
        c["minus_row"][h, h * P:(h + 1) * P] = -1.0
    dist = 2 * P - np.arange(3 * P)
    exact = BUCKETS // 2
    d = np.maximum(dist, 0)
    large = exact + (np.log(np.maximum(d, 1) / exact) / np.log(128 / exact) * (BUCKETS - exact)).astype(np.int32)
    bucket = np.where(d < exact, d, np.minimum(large, BUCKETS - 1))
    bucket = np.where((dist >= 0) & (dist < WINDOW), bucket, BUCKETS)
    c["bucket"][bucket, np.arange(3 * P)] = 1.0
    return np.ascontiguousarray(np.concatenate([c[name] for name, _ in CONST_PARTS], 1))


def kernel(**inputs):
    import concourse.bacc as bacc
    from concourse.bass_utils import run_bass_kernel_spmd

    nc = bacc.Bacc("TRN2", target_bir_lowering=False, num_devices=1)
    arrays, args = {}, {}
    for name in _INS:
        v = np.ascontiguousarray(inputs[name])
        arrays[f"in_{name}"] = v
        args[name] = nc.dram_tensor(f"in_{name}", v.shape, mybir.dt.from_np(v.dtype), kind="ExternalInput").ap()
    arrays["shape_constants"] = shape_constants()
    const = nc.dram_tensor("shape_constants", (P, NCONST), F32, kind="ExternalInput").ap()
    skew = nc.dram_tensor("skew", (SW_H, P, 3 * P), F32, kind="Internal").ap()
    out = nc.dram_tensor("out", (1, TOK, D), F32, kind="ExternalOutput").ap()
    build(nc, args, const, skew, out)
    r = run_bass_kernel_spmd(nc, [arrays], core_ids=[0])
    return r.results[0]["out"]
```
